# Optimizing a Trainium2 kernel written in Bass

```python
import math
import jax, jax.numpy as jnp
from jax import lax
import numpy as np

D_MODEL = 1024
BATCH = 1
SEQ = 512
DEPTH = 1

NORM_EPS = 1e-6
RW_HEADS = 8
RW_HEAD_DIM = 64
RW_WIDTH = RW_HEADS * RW_HEAD_DIM
DECAY_LORA = 64
AAA_LORA = 64
GATE_LORA = 160
RW_GN_EPS = 64e-5
RW_SHIFT_WIDTH = 3 * RW_WIDTH + DECAY_LORA + AAA_LORA + GATE_LORA
MLA_HEADS = 8
QK_NOPE = 64
QK_ROPE = 32
V_DIM = 64
Q_LORA = 384
KV_LORA = 256
ROPE_BASE = 10000.0
Q_BLOCK = 128
ATTN_SCALE = 1.0 / math.sqrt(QK_NOPE + QK_ROPE)
IN_WIDTH = RW_SHIFT_WIDTH + Q_LORA + KV_LORA + QK_ROPE + 2 * D_MODEL
PEER_HEADS = 8
N_KEYS = 128
N_EXPERTS = N_KEYS * N_KEYS
PEER_TOPK = 16
D_QUERY = 256
TOKEN_BLOCK = 128

kernel_name = "hybrid_rwkv7_mla_peer_block"

def rms_norm(x, w, eps=NORM_EPS):
    xf = x.astype(jnp.float32)
    y = xf * lax.rsqrt(jnp.mean(xf * xf, axis=-1, keepdims=True) + eps)
    return (y * w.astype(jnp.float32)).astype(x.dtype)

def apply_rope(x, pos):
    half = x.shape[-1] // 2
    inv_freq = ROPE_BASE ** (-jnp.arange(half, dtype=jnp.float32) / half)
    ang = pos.astype(jnp.float32)[..., None] * inv_freq
    ang = ang.reshape(ang.shape[:2] + (1,) * (x.ndim - 3) + (half,))
    cos, sin = jnp.cos(ang), jnp.sin(ang)
    xf = x.astype(jnp.float32)
    x1, x2 = xf[..., :half], xf[..., half:]
    return jnp.concatenate([x1 * cos - x2 * sin, x2 * cos + x1 * sin], axis=-1).astype(x.dtype)

def rwkv7_branch(p_rw, rw_mu, rw_w0, rw_w2, rw_a0, rw_a2, rw_g2, rw_k_k, rw_k_a, rw_r_k,
                 rw_ln_w, rw_ln_b, rw_w_o):
    B, S, _ = p_rw.shape
    p_prev = jnp.pad(p_rw, ((0, 0), (1, 0), (0, 0)))[:, :-1]
    p_mix = p_rw + rw_mu * (p_prev - p_rw)
    offs = np.cumsum([RW_WIDTH, RW_WIDTH, RW_WIDTH, DECAY_LORA, AAA_LORA]).tolist()
    r, k, v, wd, ad, gd = jnp.split(p_mix, offs, axis=-1)
    w = -jax.nn.softplus(-(rw_w0 + jnp.tanh(wd) @ rw_w2)) - 0.5
    decay = jnp.exp(-jnp.exp(w.astype(jnp.float32)))
    a = jax.nn.sigmoid(rw_a0 + ad @ rw_a2)
    g = jax.nn.sigmoid(gd) @ rw_g2
    kk = (k * rw_k_k).reshape(B, S, RW_HEADS, RW_HEAD_DIM).astype(jnp.float32)
    kk = kk / jnp.maximum(jnp.linalg.norm(kk, axis=-1, keepdims=True), 1e-12)
    k = k * (1.0 + (a - 1.0) * rw_k_a)
    hs = lambda t: t.reshape(B, S, RW_HEADS, RW_HEAD_DIM).astype(jnp.float32)
    r_h, k_h, v_h, a_h, w_h = hs(r), hs(k), hs(v), hs(a), hs(decay)

    def step(state, inp):
        r_t, w_t, k_t, v_t, kk_t, a_t = inp
        sa = jnp.einsum("bhvk,bhk->bhv", state, -kk_t)
        state = (state * w_t[:, :, None, :]
                 + sa[..., None] * (kk_t * a_t)[:, :, None, :]
                 + v_t[..., None] * k_t[:, :, None, :])
        return state, jnp.einsum("bhvk,bhk->bhv", state, r_t)

    xs = tuple(jnp.moveaxis(t, 1, 0) for t in (r_h, w_h, k_h, v_h, kk, a_h))
    s0 = jnp.zeros((B, RW_HEADS, RW_HEAD_DIM, RW_HEAD_DIM), jnp.float32)
    _, ys = lax.scan(step, s0, xs)
    y = jnp.moveaxis(ys, 0, 1)
    mu = jnp.mean(y, axis=-1, keepdims=True)
    var = jnp.mean(jnp.square(y - mu), axis=-1, keepdims=True)
    y = ((y - mu) * lax.rsqrt(var + RW_GN_EPS)).reshape(B, S, RW_WIDTH)
    y = y * rw_ln_w + rw_ln_b
    bonus = jnp.sum(r_h * k_h * rw_r_k.astype(jnp.float32), axis=-1, keepdims=True) * v_h
    y = (y + bonus.reshape(B, S, RW_WIDTH)).astype(p_rw.dtype) * g
    return y @ rw_w_o

def mla_branch(q_down, kv_down, k_pe_raw, positions, mla_q_norm_w, mla_w_uq, mla_kv_norm_w,
               mla_w_ukv, mla_qn_nope_w, mla_qn_pe_w, mla_kn_nope_w, mla_kn_pe_w, mla_w_o):
    B, S, _ = q_down.shape
    q = (rms_norm(q_down, mla_q_norm_w) @ mla_w_uq).reshape(B, S, MLA_HEADS, QK_NOPE + QK_ROPE)
    kv = (rms_norm(kv_down, mla_kv_norm_w) @ mla_w_ukv).reshape(B, S, MLA_HEADS, QK_NOPE + V_DIM)
    q_nope, q_pe = q[..., :QK_NOPE], q[..., QK_NOPE:]
    k_nope, v = kv[..., :QK_NOPE], kv[..., QK_NOPE:]
    q_nope = rms_norm(q_nope, mla_qn_nope_w)
    k_nope = rms_norm(k_nope, mla_kn_nope_w)
    q_pe = apply_rope(rms_norm(q_pe, mla_qn_pe_w), positions)
    k_pe = apply_rope(rms_norm(k_pe_raw, mla_kn_pe_w)[:, :, None, :], positions)
    q = jnp.concatenate([q_nope, q_pe], axis=-1)
    k = jnp.concatenate([k_nope, jnp.broadcast_to(k_pe, (B, S, MLA_HEADS, QK_ROPE))], axis=-1)
    nb = S // Q_BLOCK
    q_blocks = jnp.moveaxis(q.reshape(B, nb, Q_BLOCK, MLA_HEADS, QK_NOPE + QK_ROPE), 1, 0)
    k_pos = jnp.arange(S)

    def attend(args):
        q_blk, blk = args
        s = jnp.einsum("bqhd,bkhd->bhqk", q_blk, k).astype(jnp.float32) * ATTN_SCALE
        q_pos = blk * Q_BLOCK + jnp.arange(Q_BLOCK)
        s = jnp.where(k_pos[None, :] <= q_pos[:, None], s, jnp.finfo(jnp.float32).min)
        p = jax.nn.softmax(s, axis=-1).astype(v.dtype)
        return jnp.einsum("bhqk,bkhd->bqhd", p, v)

    o = lax.map(attend, (q_blocks, jnp.arange(nb)))
    o = jnp.moveaxis(o, 0, 1).reshape(B, S, MLA_HEADS * V_DIM)
    return o @ mla_w_o

def peer_ffn(hn, peer_w_query, peer_sub_keys, peer_u, peer_v):
    B, S, D = hn.shape
    T = B * S
    xt = hn.reshape(T, D)
    q = (xt @ peer_w_query).reshape(T, PEER_HEADS, 2, D_QUERY // 2)
    sc = jnp.einsum("thpd,hpnd->thpn", q, peer_sub_keys).astype(jnp.float32)
    s_top, i_top = lax.top_k(sc, PEER_TOPK)
    cand_s = (s_top[:, :, 0, :, None] + s_top[:, :, 1, None, :]).reshape(T, PEER_HEADS, PEER_TOPK * PEER_TOPK)
    cand_i = (i_top[:, :, 0, :, None] * N_KEYS + i_top[:, :, 1, None, :]).reshape(T, PEER_HEADS, PEER_TOPK * PEER_TOPK)
    best_s, best_pos = lax.top_k(cand_s, PEER_TOPK)
    expert_idx = jnp.take_along_axis(cand_i, best_pos, axis=-1)
    gates = jax.nn.softmax(best_s, axis=-1).astype(hn.dtype)
    nb = T // TOKEN_BLOCK
    xb = xt.reshape(nb, TOKEN_BLOCK, D)
    ib = expert_idx.reshape(nb, TOKEN_BLOCK, PEER_HEADS * PEER_TOPK)
    gb = gates.reshape(nb, TOKEN_BLOCK, PEER_HEADS * PEER_TOPK)

    def expert_block(args):
        x_blk, idx, g = args
        u = peer_u[idx]
        act = jax.nn.gelu(jnp.einsum("td,ted->te", x_blk, u), approximate=False)
        return jnp.einsum("te,ted->td", g * act, peer_v[idx])

    y = lax.map(expert_block, (xb, ib, gb))
    return y.reshape(B, S, D)

def setup_inputs(seed: int = 0) -> dict:
    key = jax.random.key(seed)
    ks = jax.random.split(key, 40)
    nrm = lambda i, shape, scale: jax.random.normal(ks[i], shape, jnp.float32) * scale
    gain = lambda i, n: 1.0 + 0.02 * jax.random.normal(ks[i], (n,), jnp.float32)
    return {
        "x": nrm(0, (BATCH, SEQ, D_MODEL), 1.0),
        "positions": (jnp.arange(SEQ, dtype=jnp.int32)[None, :]
                      + jax.random.randint(ks[1], (BATCH, 1), 0, 1024, jnp.int32)),
        "norm1_w": gain(2, D_MODEL),
        "w_in": nrm(3, (D_MODEL, IN_WIDTH), D_MODEL ** -0.5),
        "rw_mu": jax.random.uniform(ks[4], (RW_SHIFT_WIDTH,), jnp.float32),
        "rw_w0": jax.random.uniform(ks[5], (RW_WIDTH,), jnp.float32, -6.0, -1.0),
        "rw_w2": nrm(6, (DECAY_LORA, RW_WIDTH), 0.1),
        "rw_a0": nrm(7, (RW_WIDTH,), 0.1),
        "rw_a2": nrm(8, (AAA_LORA, RW_WIDTH), 0.1),
        "rw_g2": nrm(9, (GATE_LORA, RW_WIDTH), GATE_LORA ** -0.5),
        "rw_k_k": 0.85 + 0.05 * jax.random.normal(ks[10], (RW_WIDTH,), jnp.float32),
        "rw_k_a": 1.0 + 0.05 * jax.random.normal(ks[11], (RW_WIDTH,), jnp.float32),
        "rw_r_k": nrm(12, (RW_HEADS, RW_HEAD_DIM), 0.1),
        "rw_ln_w": gain(13, RW_WIDTH),
        "rw_ln_b": nrm(14, (RW_WIDTH,), 0.02),
        "rw_w_o": nrm(15, (RW_WIDTH, D_MODEL), RW_WIDTH ** -0.5),
        "mla_q_norm_w": gain(16, Q_LORA),
        "mla_w_uq": nrm(17, (Q_LORA, MLA_HEADS * (QK_NOPE + QK_ROPE)), Q_LORA ** -0.5),
        "mla_kv_norm_w": gain(18, KV_LORA),
        "mla_w_ukv": nrm(19, (KV_LORA, MLA_HEADS * (QK_NOPE + V_DIM)), KV_LORA ** -0.5),
        "mla_qn_nope_w": gain(20, QK_NOPE),
        "mla_qn_pe_w": gain(21, QK_ROPE),
        "mla_kn_nope_w": gain(22, QK_NOPE),
        "mla_kn_pe_w": gain(23, QK_ROPE),
        "mla_w_o": nrm(24, (MLA_HEADS * V_DIM, D_MODEL), (MLA_HEADS * V_DIM) ** -0.5),
        "w_out": nrm(25, (D_MODEL, D_MODEL), D_MODEL ** -0.5),
        "norm2_w": gain(26, D_MODEL),
        "peer_w_query": nrm(27, (D_MODEL, PEER_HEADS * D_QUERY), D_MODEL ** -0.5),
        "peer_sub_keys": nrm(28, (PEER_HEADS, 2, N_KEYS, D_QUERY // 2), (D_QUERY // 2) ** -0.5),
        "peer_u": nrm(29, (N_EXPERTS, D_MODEL), D_MODEL ** -0.5),
        "peer_v": nrm(30, (N_EXPERTS, D_MODEL), PEER_HEADS ** -0.5),
    }

def reference(x, positions, norm1_w, w_in, rw_mu, rw_w0, rw_w2, rw_a0, rw_a2, rw_g2, rw_k_k,
              rw_k_a, rw_r_k, rw_ln_w, rw_ln_b, rw_w_o, mla_q_norm_w, mla_w_uq, mla_kv_norm_w,
              mla_w_ukv, mla_qn_nope_w, mla_qn_pe_w, mla_kn_nope_w, mla_kn_pe_w, mla_w_o, w_out,
              norm2_w, peer_w_query, peer_sub_keys, peer_u, peer_v):
    h = x
    for _ in range(DEPTH):
        xn = rms_norm(h, norm1_w)
        p = xn @ w_in
        offs = np.cumsum([RW_SHIFT_WIDTH, Q_LORA, KV_LORA, QK_ROPE, D_MODEL]).tolist()
        p_rw, q_down, kv_down, k_pe_raw, g_a, g_b = jnp.split(p, offs, axis=-1)
        y_a = rwkv7_branch(p_rw, rw_mu, rw_w0, rw_w2, rw_a0, rw_a2, rw_g2, rw_k_k, rw_k_a,
                           rw_r_k, rw_ln_w, rw_ln_b, rw_w_o)
        y_b = mla_branch(q_down, kv_down, k_pe_raw, positions, mla_q_norm_w, mla_w_uq,
                         mla_kv_norm_w, mla_w_ukv, mla_qn_nope_w, mla_qn_pe_w, mla_kn_nope_w,
                         mla_kn_pe_w, mla_w_o)
        mixed = jax.nn.sigmoid(g_a) * y_a + jax.nn.sigmoid(g_b) * y_b
        h = h + mixed @ w_out
        h = h + peer_ffn(rms_norm(h, norm2_w), peer_w_query, peer_sub_keys, peer_u, peer_v)
    return h


_drawn_inputs = setup_inputs


def setup_inputs(seed=0):
    import zlib

    import numpy as np

    out = dict(_drawn_inputs(seed))
    spreads = {}
    factors = {'rw_ln_w': 28.352,
     'rw_ln_b': 29.952,
     'mla_q_norm_w': 7.651,
     'mla_kv_norm_w': 6.5,
     'mla_qn_nope_w': 8.0,
     'mla_qn_pe_w': 8.0,
     'mla_kn_nope_w': 8.0,
     'mla_kn_pe_w': 8.0,
     'rw_w2': 4.829,
     'rw_a0': 4.848,
     'rw_k_k': 3.687,
     'rw_k_a': 3.426,
     'rw_r_k': 3.052,
     'norm2_w': 7.63}
    for name, (base, spread) in spreads.items():
        noise = np.random.default_rng([zlib.crc32(name.encode()), seed]).standard_normal(out[name].shape)
        drawn = base * np.exp(spread * noise) if base else spread * noise
        out[name] = __import__('jax').numpy.asarray(drawn.astype(out[name].dtype))
    for name, factor in factors.items():
        out[name] = (out[name] * factor).astype(out[name].dtype)
    return out
```

```python
from contextlib import ExitStack

import numpy as np
import concourse.bass as bass
from concourse import mybir

F32 = mybir.dt.float32
F16 = mybir.dt.float16
I32 = mybir.dt.int32
U32 = mybir.dt.uint32
ALU = mybir.AluOpType
ACT = mybir.ActivationFunctionType
AX = mybir.AxisListType

P = 128
T = 512
D = 1024
KT = D // P
EPS = 1e-6
RW = 512
RT = RW // P
C = 64
NCH = T // C
GN_EPS = 64e-5
Q_LORA, KV_LORA, ROPE = 384, 256, 32
HEADS, NOPE, QK = 8, 64, 96
TT = T // P
PH, NK, TOPK = 8, 128, 16
PICKS = PH * TOPK
NE = NK * NK

RW_COLS = [(P * n, P) for n in range(13)] + [(1664, P), (1792, 32)]
Q_COL = 1824
KV_COL = Q_COL + Q_LORA
KPE_COL = KV_COL + KV_LORA
GA_COL = KPE_COL + ROPE
GB_COL = GA_COL + D

VECS = [("norm1_w", P, 8), ("rw_mu", P, 14), ("rw_mu_tail", 32, 1), ("rw_w0", P, 4), ("rw_a0", P, 4),
        ("rw_k_k", P, 4), ("rw_k_a", P, 4), ("rw_r_k", P, 4), ("rw_ln_w", P, 4), ("rw_ln_b", P, 4),
        ("mla_q_norm_w", P, 3), ("mla_kv_norm_w", P, 2), ("qn_w", QK, 1), ("kn_w", QK, 1),
        ("norm2_w", P, 8), ("inv_freq", QK, 1)]
VEC_AT = {name: sum(t for _, _, t in VECS[:n]) for n, (name, _, _) in enumerate(VECS)}
NV = sum(t for _, _, t in VECS)

LEVELS = [1, 2, 4, 8, 16, 32]
CONSTS = [("ones", P), ("head_ones", P), ("ident", P), ("qk_ones", QK), ("rope_swap", QK), ("iota", P),
          ("causal", P), ("chunk_start", T), ("strict", C), ("upto", C)] + \
         [(f"level_t{m}", C) for m in LEVELS] + [("level1", C)]
CONST_AT = {name: (sum(c for _, c in CONSTS[:n]), cols) for n, (name, cols) in enumerate(CONSTS)}
NCONST = sum(c for _, c in CONSTS)


def constant_array():
    a = np.zeros((P, NCONST), np.float32)

    def put(name, m):
        at, cols = CONST_AT[name]
        a[:m.shape[0], at:at + cols] = m

    i, j = np.arange(P)[:, None], np.arange(P)[None, :]
    put("ones", np.ones((P, P)))
    put("head_ones", (i // 64 == j // 64) * 1.0)
    put("ident", (i == j) * 1.0)
    q, r = np.arange(QK)[:, None], np.arange(QK)[None, :]
    put("qk_ones", np.where((q < NOPE) & (r < NOPE), 1 / NOPE, 0) + np.where((q >= NOPE) & (r >= NOPE), 1 / ROPE, 0))
    half = ROPE // 2
    put("rope_swap", np.where((r >= NOPE) & (r < NOPE + half) & (q == r + half), -1.0, 0)
        + np.where((r >= NOPE + half) & (q == r - half), 1.0, 0))
    put("iota", np.broadcast_to(j, (P, P)) * 1.0)
    put("causal", np.where(j <= i, 0.0, -1e30))
    put("chunk_start", np.broadcast_to(np.arange(T)[None] % C != 0, (P, T)) * 1.0)
    s, t = np.arange(P)[:, None] % C, np.arange(C)[None, :]
    put("strict", (s < t) * 1.0)
    put("upto", (s <= t) * 1.0)
    for m in LEVELS:
        put(f"level_t{m}", ((t // (2 * m) == s // (2 * m)) & (t // m % 2 == 1) & (s // m % 2 == 0)) * 1.0)
    put("level1", ((s // 2 == t // 2) & (s % 2 == 1) & (t % 2 == 0)) * 1.0)
    return a


class Kit:
    pass


def chained(eng, sem):
    n = [0]

    def link(ins):
        n[0] += 1
        ins.then_inc(sem, 1)
        eng.wait_ge(sem, n[0])
    return link


def phase_norm_and_rwkv_in(nc, k, io):
    x = k.view(64, [KT, T])
    sq = k.view(80, [KT, T])
    ring = [k.view(96 + 4 * s, [KT, P]) for s in range(4)]
    raw = [k.view(112 + 3 * s, [T + 1]) for s in range(2)]
    diff = k.view(118, [T])
    rt, rstd = k.view(120, [T]), k.view(122, [T])
    xn, mix = k.view(0, [KT, T]), k.view(32, [15, T])
    w_in = io["w_in"].rearrange("(k p) n -> p k n", p=P)
    NB = 3
    with nc.Block() as block:
        x_ld = [k.sem(f"x_ld{n}") for n in range(KT)]
        small_ld, sq_ready, ss_done, rt_ready, rstd_ready = map(k.sem, ("small_ld", "sq_ready", "ss_done", "rt_ready", "rstd_ready"))
        w_ld = [k.sem(f"w_in_ld{s}") for s in range(4)]
        xn_ready, proj_done, raw_ready, pad_ready, diff_ready, mix_done = map(
            k.sem, ("xn_ready", "proj_done", "raw_ready", "pad_ready", "diff_ready", "mix_done"))

        @block.sync
        def _(sp):
            for n in range(KT):
                sp.dma_start(x[:, n], io["xT"][n * P:(n + 1) * P, :]).then_inc(x_ld[n], 16)
                if n == 0:
                    sp.dma_start(k.consts[:, :], io["consts"]).then_inc(small_ld, 16)
                    sp.dma_start(k.vecs[:, :], io["vecs"]).then_inc(small_ld, 16)
            for n, (col, m) in enumerate(RW_COLS):
                if n >= 4:
                    sp.wait_ge(proj_done, n - 3)
                sp.dma_start(ring[n % 4][:, :, 0:m], w_in[:, :, col:col + m]).then_inc(w_ld[n % 4], 16)

        @block.scalar
        def _(act):
            for n in range(KT):
                act.wait_ge(x_ld[n], 16)
                act.activation(sq[:, n], x[:, n], ACT.Square).then_inc(sq_ready, 1)
            act.wait_ge(ss_done, 1)
            act.wait_ge(pad_ready, 3)
            act.activation(rt, k.ps[:, 0], ACT.Sqrt, scale=1.0 / D, bias=k.eps[:, 0:1]).then_inc(rt_ready, 1)
            for n, (_, m) in enumerate(RW_COLS):
                act.wait_ge(proj_done, n + 1)
                act.wait_ge(pad_ready, 3)
                if n >= 2:
                    act.wait_ge(mix_done, n - 1)
                act.activation(raw[n % 2][0:m, 1:T + 1], k.ps[0:m, 1 + n % NB], ACT.Copy).then_inc(raw_ready, 1)

        @block.vector
        def _(dve):
            dve.memset(raw[0][:, 0:1], 0.0).then_inc(pad_ready, 1)
            dve.memset(raw[1][:, 0:1], 0.0).then_inc(pad_ready, 1)
            dve.memset(k.eps[:, 0:1], EPS).then_inc(pad_ready, 1)
            dve.memset(k.eps[:, 1:2], GN_EPS)
            dve.wait_ge(small_ld, 32)
            dve.wait_ge(rt_ready, 1)
            dve.reciprocal(rstd, rt).then_inc(rstd_ready, 1)
            dve.wait_ge(rstd_ready, 1)
            for n in range(KT):
                dve.scalar_tensor_tensor(xn[:, n], x[:, n], k.vec("norm1_w", n), rstd,
                                         ALU.mult, ALU.mult).then_inc(xn_ready, 1)
            for n, (_, m) in enumerate(RW_COLS):
                dve.wait_ge(raw_ready, n + 1)
                if n:
                    dve.wait_ge(mix_done, n)
                prev, cur = raw[n % 2][0:m, 0:T], raw[n % 2][0:m, 1:T + 1]
                dve.tensor_tensor(diff[0:m], prev, cur, ALU.subtract).then_inc(diff_ready, 1)
                dve.wait_ge(diff_ready, n + 1)
                dve.scalar_tensor_tensor(mix[0:m, n], diff[0:m], k.vec("rw_mu", n)[0:m], cur,
                                         ALU.mult, ALU.add).then_inc(mix_done, 1)

        @block.tensor
        def _(pe):
            pe.wait_ge(small_ld, 32)
            for n in range(KT):
                pe.wait_ge(sq_ready, n + 1)
                last = pe.matmul(k.ps[:, 0], k.const("ones"), sq[:, n], start=n == 0, stop=n == KT - 1)
            last.then_inc(ss_done, 1)
            for n, (_, m) in enumerate(RW_COLS):
                pe.wait_ge(w_ld[n % 4], 16 * (n // 4 + 1))
                if n >= NB:
                    pe.wait_ge(raw_ready, n - NB + 1)
                for f in range(KT):
                    if n == 0:
                        pe.wait_ge(xn_ready, f + 1)
                    last = pe.matmul(k.ps[0:m, 1 + n % NB], ring[n % 4][:, f, 0:m], xn[:, f],
                                     start=f == 0, stop=f == KT - 1)
                last.then_inc(proj_done, 1)


def phase_rwkv_prepare(nc, k, io):
    mix = k.view(32, [15, T])
    r, key, v = mix[:, 0:4], mix[:, 4:8], mix[:, 8:12]
    at, bt, kt, rt_, g, bonus = (k.view(64 + 8 * n, [RT, T]) for n in range(6))
    lw, L, ex, ea, a, kk, kp = (k.view(112 + 8 * n, [RT, T]) for n in range(7))
    w2a2 = k.view(168, [RW])
    g2a, g2b = k.view(170, [RW]), k.view(172, [RW])
    tw, sg = k.view(174, [T]), k.view(176, [2, T])
    inv_n = k.view(180, [RT, T])
    ps = k.ps
    with nc.Block() as block:
        lora_ld, tw_ready, sg_ready, z_done, za_done, g_done, kk2_done, rk_done = map(
            k.sem, ("lora_ld", "tw_ready", "sg_ready", "z_done", "za_done", "g_done", "kk2_done", "rk_done"))
        sw_ready, a_ready, g_ready, kk2_ready, norm_ready = map(
            k.sem, ("sw_ready", "a_ready", "g_ready", "kk2_ready", "norm_ready"))
        ss_ready, ex_in, L_ready, rk_ready, dve_chain, ea_ready, en_ready, ex_ready = map(
            k.sem, ("ss_ready", "ex_in", "L_ready", "rk_ready", "dve_chain2", "ea_ready", "en_ready", "ex_ready"))

        @block.sync
        def _(sp):
            sp.dma_start(w2a2[0:64], io["rw_w2"]).then_inc(lora_ld, 16)
            sp.dma_start(w2a2[64:128], io["rw_a2"]).then_inc(lora_ld, 16)
            sp.dma_start(g2a, io["rw_g2"][0:P, :]).then_inc(lora_ld, 16)
            sp.dma_start(g2b[0:32], io["rw_g2"][P:160, :]).then_inc(lora_ld, 16)

        @block.scalar
        def _(act):
            act.activation(tw[0:64], mix[0:64, 12], ACT.Tanh).then_inc(tw_ready, 1)
            act.activation(sg[:, 0], mix[:, 13], ACT.Sigmoid).then_inc(sg_ready, 1)
            act.activation(sg[0:32, 1], mix[0:32, 14], ACT.Sigmoid).then_inc(sg_ready, 1)
            for j in range(RT):
                act.wait_ge(z_done, j + 1)
                act.activation(lw[:, j], ps[:, j], ACT.Sigmoid, bias=k.vec("rw_w0", j)).then_inc(sw_ready, 1)
            for j in range(RT):
                act.wait_ge(za_done, j + 1)
                act.activation(a[:, j], ps[:, 4 + j], ACT.Sigmoid, bias=k.vec("rw_a0", j)).then_inc(a_ready, 1)
            for j in range(RT):
                act.wait_ge(g_done, j + 1)
                act.activation(g[:, j], ps[:, j], ACT.Copy).then_inc(g_ready, 1)
            for j in range(RT):
                act.activation(kp[:, j], key[:, j], ACT.Square, scale=k.vec("rw_k_k", j)).then_inc(kk2_ready, 1)
            act.wait_ge(ss_ready, 1)
            act.activation(inv_n[:, :], inv_n[:, :], ACT.Sqrt).then_inc(norm_ready, 1)
            act.wait_ge(L_ready, RT)
            act.activation(ea[:, :], L[:, :], ACT.Exp).then_inc(ea_ready, 1)
            act.wait_ge(ex_in, 1)
            act.activation(ex[:, :], ex[:, :], ACT.Exp).then_inc(ex_ready, 1)
            act.wait_ge(ea_ready, 1)
            act.activation(L[:, :], L[:, :], ACT.Exp, scale=-1.0).then_inc(en_ready, 1)

        @block.vector
        def _(dve):
            link = chained(dve, dve_chain)
            for j in range(RT):
                dve.wait_ge(sw_ready, j + 1)
                link(dve.tensor_scalar(lw[:, j], lw[:, j], -float(np.exp(-0.5)), None, ALU.mult))
                dve.tensor_tensor_scan(L[:, j], k.const("chunk_start"), lw[:, j], 0.0,
                                       ALU.mult, ALU.add).then_inc(L_ready, 1)
            dve.wait_ge(L_ready, RT)
            dve.tensor_tensor(ex[:, :], L[:, :], lw[:, :], ALU.subtract).then_inc(ex_in, 1)
            dve.wait_ge(kk2_done, RT)
            dve.tensor_scalar(inv_n[:, :], ps[:, 4:8], 1e-24, None, ALU.max).then_inc(ss_ready, 1)
            dve.wait_ge(norm_ready, 1)
            link(dve.reciprocal(inv_n[:, :], inv_n[:, :]))
            for j in range(RT):
                last = dve.scalar_tensor_tensor(kk[:, j], key[:, j], k.vec("rw_k_k", j), inv_n[:, j], ALU.mult, ALU.mult)
            link(last)
            dve.wait_ge(a_ready, RT)
            link(dve.tensor_tensor(bt[:, :], kk[:, :], a[:, :], ALU.mult))
            for j in range(RT):
                last = dve.tensor_scalar(a[:, j], a[:, j], 1.0, k.vec("rw_k_a", j), ALU.subtract, ALU.mult)
            link(last)
            link(dve.scalar_tensor_tensor(kp[:, :], a[:, :], 1.0, key[:, :], ALU.add, ALU.mult))
            for j in range(RT):
                dve.scalar_tensor_tensor(a[:, j], r[:, j], k.vec("rw_r_k", j), kp[:, j],
                                         ALU.mult, ALU.mult).then_inc(rk_ready, 1)
            dve.wait_ge(ex_ready, 1)
            dve.scalar_tensor_tensor(at[:, :], kk[:, :], -1.0, ex[:, :], ALU.mult, ALU.mult)
            dve.wait_ge(en_ready, 1)
            dve.tensor_tensor(bt[:, :], bt[:, :], L[:, :], ALU.mult)
            dve.tensor_tensor(kt[:, :], kp[:, :], L[:, :], ALU.mult)
            dve.tensor_tensor(rt_[:, :], r[:, :], ea[:, :], ALU.mult)
            dve.tensor_copy(k.chunk_decay[:, :, :], ea.rearrange("p j (c t) -> p j c t", t=C)[:, :, :, C - 1])
            dve.wait_ge(rk_done, RT)
            dve.tensor_tensor(bonus[:, :], ps[:, 0:4], v[:, :], ALU.mult)

        @block.tensor
        def _(pe):
            pe.wait_ge(lora_ld, 64)
            pe.wait_ge(tw_ready, 1)
            for j in range(RT):
                pe.matmul(ps[:, j], w2a2[0:64, j * P:(j + 1) * P], tw[0:64], start=True, stop=True).then_inc(z_done, 1)
            for j in range(RT):
                pe.matmul(ps[:, 4 + j], w2a2[64:128, j * P:(j + 1) * P], mix[64:128, 12],
                          start=True, stop=True).then_inc(za_done, 1)
            pe.wait_ge(sg_ready, 2)
            for j in range(RT):
                pe.wait_ge(sw_ready, j + 1)
                pe.matmul(ps[:, j], g2a[:, j * P:(j + 1) * P], sg[:, 0], start=True, stop=False)
                pe.matmul(ps[:, j], g2b[0:32, j * P:(j + 1) * P], sg[0:32, 1], start=False, stop=True).then_inc(g_done, 1)
            for j in range(RT):
                pe.wait_ge(kk2_ready, j + 1)
                pe.wait_ge(a_ready, j + 1)
                pe.matmul(ps[:, 4 + j], k.const("head_ones"), kp[:, j], start=True, stop=True).then_inc(kk2_done, 1)
            for j in range(RT):
                pe.wait_ge(rk_ready, j + 1)
                pe.wait_ge(g_ready, j + 1)
                pe.matmul(ps[:, j], k.const("head_ones"), a[:, j], start=True, stop=True).then_inc(rk_done, 1)



def phase_delta_rule(nc, k, io):
    at, bt, kt, rt_ = (k.view(64 + 8 * n, [RT, T]) for n in range(4))
    v = k.view(48, [RT, T])
    W = NCH * RT * C
    AabT, AakT, Vt = k.view(32, [W]), k.view(40, [W]), k.view(56, [W])
    ArbT, ArkT, Tm, TmT, X, Am, Bt, Kt = (k.view(112 + 8 * n, [W]) for n in range(8))
    ST, R, SA = k.view(176, [RT, C]), k.view(177, [RT, C]), k.view(178, [RT, C])
    y = k.view(184, [RT, T])
    ps = k.ps
    GR = W // 512
    half = [slice(0, 64), slice(64, 128)]

    def mask(name, e=None, n=8):
        m = k.const(name)[:, 0:C] if e is None else k.const(name)[half[e], 0:C]
        return m.unsqueeze(1).to_broadcast([m.shape[0], n, C])

    def blocks(a):
        return a.rearrange("p (n t) -> p n t", t=C)

    units = []
    for g in range(GR):
        units += [("gram", AabT, bt, at, "strict", g), ("gram", X, at, bt, "level1", g)]
    for (grams, turns) in (((AakT, kt, at, "strict"), (Vt, v)), ((ArbT, bt, rt_, "upto"), (Bt, bt)),
                           ((ArkT, kt, rt_, "upto"), (Kt, kt))):
        for g in range(GR):
            units += [("gram", *grams, g), ("turn", *turns, None, None, g)]
    count = {kind: [sum(u[0] == kind for u in units[:n + 1]) for n in range(len(units))] for kind in ("gram", "turn")}

    with nc.Block() as block:
        pair_done, gram_out, turn_out, am_ready, t_init = map(k.sem, ("pair_done", "gram_out", "turn_out", "am_ready", "t_init"))
        x_done, x_out, t_done, t_out, tt_done, tt_out = map(k.sem, ("x_done", "x_out", "t_done", "t_out", "tt_done", "tt_out"))
        r_done, r_out0, r_out1, sa_done, sa_out0, sa_out1 = map(
            k.sem, ("r_done", "r_out0", "r_out1", "sa_done", "sa_out0", "sa_out1"))
        s_done, s_out, y_done, y_out0, y_out1 = map(k.sem, ("s_done", "s_out", "y_done", "y_out0", "y_out1"))

        @block.tensor
        def _(pe):
            for u, (kind, dst, lhs, rhs, _, g) in enumerate(units):
                if u >= 4:
                    before = units[u - 4][0]
                    pe.wait_ge(gram_out if before == "gram" else turn_out, count[before][u - 4])
                for n in range(8):
                    c, j = divmod(8 * g + n, RT)
                    t = slice(c * C, (c + 1) * C)
                    for e in range(2):
                        right = rhs[half[e], j, t] if kind == "gram" else k.const("ident")[half[e], half[e]]
                        last = pe.matmul(ps[half[e], 2 * (u % 4) + e, n * C:(n + 1) * C],
                                         lhs[half[e], j, t], right, start=True, stop=True)
                last.then_inc(pair_done, 1)
            pe.wait_ge(gram_out, count["gram"][-1])
            pe.wait_ge(turn_out, count["turn"][-1])

            def cols(n):
                return slice(n * C, (n + 1) * C)

            def x_products(lv, g):
                n = (lv - 1) * GR + g
                if g == 0:
                    pe.wait_ge(am_ready, lv)
                if lv == 1:
                    pe.wait_ge(t_init, 2)
                else:
                    pe.wait_ge(t_out, (lv - 2) * GR + g + 1)
                if n >= 2:
                    pe.wait_ge(x_out, n - 1)
                for q in range(8):
                    for e in range(2):
                        last = pe.matmul(ps[half[e], 2 * (n % 2) + e, cols(q)], Am[half[e], cols(8 * g + q)],
                                         Tm[half[e], cols(8 * g + q)], start=True, stop=True)
                last.then_inc(x_done, 1)

            def t_products(lv, g):
                n = (lv - 1) * GR + g
                pe.wait_ge(x_out, n + 1)
                if lv > 1:
                    pe.wait_ge(tt_out, (lv - 2) * GR + g + 1)
                if lv < len(LEVELS) - 1:
                    if n:
                        pe.wait_ge(t_out, n)
                    for q in range(8):
                        for e in range(2):
                            last = pe.matmul(ps[half[e], 4 + e, cols(q)], TmT[half[e], cols(8 * g + q)],
                                             X[half[e], cols(8 * g + q)], start=True, stop=True)
                    last.then_inc(t_done, 1)
                if n:
                    pe.wait_ge(tt_out, n)
                for q in range(8):
                    for e in range(2):
                        last = pe.matmul(ps[half[e], 6 + e, cols(q)], X[half[e], cols(8 * g + q)],
                                         TmT[half[e], cols(8 * g + q)], start=True, stop=True)
                last.then_inc(tt_done, 1)

            for lv in range(1, len(LEVELS)):
                for g in range(GR + 1):
                    if g < GR:
                        x_products(lv, g)
                    if g:
                        t_products(lv, g - 1)
            pe.wait_ge(tt_out, (len(LEVELS) - 1) * GR)

            for c in range(NCH):
                t = slice(c * C, (c + 1) * C)
                pair = [(j, e, cols(RT * c + j)) for j in range(RT) for e in range(2)]
                if c:
                    pe.wait_ge(s_out, c)
                for j, e, m in pair:
                    out = ps[half[e], e, cols(j)]
                    if c:
                        pe.matmul(out, at[half[e], j, t], ST[half[e], j], start=True, stop=False)
                    last = pe.matmul(out, AakT[half[e], m], Vt[half[e], m], start=not c, stop=True)
                last.then_inc(r_done, 1)
                pe.wait_ge(r_out0, c + 1)
                pe.wait_ge(r_out1, c + 1)
                for j, e, m in pair:
                    last = pe.matmul(ps[half[e], 2 + e, cols(j)], TmT[half[e], m], R[half[e], j], start=True, stop=True)
                last.then_inc(sa_done, 1)
                pe.wait_ge(sa_out0, c + 1)
                pe.wait_ge(sa_out1, c + 1)
                if c < NCH - 1:
                    for j, e, m in pair:
                        out = ps[half[e], 6 + e, cols(j)]
                        pe.matmul(out, Bt[half[e], m], SA[half[e], j], start=True, stop=False)
                        if c:
                            pe.matmul(out, k.const("ident")[half[e], half[e]], ST[half[e], j], start=False, stop=False)
                        last = pe.matmul(out, Kt[half[e], m], Vt[half[e], m], start=False, stop=True)
                    last.then_inc(s_done, 1)
                if c:
                    pe.wait_ge(y_out0, c)
                    pe.wait_ge(y_out1, c)
                for j, e, m in pair:
                    out = ps[half[e], 4 + e, cols(j)]
                    pe.matmul(out, SA[half[e], j], ArbT[half[e], m], start=True, stop=False)
                    if c:
                        pe.matmul(out, ST[half[e], j], rt_[half[e], j, t], start=False, stop=False)
                    last = pe.matmul(out, Vt[half[e], m], ArkT[half[e], m], start=False, stop=True)
                last.then_inc(y_done, 1)

        @block.scalar
        def _(act):
            for u, (kind, dst, _, _, _, g) in enumerate(units):
                if kind == "turn":
                    act.wait_ge(pair_done, u + 1)
                    for e in range(2):
                        last = act.activation(dst[half[e], g * 512:(g + 1) * 512], ps[half[e], 2 * (u % 4) + e], ACT.Copy)
                    last.then_inc(turn_out, 1)
            for n in range((len(LEVELS) - 1) * GR):
                g = n % GR
                act.wait_ge(x_done, n + 1)
                if n < GR:
                    act.wait_ge(t_init, 2)
                else:
                    act.wait_ge(tt_done, n - GR + 1)
                for e in range(2):
                    last = act.activation(X[half[e], g * 512:(g + 1) * 512], ps[half[e], 2 * (n % 2) + e], ACT.Copy)
                last.then_inc(x_out, 1)
            for c in range(NCH):
                act.wait_ge(r_done, c + 1)
                act.activation(R[half[0]], ps[half[0], 0, 0:RT * C], ACT.Copy).then_inc(r_out0, 1)
                act.wait_ge(sa_done, c + 1)
                if c:
                    act.wait_ge(y_done, c)
                act.activation(SA[half[0]], ps[half[0], 2, 0:RT * C], ACT.Copy).then_inc(sa_out0, 1)
                act.wait_ge(y_done, c + 1)
                act.activation(y[half[0], :, c * C:(c + 1) * C], ps[half[0], 4, 0:RT * C], ACT.Copy).then_inc(y_out0, 1)

        @block.vector
        def _(dve):
            for u, (kind, dst, _, _, m, g) in enumerate(units):
                if kind == "gram":
                    dve.wait_ge(pair_done, u + 1)
                    for e in range(2):
                        last = dve.tensor_tensor(blocks(dst[half[e], g * 512:(g + 1) * 512]),
                                                 blocks(ps[half[e], 2 * (u % 4) + e]), mask(m, e), ALU.mult)
                    last.then_inc(gram_out, 1)
            dve.wait_ge(gram_out, count["gram"][-1])
            ident = [k.const("ident")[half[e], half[e]].unsqueeze(1).to_broadcast([64, W // C, C]) for e in range(2)]
            dve.tensor_tensor(blocks(TmT), blocks(AabT), mask("level_t1", n=W // C), ALU.mult).then_inc(am_ready, 1)
            dve.tensor_tensor(blocks(Am), blocks(AabT), mask("level_t2", n=W // C), ALU.mult)
            for e in range(2):
                last = dve.tensor_tensor(blocks(Tm[half[e]]), blocks(X[half[e]]), ident[e], ALU.add)
            last.then_inc(t_init, 1)
            dve.wait_ge(am_ready, 1)
            for e in range(2):
                last = dve.tensor_tensor(blocks(TmT[half[e]]), blocks(TmT[half[e]]), ident[e], ALU.add)
            last.then_inc(t_init, 1)
            for lv in range(1, len(LEVELS)):
                if lv > 1:
                    dve.wait_ge(x_done, (lv - 1) * GR)
                    dve.tensor_tensor(blocks(Am), blocks(AabT), mask(f"level_t{LEVELS[lv]}", n=W // C),
                                      ALU.mult).then_inc(am_ready, 1)
                for g in range(GR):
                    n = (lv - 1) * GR + g
                    gs = slice(g * 512, (g + 1) * 512)
                    if lv < len(LEVELS) - 1:
                        dve.wait_ge(t_done, n + 1)
                        for e in range(2):
                            last = dve.tensor_tensor(Tm[half[e], gs], Tm[half[e], gs], ps[half[e], 4 + e], ALU.add)
                        last.then_inc(t_out, 1)
                    dve.wait_ge(tt_done, n + 1)
                    for e in range(2):
                        last = dve.tensor_tensor(TmT[half[e], gs], TmT[half[e], gs], ps[half[e], 6 + e], ALU.add)
                    last.then_inc(tt_out, 1)
            for c in range(NCH):
                dve.wait_ge(r_done, c + 1)
                dve.tensor_copy(R[half[1]], ps[half[1], 1, 0:RT * C]).then_inc(r_out1, 1)
                dve.wait_ge(sa_done, c + 1)
                if c:
                    dve.wait_ge(y_done, c)
                dve.tensor_copy(SA[half[1]], ps[half[1], 3, 0:RT * C]).then_inc(sa_out1, 1)
                dve.wait_ge(y_done, c + 1)
                if c < NCH - 1:
                    dve.wait_ge(s_done, c + 1)
                    for e in range(2):
                        last = dve.tensor_tensor(ST[half[e]], ps[half[e], 6 + e, 0:RT * C].rearrange("p (j t) -> p j t", j=RT),
                                                 k.chunk_decay[half[e], :, c:c + 1].to_broadcast([64, RT, C]), ALU.mult)
                    last.then_inc(s_out, 1)
                dve.tensor_copy(y[half[1], :, c * C:(c + 1) * C], ps[half[1], 5, 0:RT * C]).then_inc(y_out1, 1)


def phase_rwkv_out(nc, k, io):
    g, bonus, y = k.view(96, [RT, T]), k.view(104, [RT, T]), k.view(184, [RT, T])
    d, sq, s, yg = k.view(112, [RT, T]), k.view(120, [RT, T]), k.view(128, [RT, T]), k.view(16, [RT, T])
    ps = k.ps
    with nc.Block() as block:
        mean_done, dev_ready, dev2_ready, var_done, sd_ready, gn_chain = map(
            k.sem, ("mean_done", "dev_ready", "dev2_ready", "var_done", "sd_ready", "gn_chain"))

        @block.tensor
        def _(pe):
            for j in range(RT):
                pe.matmul(ps[:, j], k.const("head_ones"), y[:, j], start=True, stop=True).then_inc(mean_done, 1)
            for j in range(RT):
                pe.wait_ge(dev2_ready, j + 1)
                pe.matmul(ps[:, 4 + j], k.const("head_ones"), sq[:, j], start=True, stop=True).then_inc(var_done, 1)

        @block.scalar
        def _(act):
            for j in range(RT):
                act.wait_ge(dev_ready, j + 1)
                act.activation(sq[:, j], d[:, j], ACT.Square).then_inc(dev2_ready, 1)
            for j in range(RT):
                act.wait_ge(var_done, j + 1)
                act.activation(s[:, j], ps[:, 4 + j], ACT.Sqrt, scale=1.0 / 64, bias=k.eps[:, 1:2]).then_inc(sd_ready, 1)

        @block.vector
        def _(dve):
            link = chained(dve, gn_chain)
            for j in range(RT):
                dve.wait_ge(mean_done, j + 1)
                dve.scalar_tensor_tensor(d[:, j], ps[:, j], -1.0 / 64, y[:, j], ALU.mult, ALU.add).then_inc(dev_ready, 1)
            dve.wait_ge(sd_ready, RT)
            dve.wait_ge(dev_ready, RT)
            link(dve.reciprocal(s[:, :], s[:, :]))
            link(dve.tensor_tensor(d[:, :], d[:, :], s[:, :], ALU.mult))
            for j in range(RT):
                last = dve.tensor_scalar(d[:, j], d[:, j], k.vec("rw_ln_w", j), k.vec("rw_ln_b", j), ALU.mult, ALU.add)
            link(last)
            link(dve.tensor_tensor(d[:, :], d[:, :], bonus[:, :], ALU.add))
            link(dve.tensor_tensor(yg[:, :], d[:, :], g[:, :], ALU.mult))


def phase_mla_project(nc, k, io):
    xn = k.view(0, [KT, T])
    ring = [k.view(32 + 4 * s, [KT, P]) for s in range(4)]
    down = k.view(48, [5, T])
    sq = k.view(58, [5, T])
    rstd = k.view(68, [2, T])
    w_uq, w_ukv = k.view(72, [3, HEADS * QK]), k.view(81, [2, HEADS * 2 * NOPE])
    Q, K, V = k.view(90, [HEADS, T]), k.view(106, [HEADS, T]), k.view(122, [TT, HEADS * NOPE])
    cos, sin = k.view(130, [T]), k.view(132, [T])
    turned = k.view(134, [T])
    hsq, hsd = k.view(136, [2, T]), k.view(140, [2, T])
    pos, ang, turns, red = k.view(144, [T], I32), k.view(146, [T]), k.view(148, [T]), k.view(150, [T])
    w_in = io["w_in"].rearrange("(k p) n -> p k n", p=P)
    cols = [(Q_COL + n * P, P) for n in range(5)] + [(KPE_COL, ROPE)]
    rope = slice(NOPE, QK)
    items = [("q", h) for h in range(HEADS)] + [("k", h) for h in range(HEADS)]
    rows = [QK if kind == "q" or h == 0 else NOPE for kind, h in items]
    roped = [i for i in range(16) if rows[i] == QK]
    ps = k.ps
    TWO_PI = 2 * np.pi
    C1 = 6.28125
    C2 = float(np.float32(np.round((TWO_PI - C1) * 2 ** 20) / 2 ** 20))
    C3 = float(TWO_PI - C1 - C2)
    MAGIC = 1.5 * 2 ** 23
    with nc.Block() as block:
        w_ld = [k.sem(f"mla_w_ld{s}") for s in range(6)]
        up_ld, pos_ld, down_done, down_ready, dsq_ready, dss_done, dsd_ready, down_normed = map(
            k.sem, ("up_ld", "pos_ld", "down_done", "down_ready", "dsq_ready", "dss_done", "dsd_ready", "down_normed"))
        ang_ready, sin_ready, cos_in, head_done, head_ready, hsq_ready, hss_done, hsd_ready, head_normed = map(
            k.sem, ("ang_ready", "sin_ready", "cos_in", "head_done", "head_ready", "hsq_ready", "hss_done", "hsd_ready", "head_normed"))
        swap_done, roped_ready, mla_chain, v_done, v_ready, kpe_copied = map(
            k.sem, ("swap_done", "roped_ready", "mla_chain", "v_done", "v_ready", "kpe_copied"))

        @block.sync
        def _(sp):
            sp.dma_start(pos[0:QK], io["positions"].to_broadcast([QK, T])).then_inc(pos_ld, 16)
            for n, (col, m) in enumerate(cols):
                if n >= 4:
                    sp.wait_ge(down_done, n - 3)
                sp.dma_start(ring[n % 4][:, :, 0:m], w_in[:, :, col:col + m]).then_inc(w_ld[n], 16)
                if n == 3:
                    sp.dma_start(w_uq, io["mla_w_uq"].rearrange("(k p) n -> p k n", p=P)).then_inc(up_ld, 16)
                    sp.dma_start(w_ukv, io["mla_w_ukv"].rearrange("(k p) n -> p k n", p=P)).then_inc(up_ld, 16)

        @block.tensor
        def _(pe):
            for n in range(5):
                pe.wait_ge(w_ld[n], 16)
                for f in range(KT):
                    last = pe.matmul(ps[:, n], ring[n % 4][:, f], xn[:, f], start=f == 0, stop=f == KT - 1)
                last.then_inc(down_done, 1)
            for n in range(5):
                pe.wait_ge(dsq_ready, n + 1)
                last = pe.matmul(ps[:, 5 + n // 3], k.const("ones"), sq[:, n], start=n in (0, 3), stop=n in (2, 4))
                if n in (2, 4):
                    last.then_inc(dss_done, 1)
            pe.wait_ge(w_ld[5], 16)
            pe.wait_ge(up_ld, 32)

            def main(i):
                kind, h = items[i]
                if i == 0:
                    pe.wait_ge(down_normed, 3)
                    pe.wait_ge(down_ready, 5)
                if i == HEADS:
                    pe.wait_ge(down_normed, 5)
                if i >= 2:
                    pe.wait_ge(head_ready, i - 1)
                out = ps[:, i % 2]
                if kind == "q":
                    for f in range(3):
                        last = pe.matmul(out[0:QK], w_uq[:, f, h * QK:(h + 1) * QK], down[:, f], start=f == 0, stop=f == 2)
                else:
                    if h == 0:
                        for f in range(KT):
                            pe.matmul(out[rope], ring[1][:, f, 0:ROPE], xn[:, f], start=f == 0, stop=f == KT - 1)
                    for f in range(2):
                        last = pe.matmul(out[0:NOPE], w_ukv[:, f, h * P:h * P + NOPE], down[:, 3 + f], start=f == 0, stop=f == 1)
                last.then_inc(head_done, 1)

            def squares(i):
                pe.wait_ge(hsq_ready, i + 1)
                if i >= 2:
                    pe.wait_ge(hsd_ready, i - 1)
                m = rows[i]
                pe.matmul(ps[0:m, 2 + i % 2], k.const("qk_ones")[0:m, 0:m], hsq[0:m, i % 2], start=True, stop=True).then_inc(hss_done, 1)

            def swap(i):
                kind, h = items[i]
                n = roped.index(i)
                pe.wait_ge(head_normed, i + 1)
                if n >= 2:
                    pe.wait_ge(roped_ready, n - 1)
                pe.matmul(ps[0:QK, 4 + n % 2], k.const("rope_swap")[0:QK], (Q if kind == "q" else K)[0:QK, h],
                          start=True, stop=True).then_inc(swap_done, 1)

            pe.wait_ge(dsd_ready, 2)
            for i in range(18):
                if i < 16:
                    main(i)
                if 1 <= i <= 16:
                    squares(i - 1)
                if i >= 2 and i - 2 in roped:
                    swap(i - 2)
            for t in range(TT):
                if t >= 2:
                    pe.wait_ge(v_ready, t - 1)
                for f in range(2):
                    last = pe.matmul(ps[:, 6 + t % 2], down[:, 3 + f, t * P:(t + 1) * P],
                                     w_ukv[:, f].rearrange("p (h c) -> p h c", h=HEADS)[:, :, NOPE:], start=f == 0, stop=f == 1)
                last.then_inc(v_done, 1)

        @block.scalar
        def _(act):
            for n in range(5):
                act.wait_ge(down_done, n + 1)
                act.activation(sq[:, n], ps[:, n], ACT.Square).then_inc(dsq_ready, 1)
                act.activation(down[:, n], ps[:, n], ACT.Copy).then_inc(down_ready, 1)
            for n in range(2):
                act.wait_ge(dss_done, n + 1)
                act.activation(rstd[:, n], ps[:, 5 + n], ACT.Sqrt, scale=1.0 / (Q_LORA, KV_LORA)[n],
                               bias=k.eps[:, 0:1]).then_inc(dsd_ready, 1)
            act.wait_ge(ang_ready, 1)
            act.activation(sin[0:QK], sin[0:QK], ACT.Sin).then_inc(sin_ready, 1)
            act.wait_ge(cos_in, 1)
            act.activation(cos[0:QK], cos[0:QK], ACT.Sin).then_inc(sin_ready, 1)
            for i in range(17):
                if i < 16:
                    kind, h = items[i]
                    m = rows[i]
                    act.wait_ge(head_done, i + 1)
                    if i >= 2:
                        act.wait_ge(hss_done, i - 1)
                    act.activation(hsq[0:m, i % 2], ps[0:m, i % 2], ACT.Square).then_inc(hsq_ready, 1)
                    act.activation((Q if kind == "q" else K)[0:m, h], ps[0:m, i % 2], ACT.Copy).then_inc(head_ready, 1)
                if i:
                    m = rows[i - 1]
                    act.wait_ge(hss_done, i)
                    if i >= 3:
                        act.wait_ge(head_normed, i - 2)
                    act.activation(hsd[0:m, (i - 1) % 2], ps[0:m, 2 + (i - 1) % 2], ACT.Sqrt, bias=k.eps[0:m, 0:1]).then_inc(hsd_ready, 1)
            for t in range(TT):
                act.wait_ge(v_done, t + 1)
                act.activation(V[:, t], ps[:, 6 + t % 2], ACT.Copy).then_inc(v_ready, 1)

        @block.vector
        def _(dve):
            link = chained(dve, mla_chain)
            dve.wait_ge(pos_ld, 16)
            link(dve.tensor_copy(ang[0:QK], pos[0:QK]))
            link(dve.tensor_scalar(ang[0:QK], ang[0:QK], k.vec("inv_freq")[0:QK], None, ALU.mult))
            for table, quarter, ready in ((sin, 0.0, ang_ready), (cos, 0.25, cos_in)):
                link(dve.tensor_scalar(turns[0:QK], ang[0:QK], 1 / TWO_PI, quarter, ALU.mult, ALU.add))
                link(dve.tensor_scalar(turns[0:QK], turns[0:QK], MAGIC, None, ALU.add))
                link(dve.tensor_scalar(turns[0:QK], turns[0:QK], MAGIC, None, ALU.subtract))
                link(dve.scalar_tensor_tensor(red[0:QK], turns[0:QK], -C1, ang[0:QK], ALU.mult, ALU.add))
                link(dve.scalar_tensor_tensor(red[0:QK], turns[0:QK], -C2, red[0:QK], ALU.mult, ALU.add))
                link(dve.scalar_tensor_tensor(red[0:QK], turns[0:QK], -C3, red[0:QK], ALU.mult, ALU.add))
                link(dve.tensor_scalar(red[0:QK], red[0:QK], quarter * TWO_PI, None, ALU.add))
                dve.tensor_scalar(table[0:QK], red[0:QK], float(np.float32(3.1415925)), -float(np.float32(3.1415925)),
                                  ALU.min, ALU.max).then_inc(ready, 1)
                dve.wait_ge(ready, 1)
            for n in range(2):
                dve.wait_ge(dsd_ready, n + 1)
                link(dve.reciprocal(rstd[:, n], rstd[:, n]))
                for f in ((0, 1, 2), (3, 4))[n]:
                    dve.wait_ge(down_ready, f + 1)
                    dve.scalar_tensor_tensor(down[:, f], down[:, f], k.vec("mla_q_norm_w", f), rstd[:, n],
                                             ALU.mult, ALU.mult).then_inc(down_normed, 1)
            dve.wait_ge(sin_ready, 2)

            def turn(i):
                kind, h = items[i]
                n = roped.index(i)
                x = (Q if kind == "q" else K)[rope, h]
                dve.wait_ge(swap_done, n + 1)
                link(dve.tensor_tensor(turned[rope], ps[rope, 4 + n % 2], sin[rope], ALU.mult))
                link(dve.tensor_tensor(x, x, cos[rope], ALU.mult))
                dve.tensor_tensor(x, x, turned[rope], ALU.add).then_inc(roped_ready, 1)
                dve.wait_ge(roped_ready, n + 1)

            for i in range(17):
                if i < 16:
                    kind, h = items[i]
                    m = rows[i]
                    x = (Q if kind == "q" else K)[0:m, h]
                    dve.wait_ge(hsd_ready, i + 1)
                    dve.wait_ge(head_ready, i + 1)
                    link(dve.reciprocal(hsd[0:m, i % 2], hsd[0:m, i % 2]))
                    dve.scalar_tensor_tensor(x, x, k.vec("qn_w" if kind == "q" else "kn_w")[0:m], hsd[0:m, i % 2],
                                             ALU.mult, ALU.mult).then_inc(head_normed, 1)
                if i and i - 1 in roped:
                    turn(i - 1)

        @block.gpsimd
        def _(pool):
            pool.wait_ge(roped_ready, len(roped))
            for h in range(1, HEADS):
                pool.tensor_copy(K[rope, h], K[rope, 0]).then_inc(kpe_copied, 1)


def phase_attention(nc, k, io):
    Q, K, V = k.view(90, [HEADS, T]), k.view(106, [HEADS, T]), k.view(122, [TT, HEADS * NOPE])
    oT = k.view(24, [RT, T])
    probs, probsT, diag = k.view(130, [2, T]), k.view(134, [2, TT, P]), k.view(138, [2, P])
    mx, nb, rs, ri = (k.view(140 + n, [32]) for n in range(4))
    scale = float(1.0 / np.sqrt(QK))
    units = [(h, q) for h in range(HEADS) for q in range(TT)]
    ps = k.ps
    with nc.Block() as block:
        s_done, masked, max_ready, nb_ready, exp_ready, diag_ready, pt_done, pt_out, o_done, o_out, rinv_ready = map(
            k.sem, ("s_done", "masked", "max_ready", "nb_ready", "exp_ready", "diag_ready", "pt_done", "pt_out", "o_done2", "o_out", "rinv_ready"))

        @block.tensor
        def _(pe):
            def scores(u):
                h, q = units[u]
                if u >= 2:
                    pe.wait_ge(exp_ready, u - 1)
                n = (q + 1) * P
                pe.matmul(ps[:, u % 2, 0:n], Q[0:QK, h, q * P:n], K[0:QK, h, 0:n], start=True, stop=True).then_inc(s_done, 1)

            def weighted(u):
                h, q = units[u]
                half = slice(64 * (h % 2), 64 * (h % 2) + 64)
                pe.wait_ge(diag_ready, u + 1)
                if u >= 2:
                    pe.wait_ge(pt_out, u - 1)
                for t in range(q + 1):
                    last = pe.matmul(ps[:, 2 + u % 2, t * P:(t + 1) * P], probs[:, u % 2, t * P:(t + 1) * P],
                                     diag[:, u % 2], start=True, stop=True)
                last.then_inc(pt_done, 1)

            def values(u):
                h, q = units[u]
                half = slice(64 * (h % 2), 64 * (h % 2) + 64)
                pe.wait_ge(pt_out, u + 1)
                if q == 0 and h >= 2:
                    pe.wait_ge(o_out, h - 1)
                for t in range(q + 1):
                    last = pe.matmul(ps[half, 4 + h % 2, q * P:(q + 1) * P], V[:, t, h * NOPE:(h + 1) * NOPE],
                                     probsT[:, u % 2, t], start=t == 0, stop=t == q)
                last.then_inc(o_done, 1)

            for u in range(len(units) + 2):
                if u < len(units):
                    scores(u)
                if 1 <= u <= len(units):
                    weighted(u - 1)
                if u >= 2:
                    values(u - 2)

        @block.vector
        def _(dve):
            def top(u):
                h, q = units[u]
                dve.wait_ge(s_done, u + 1)
                own = ps[:, u % 2, q * P:(q + 1) * P]
                dve.tensor_tensor(own, own, k.const("causal"), ALU.add).then_inc(masked, 1)
                dve.wait_ge(masked, u + 1)
                dve.reduce_max(mx[:, u:u + 1], ps[:, u % 2, 0:(q + 1) * P], AX.X).then_inc(max_ready, 1)
                dve.wait_ge(max_ready, u + 1)
                dve.tensor_scalar(nb[:, u:u + 1], mx[:, u:u + 1], -scale, None, ALU.mult).then_inc(nb_ready, 1)

            def bottom(u):
                dve.wait_ge(exp_ready, u + 1)
                if u >= 2:
                    dve.wait_ge(pt_done, u - 1)
                dve.reciprocal(ri[:, u:u + 1], rs[:, u:u + 1]).then_inc(rinv_ready, 1)
                dve.wait_ge(rinv_ready, u + 1)
                dve.tensor_scalar(diag[:, u % 2], k.const("ident"), ri[:, u:u + 1], None, ALU.mult).then_inc(diag_ready, 1)

            def turned(u):
                h, q = units[u]
                dve.wait_ge(pt_done, u + 1)
                if u >= 2:
                    dve.wait_ge(o_done, u - 1)
                dve.tensor_copy(probsT[:, u % 2, 0:q + 1], ps[:, 2 + u % 2, 0:(q + 1) * P].rearrange("p (t c) -> p t c", c=P)).then_inc(pt_out, 1)

            for u in range(len(units) + 1):
                if u < len(units):
                    top(u)
                    bottom(u)
                if u:
                    turned(u - 1)

        @block.scalar
        def _(act):
            def copy_out(h):
                half = slice(64 * (h % 2), 64 * (h % 2) + 64)
                act.wait_ge(o_done, TT * (h + 1))
                act.activation(oT[half, h // 2], ps[half, 4 + h % 2], ACT.Copy).then_inc(o_out, 1)

            for u, (h, q) in enumerate(units):
                act.wait_ge(nb_ready, u + 1)
                if u >= 2:
                    act.wait_ge(pt_done, u - 1)
                n = (q + 1) * P
                act.activation(probs[:, u % 2, 0:n], ps[:, u % 2, 0:n], ACT.Exp, scale=scale, bias=nb[:, u:u + 1],
                               accum_out=rs[:, u:u + 1]).then_inc(exp_ready, 1)
                if q == 1 and h:
                    copy_out(h - 1)
            copy_out(HEADS - 1)


def phase_merge(nc, k, io):
    xn, yg, oT = k.view(0, [KT, T]), k.view(16, [RT, T]), k.view(24, [RT, T])
    hT = k.view(32, [KT, T])
    mixed = k.view(48, [KT, T])
    gate_ring = [k.view(64 + 4 * s, [KT, P]) for s in range(6)]
    out_ring = [k.view(88 + 2 * s, [RT, P]) for s in range(6)]
    xres = k.view(100, [KT, T])
    ga, gb = k.view(116, [2, T]), k.view(120, [2, T])
    ps = k.ps
    part = lambda w: w.rearrange("(k p) n -> p k n", p=P)
    w_in, w_a, w_b, w_out = (part(io[n]) for n in ("w_in", "rw_w_o", "mla_w_o", "w_out"))
    with nc.Block() as block:
        gate_ld = [k.sem(f"gate_ld{s}") for s in range(6)]
        out_ld = [k.sem(f"out_ld{s}") for s in range(6)]
        x_ld, g_done, y_done, gate_ready, part_ready, mixed_ready, h_done, h_ready = map(
            k.sem, ("xres_ld", "mg_done", "my_done", "gate_ready", "part_ready", "mixed_ready", "h_done", "h_ready"))
        loads = [(w_in, col + n * P) for n in range(KT) for col in (GA_COL, GB_COL)] + [(w_out, n * P) for n in range(KT)]

        @block.sync
        def _(sp):
            sp.dma_start(xres, io["xT"].rearrange("(k p) n -> p k n", p=P)).then_inc(x_ld, 16)
            for n, (w, col) in enumerate(loads):
                if n >= 6:
                    old = n - 6
                    if old < 2 * KT:
                        sp.wait_ge(g_done, old + 1)
                    else:
                        sp.wait_ge(h_done, old - 2 * KT + 1)
                sp.dma_start(gate_ring[n % 6], w[:, :, col:col + P]).then_inc(gate_ld[n % 6], 16)
                if n < 2 * KT:
                    if n >= 6:
                        sp.wait_ge(y_done, n - 5)
                    sp.dma_start(out_ring[n % 6], (w_a, w_b)[n % 2][:, :, n // 2 * P:(n // 2 + 1) * P]).then_inc(out_ld[n % 6], 16)

        @block.tensor
        def _(pe):
            for n in range(2 * KT):
                pe.wait_ge(gate_ld[n % 6], 16 * (n // 6 + 1))
                if n >= 4:
                    pe.wait_ge(gate_ready, n - 3)
                for f in range(KT):
                    last = pe.matmul(ps[:, n % 4], gate_ring[n % 6][:, f], xn[:, f], start=f == 0, stop=f == KT - 1)
                last.then_inc(g_done, 1)
                pe.wait_ge(out_ld[n % 6], 16 * (n // 6 + 1))
                if n >= 4:
                    pe.wait_ge(part_ready, n - 3)
                for f in range(RT):
                    last = pe.matmul(ps[:, 4 + n % 4], out_ring[n % 6][:, f], (yg, oT)[n % 2][:, f], start=f == 0, stop=f == RT - 1)
                last.then_inc(y_done, 1)
            for n in range(KT):
                m = 2 * KT + n
                pe.wait_ge(gate_ld[m % 6], 16 * (m // 6 + 1))
                if n == 0:
                    pe.wait_ge(gate_ready, 2 * KT)
                if n >= 4:
                    pe.wait_ge(h_ready, n - 3)
                for f in range(KT):
                    if n == 0:
                        pe.wait_ge(mixed_ready, f + 1)
                    last = pe.matmul(ps[:, n % 4], gate_ring[m % 6][:, f], mixed[:, f], start=f == 0, stop=f == KT - 1)
                last.then_inc(h_done, 1)

        @block.scalar
        def _(act):
            for n in range(2 * KT):
                act.wait_ge(g_done, n + 1)
                if n >= 4:
                    act.wait_ge(mixed_ready, n // 2 - 1)
                act.activation((ga, gb)[n % 2][:, n // 2 % 2], ps[:, n % 4], ACT.Sigmoid).then_inc(gate_ready, 1)

        @block.vector
        def _(dve):
            for n in range(2 * KT):
                dve.wait_ge(gate_ready, n + 1)
                dve.wait_ge(y_done, n + 1)
                g = (ga, gb)[n % 2][:, n // 2 % 2]
                dve.tensor_tensor(g, g, ps[:, 4 + n % 4], ALU.mult).then_inc(part_ready, 1)
                if n % 2:
                    dve.wait_ge(part_ready, n + 1)
                    dve.tensor_tensor(mixed[:, n // 2], ga[:, n // 2 % 2], g, ALU.add).then_inc(mixed_ready, 1)
            dve.wait_ge(x_ld, 16)
            for n in range(KT):
                dve.wait_ge(h_done, n + 1)
                dve.tensor_tensor(hT[:, n], ps[:, n % 4], xres[:, n], ALU.add).then_inc(h_ready, 1)


def phase_route_scores(nc, k, io):
    hT, hn, h_hi, h_lo = k.view(32, [KT, T]), k.view(0, [KT, T]), k.view(16, [KT, T], F16), k.view(24, [KT, T], F16)
    ring = [k.view(48 + 4 * s, [KT, P]) for s in range(4)]
    qT = k.view(64, [2, T])
    subk = k.view(68, [2 * PH, NK])
    sq, rstd = k.view(76, [KT, T]), k.view(92, [T])
    sc = k.view(96, [TT, 2 * PH, NK])
    top, top_i = k.top, k.top_i
    rest = k.view(94, [2, NK])
    w_q = io["peer_w_query"].rearrange("(k p) n -> p k n", p=P)
    ps = k.ps
    with nc.Block() as block:
        w_ld = [k.sem(f"w_ld{s}") for s in range(4)]
        subk_ld, sq_ready, ss_done, rt_ready, rstd_ready, hn_ready, hi_ready, lo_ready = map(
            k.sem, ("subk_ld", "sq_ready", "ss_done", "rt_ready", "rstd_ready", "hn_ready", "hi_ready", "lo_ready"))
        q_done, q_out, sc_done, sc_out, top_step = map(k.sem, ("q_done", "q_out", "sc_done", "sc_out", "top_step"))

        @block.sync
        def _(sp):
            sp.dma_start(subk, io["sub_keysT"]).then_inc(subk_ld, 16)
            for n in range(2 * PH):
                if n >= 4:
                    sp.wait_ge(q_done, n - 3)
                sp.dma_start(ring[n % 4], w_q[:, :, n * P:(n + 1) * P]).then_inc(w_ld[n % 4], 16)

        @block.tensor
        def _(pe):
            for n in range(KT):
                pe.wait_ge(sq_ready, n + 1)
                last = pe.matmul(ps[:, 0], k.const("ones"), sq[:, n], start=n == 0, stop=n == KT - 1)
            last.then_inc(ss_done, 1)

            def scores(n):
                pe.wait_ge(q_out, n + 1)
                if n >= 2:
                    pe.wait_ge(sc_out, n - 1)
                for t in range(TT):
                    last = pe.matmul(ps[:, 3 + n % 2, t * P:(t + 1) * P], qT[:, n % 2, t * P:(t + 1) * P], subk[:, n],
                                     start=True, stop=True)
                last.then_inc(sc_done, 1)

            pe.wait_ge(subk_ld, 16)
            for n in range(2 * PH):
                pe.wait_ge(w_ld[n % 4], 16 * (n // 4 + 1))
                if n >= 2:
                    pe.wait_ge(q_out, n - 1)
                for f in range(KT):
                    if n == 0:
                        pe.wait_ge(hn_ready, f + 1)
                    last = pe.matmul(ps[:, 1 + n % 2], ring[n % 4][:, f], hn[:, f], start=f == 0, stop=f == KT - 1)
                last.then_inc(q_done, 1)
                if n:
                    scores(n - 1)
            scores(2 * PH - 1)

        @block.scalar
        def _(act):
            for n in range(KT):
                act.activation(sq[:, n], hT[:, n], ACT.Square).then_inc(sq_ready, 1)
            act.wait_ge(ss_done, 1)
            act.activation(rstd, ps[:, 0], ACT.Sqrt, scale=1.0 / D, bias=k.eps[:, 0:1]).then_inc(rt_ready, 1)
            for n in range(KT):
                act.wait_ge(hn_ready, n + 1)
                act.activation(h_hi[:, n], hn[:, n], ACT.Copy).then_inc(hi_ready, 1)

            def score_copy(n):
                act.wait_ge(sc_done, n + 1)
                act.activation(sc[:, :, n], ps[:, 3 + n % 2].rearrange("p (t n) -> p t n", t=TT), ACT.Copy).then_inc(sc_out, 1)

            for n in range(2 * PH):
                act.wait_ge(q_done, n + 1)
                if n >= 2:
                    act.wait_ge(sc_done, n - 1)
                act.activation(qT[:, n % 2], ps[:, 1 + n % 2], ACT.Copy).then_inc(q_out, 1)
                if n:
                    score_copy(n - 1)
            score_copy(2 * PH - 1)

        @block.vector
        def _(dve):
            dve.wait_ge(rt_ready, 1)
            dve.reciprocal(rstd, rstd).then_inc(rstd_ready, 1)
            dve.wait_ge(rstd_ready, 1)
            for n in range(KT):
                dve.scalar_tensor_tensor(hn[:, n], hT[:, n], k.vec("norm2_w", n), rstd, ALU.mult, ALU.mult).then_inc(hn_ready, 1)
            for n in range(KT):
                dve.wait_ge(hi_ready, n + 1)
                dve.tensor_tensor(h_lo[:, n], hn[:, n], h_hi[:, n], ALU.subtract).then_inc(lo_ready, 1)
            steps = 0
            for n in range(2 * PH):
                dve.wait_ge(sc_out, n + 1)
                for t in range(0, TT, 2):
                    two = [(sc[:, t + b, n], top[:, t + b, n], top_i[:, t + b, n], rest[:, b]) for b in range(2)]
                    if steps:
                        dve.wait_ge(top_step, steps)
                    for stage in (lambda s, v, i, r: dve.max(v[:, 0:8], s),
                                  lambda s, v, i, r: dve.max_index(i[:, 0:8], v[:, 0:8], s),
                                  lambda s, v, i, r: dve.match_replace(r, v[:, 0:8], s, -3.0e38),
                                  lambda s, v, i, r: dve.max(v[:, 8:16], r),
                                  lambda s, v, i, r: dve.max_index(i[:, 8:16], v[:, 8:16], r)):
                        for b in range(2):
                            stage(*two[b]).then_inc(top_step, 1)
                        steps += 2
                        dve.wait_ge(top_step, steps)


def phase_route_picks(nc, k, io):
    top, top_i = k.top, k.top_i
    cand, rest = k.view(48, [PH, 256]), k.view(56, [2, 256])
    best, best_i = k.view(58, [PH, TOPK]), k.view(59, [PH, TOPK], U32)
    pos = k.view(60, [2, PICKS], U32)
    posf, keyf = k.view(61, [2, PICKS]), k.view(62, [2 * PH, TOPK])
    hit = k.view(64, [PICKS, TOPK])
    picked = k.view(72, [3, PICKS])
    gsum = k.view(74, [PH])
    picksT = k.picksT
    iota16 = k.const("iota")[:, 0:TOPK].unsqueeze(1).to_broadcast([P, PICKS, TOPK])
    ps = k.ps
    with nc.Block() as block:
        step, gate_in, gate_exp, picked_ready, turn_done, turn_out = map(
            k.sem, ("step", "gate_in", "gate_exp", "picked_ready", "turn_done", "turn_out"))

        @block.tensor
        def _(pe):
            for t in range(TT):
                pe.wait_ge(picked_ready, t + 1)
                for n in range(3):
                    last = pe.matmul(ps[:, n, t * P:(t + 1) * P], picked[:, n], k.const("ident"), start=True, stop=True)
                last.then_inc(turn_done, 1)

        @block.scalar
        def _(act):
            for t in range(TT):
                act.wait_ge(gate_in, t + 1)
                act.activation(picked[:, 2], picked[:, 2], ACT.Exp).then_inc(gate_exp, 1)
            act.wait_ge(turn_done, TT)
            for n in range(3):
                act.activation(picksT[:, n], ps[:, n], ACT.Copy).then_inc(turn_out, 1)

        @block.vector
        def _(dve):
            link = chained(dve, step)
            for t in range(TT):
                pair = top[:, t].rearrange("p (h s) a -> p s h a", s=2)
                first, second = pair[:, 0], pair[:, 1]
                link(dve.tensor_copy(keyf[:, :, :], top_i[:, t]))
                link(dve.tensor_tensor(cand.rearrange("p h (a b) -> p h a b", a=TOPK),
                                       first.unsqueeze(3).to_broadcast([P, PH, TOPK, TOPK]),
                                       second.unsqueeze(2).to_broadcast([P, PH, TOPK, TOPK]), ALU.add))
                for h in range(0, PH, 2):
                    two = [(cand[:, h + b], best[:, h + b], best_i[:, h + b], rest[:, b]) for b in range(2)]
                    for stage in (lambda s, v, i, r: dve.max(v[:, 0:8], s),
                                  lambda s, v, i, r: dve.max_index(i[:, 0:8], v[:, 0:8], s),
                                  lambda s, v, i, r: dve.match_replace(r, v[:, 0:8], s, -3.0e38),
                                  lambda s, v, i, r: dve.max(v[:, 8:16], r),
                                  lambda s, v, i, r: dve.max_index(i[:, 8:16], v[:, 8:16], r)):
                        for b in range(2):
                            link(stage(*two[b]))
                if t:
                    dve.wait_ge(turn_done, t)
                flat_i = best_i.rearrange("p h a -> p (h a)")
                link(dve.tensor_scalar(pos[:, 0], flat_i, 4, None, ALU.logical_shift_right))
                link(dve.tensor_scalar(pos[:, 1], flat_i, 15, None, ALU.bitwise_and))
                link(dve.tensor_copy(posf[:, :, :], pos[:, :, :]))
                dve.tensor_tensor(picked[:, 2].rearrange("p (h a) -> p h a", h=PH), best[:, :, :],
                                  best[:, :, 0:1].to_broadcast([P, PH, TOPK]), ALU.subtract).then_inc(gate_in, 1)
                keys = keyf.rearrange("p (h s) a -> p s h a", s=2)
                for n in range(2):
                    link(dve.tensor_tensor(hit[:, :, :], posf[:, n].unsqueeze(2).to_broadcast([P, PICKS, TOPK]), iota16, ALU.is_equal))
                    link(dve.tensor_tensor(hit.rearrange("p (h q) a -> p h q a", h=PH), hit.rearrange("p (h q) a -> p h q a", h=PH),
                                           keys[:, n].unsqueeze(2).to_broadcast([P, PH, TOPK, TOPK]), ALU.mult))
                    link(dve.tensor_reduce(picked[:, n], hit[:, :, :], AX.X, ALU.add))
                dve.wait_ge(gate_exp, t + 1)
                gates = picked[:, 2].rearrange("p (h a) -> p h a", h=PH)
                link(dve.tensor_reduce(gsum, gates, AX.X, ALU.add))
                link(dve.reciprocal(gsum, gsum))
                dve.tensor_tensor(gates, gates, gsum.unsqueeze(2).to_broadcast([P, PH, TOPK]), ALU.mult).then_inc(picked_ready, 1)
                dve.wait_ge(picked_ready, t + 1)


STAGE = 64


def phase_gate_matrix(nc, k, io):
    key1, key2, gate = (k.picksT[:, n] for n in range(3))
    SL = 8
    one_j, gated_i = k.view(48, [SL, NK]), k.view(52, [SL, NK])
    stage = [k.view(56 + 32 * s, [NK, STAGE]) for s in range(2)]
    Gd = io["gates"].rearrange("i j t -> j i t")
    ps = k.ps
    with nc.Block() as block:
        hot_ready, g_done, staged = map(k.sem, ("hot_ready", "g_done", "staged"))
        stored = [k.sem(f"stored{s}") for s in range(2)]
        ROUNDS = T // (2 * STAGE)

        def rounds(eng, body):
            body(0)
            with eng.Fori(1, ROUNDS) as it:
                body(it)

        def wait(eng, sem, value):
            if not isinstance(value, int) or value > 0:
                eng.wait_ge(sem, value)

        @block.vector
        def _(dve):
            def body(it):
                for t in range(2 * STAGE):
                    at = it * 2 * STAGE + t
                    if t >= SL:
                        dve.wait_ge(g_done, at - SL + 1)
                    else:
                        wait(dve, g_done, it * 2 * STAGE)
                    dve.tensor_scalar(one_j[:, t % SL], k.const("iota"), key2[:, bass.ds(at, 1)], None, ALU.is_equal)
                    dve.tensor_scalar(gated_i[:, t % SL], k.const("iota"), key1[:, bass.ds(at, 1)], gate[:, bass.ds(at, 1)],
                                      ALU.is_equal, ALU.mult).then_inc(hot_ready, 1)
            rounds(dve, body)

        @block.tensor
        def _(pe):
            def body(it):
                for t in range(2 * STAGE):
                    if t % 4 == 0:
                        wait(pe, staged, it * (2 * STAGE // 4) + max(t // 4 - 7, 0))
                    pe.wait_ge(hot_ready, it * 2 * STAGE + t + 1)
                    pe.matmul(ps[:, t // 4 % 8, t % 4 * P:(t % 4 + 1) * P], one_j[:, t % SL], gated_i[:, t % SL],
                              start=True, stop=True).then_inc(g_done, 1)
            rounds(pe, body)

        @block.scalar
        def _(act):
            def body(it):
                for q in range(2 * STAGE // 4):
                    s, at = divmod(4 * q, STAGE)
                    if at == 0:
                        wait(act, stored[s], it * 16)
                    act.wait_ge(g_done, it * 2 * STAGE + 4 * q + 4)
                    act.activation(stage[s][:, :, at:at + 4].rearrange("p i t -> p t i"),
                                   ps[:, q % 8].rearrange("p (t i) -> p t i", t=4), ACT.Copy).then_inc(staged, 1)
            rounds(act, body)

        @block.sync
        def _(sp):
            def body(it):
                for s in range(2):
                    sp.wait_ge(staged, it * (2 * STAGE // 4) + (s + 1) * (STAGE // 4))
                    sp.dma_start(Gd[:, :, bass.ds(it * 2 * STAGE + s * STAGE, STAGE)], stage[s]).then_inc(stored[s], 16)
            rounds(sp, body)
            for s in range(2):
                sp.wait_ge(stored[s], 16 * ROUNDS)


SCALE = 256.0
GROUP = 4


def phase_experts(nc, k, io):
    h_hi, h_lo, y = k.view(16, [KT, T], F16), k.view(24, [KT, T], F16), k.view(32, [KT, T])
    u_raw, v_raw = k.view(48, [4, KT, P]), k.view(64, [4, D])
    u_hi, u_lo = k.view(80, [4, KT, P], F16), k.view(88, [4, KT, P], F16)
    v_hi, v_lo = k.view(96, [8, D], F16), k.view(112, [8, D], F16)
    a_hi, a_lo = k.view(128, [8, T], F16), k.view(136, [8, T], F16)
    G = k.view(144, [8, T])
    acts = k.view(160, [2, T])
    uT, v, Gd = io["uT"], io["peer_v"].rearrange("(i j) d -> i j d", j=NK), io["gates"]
    out = io["outT"].rearrange("(k p) t -> p k t", p=P)
    ps = k.ps
    N = NK
    with nc.Block() as block:
        u_ld, v_ld = ([k.sem(f"{x}_ld{s}") for s in range(4)] for x in "uv")
        g_ld = [k.sem(f"g_ld{s}") for s in range(8)]
        u_hi_ready, u_lo_ready, v_hi_ready, v_lo_ready, act_ready, weighted, a_hi_ready, a_ready = map(
            k.sem, ("u_hi_ready", "u_lo_ready", "v_hi_ready", "v_lo_ready", "act_ready", "weighted", "a_hi_ready", "a_ready"))
        act_done, out_done, y_added, stored = map(k.sem, ("act_done", "out_done", "y_added", "stored"))

        def wait(eng, sem, value):
            if not isinstance(value, int) or value > 0:
                eng.wait_ge(sem, value)

        def steps(eng, step):
            for r in range(8):
                step(0, r, r)
            with eng.Fori(1, N // 8 - 1) as it:
                for r in range(8):
                    step(it, r, it * 8 + r)
            for r in range(8):
                step(N // 8 - 1, r, N - 8 + r)
            for r in range(GROUP):
                step(N // 8, r, N + r)

        def tile_of(n):
            return not isinstance(n, int) or n < N

        @block.sync
        def _(sp):
            def step(it, r, n):
                if tile_of(n):
                    wait(sp, u_lo_ready, n - 3)
                    sp.dma_start(u_raw[:, r % 4], uT[bass.ds(n, 1)].rearrange("i p f e -> (i p) f e")).then_inc(u_ld[r % 4], 16)
                    wait(sp, v_lo_ready, n - 3)
                    sp.dma_start(v_raw[:, r % 4], v[bass.ds(n, 1)].rearrange("i j d -> (i j) d")).then_inc(v_ld[r % 4], 16)
                    wait(sp, weighted, n - 7)
                    sp.dma_start(G[:, r], Gd[bass.ds(n, 1)].rearrange("i j t -> (i j) t")).then_inc(g_ld[r], 16)
            steps(sp, step)
            sp.wait_ge(y_added, N // GROUP * KT)
            sp.dma_start(out, y).then_inc(stored, 16)
            sp.wait_ge(stored, 16)

        @block.scalar
        def _(act):
            def split_u(it, r, m):
                act.wait_ge(u_ld[r % 4], (it * 2 + r // 4 + 1) * 16)
                wait(act, act_done, m - 3)
                act.activation(u_hi[:, r % 4], u_raw[:, r % 4], ACT.Copy, scale=SCALE).then_inc(u_hi_ready, 1)

            def step(it, r, n):
                if isinstance(n, int) and n == 0:
                    split_u(0, 0, 0)
                    split_u(0, 1, 1)
                if tile_of(n) and (not isinstance(n, int) or n + 2 < N):
                    split_u(it + (r + 2) // 8, (r + 2) % 8, n + 2)
                if tile_of(n):
                    act.wait_ge(v_ld[r % 4], (it * 2 + r // 4 + 1) * 16)
                    wait(act, out_done, ((it * 2) + r // 4 - 1) * KT)
                    act.activation(v_hi[:, r], v_raw[:, r % 4], ACT.Copy, scale=SCALE).then_inc(v_hi_ready, 1)
                    act.wait_ge(act_done, n + 1)
                    wait(act, a_ready, n - 1)
                    act.activation(acts[:, r % 2], ps[:, r % 2], ACT.Gelu, scale=1 / SCALE).then_inc(act_ready, 1)
            steps(act, step)

        @block.vector
        def _(dve):
            def split_u(r, m):
                dve.wait_ge(u_hi_ready, m + 1)
                dve.scalar_tensor_tensor(u_lo[:, r % 4], u_raw[:, r % 4], SCALE, u_hi[:, r % 4],
                                         ALU.mult, ALU.subtract).then_inc(u_lo_ready, 1)

            def step(it, r, n):
                if isinstance(n, int) and n == 0:
                    split_u(0, 0)
                    split_u(1, 1)
                if tile_of(n) and (not isinstance(n, int) or n + 2 < N):
                    split_u(r + 2, n + 2)
                if tile_of(n):
                    dve.wait_ge(v_hi_ready, n + 1)
                    dve.scalar_tensor_tensor(v_lo[:, r], v_raw[:, r % 4], SCALE, v_hi[:, r],
                                             ALU.mult, ALU.subtract).then_inc(v_lo_ready, 1)
                    dve.wait_ge(act_ready, n + 1)
                    dve.wait_ge(g_ld[r], (it + 1) * 16)
                    x = acts[:, r % 2]
                    dve.tensor_tensor(x, x, G[:, r], ALU.mult).then_inc(weighted, 1)
                    dve.wait_ge(weighted, n + 1)
                    wait(dve, out_done, ((it * 2) + r // 4 - 1) * KT)
                    dve.tensor_copy(a_hi[:, r], x).then_inc(a_hi_ready, 1)
                    dve.wait_ge(a_hi_ready, n + 1)
                    dve.tensor_tensor(a_lo[:, r], x, a_hi[:, r], ALU.subtract).then_inc(a_ready, 1)
                if not (isinstance(n, int) and n < GROUP):
                    for b in range(2):
                        d = 2 * (r % 4) + b
                        nth = (it * 2 + r // 4 - 1) * KT + d
                        dve.wait_ge(out_done, nth + 1)
                        wait(dve, y_added, nth + 1 - KT)
                        dve.scalar_tensor_tensor(y[:, d], ps[:, 2 + d % 4], 1 / SCALE, y[:, d], ALU.mult, ALU.add).then_inc(y_added, 1)
            steps(dve, step)

        @block.tensor
        def _(pe):
            def step(it, r, n):
                if tile_of(n):
                    pe.wait_ge(u_lo_ready, n + 1)
                    wait(pe, act_ready, n - 1)
                    for f in range(KT):
                        for w, x in ((u_hi, h_hi), (u_hi, h_lo), (u_lo, h_hi)):
                            last = pe.matmul(ps[:, r % 2], w[:, r % 4, f], x[:, f],
                                             start=f == 0 and x is h_hi and w is u_hi, stop=f == KT - 1 and w is u_lo)
                    last.then_inc(act_done, 1)
                if not (isinstance(n, int) and n < GROUP):
                    group = it * 2 + r // 4 - 1
                    if r % 4 == 0:
                        pe.wait_ge(a_ready, (group + 1) * GROUP)
                        pe.wait_ge(v_lo_ready, (group + 1) * GROUP)
                    for b in range(2):
                        d = 2 * (r % 4) + b
                        wait(pe, y_added, group * KT + d - 3)
                        for q in range(GROUP):
                            s = (r // 4 + 1) % 2 * 4 + q
                            for w, x in ((v_hi, a_hi), (v_hi, a_lo), (v_lo, a_hi)):
                                last = pe.matmul(ps[:, 2 + d % 4], w[:, s, d * P:(d + 1) * P], x[:, s],
                                                 start=q == 0 and x is a_hi and w is v_hi, stop=q == GROUP - 1 and w is v_lo)
                        last.then_inc(out_done, 1)
            steps(pe, step)


def laid_out(inputs):
    get = lambda n: np.asarray(inputs[n])
    q_w = np.concatenate([get("mla_qn_nope_w"), get("mla_qn_pe_w")])
    k_w = np.concatenate([get("mla_kn_nope_w"), get("mla_kn_pe_w")])
    half = ROPE // 2
    freq = (np.float32(10000.0) ** (-np.arange(half, dtype=np.float32) / np.float32(half))).astype(np.float32)
    given = {"qn_w": q_w, "kn_w": k_w, "rw_mu": get("rw_mu")[:14 * P], "rw_mu_tail": get("rw_mu")[14 * P:],
             "inv_freq": np.concatenate([np.zeros(NOPE, np.float32), freq, freq])}
    columns = []
    for name, rows, tiles in VECS:
        v = given[name] if name in given else get(name).reshape(-1)
        padded = np.zeros((P, tiles), np.float32)
        padded[:rows] = v.reshape(tiles, rows).T
        columns.append(padded)
    out = {"xT": get("x")[0].T, "positions": get("positions"), "vecs": np.concatenate(columns, axis=1),
           "consts": constant_array()}
    for name in ("w_in", "rw_w2", "rw_a2", "rw_g2", "rw_w_o", "mla_w_uq", "mla_w_ukv", "mla_w_o", "w_out",
                 "peer_w_query", "peer_v"):
        out[name] = get(name)
    out["sub_keysT"] = get("peer_sub_keys").reshape(2 * PH, NK, P).transpose(2, 0, 1)
    out["uT"] = get("peer_u").reshape(NK, NK, KT, P).transpose(0, 3, 2, 1)
    return {name: np.ascontiguousarray(a) for name, a in out.items()}




def build(nc, io, upto=99, dbg=None):
    with ExitStack() as ctx:
        k = Kit()
        arena = ctx.enter_context(nc.sbuf_tensor("arena", [P, ARENA_KB * 256], F32))
        k.consts = ctx.enter_context(nc.sbuf_tensor("consts", [P, NCONST], F32))
        k.vecs = ctx.enter_context(nc.sbuf_tensor("vecs", [P, NV], F32))
        k.eps = ctx.enter_context(nc.sbuf_tensor("eps", [P, 2], F32))
        k.chunk_decay = ctx.enter_context(nc.sbuf_tensor("chunk_decay", [P, RT, NCH], F32))
        k.ps = ctx.enter_context(nc.psum_tensor("ps", [P, 8, 512], F32))

        io = dict(io, gates=nc.dram_tensor("gates", (NK, NK, T), F32, kind="Internal").ap())

        def view(at_kb, shape, dtype=F32):
            words = int(np.prod(shape)) * mybir.dt.size(dtype) // 4
            a = arena[:, at_kb * 256:at_kb * 256 + words]
            if dtype != F32:
                a = a.bitcast(dtype)
            if len(shape) > 1:
                names = "abcd"[:len(shape)]
                a = a.rearrange(f"p ({' '.join(names)}) -> p {' '.join(names)}", **dict(zip(names[1:], shape[1:])))
            return a

        k.view = view
        k.top, k.top_i = view(136, [TT, 2 * PH, TOPK]), view(140, [TT, 2 * PH, TOPK], U32)
        k.picksT = view(144, [3, T])
        sems = []

        def sem(name):
            sems.append(nc.alloc_semaphore(name=f"{k.phase}_{name}"))
            return sems[-1]

        k.sem = sem
        k.vec = lambda name, n=0: k.vecs[:, VEC_AT[name] + n:VEC_AT[name] + n + 1]
        k.const = lambda name: k.consts[:, CONST_AT[name][0]:sum(CONST_AT[name])]
        for n, phase in enumerate(PHASES):
            if n < upto:
                k.phase = phase.__name__.removeprefix("phase_")
                phase(nc, k, io)
                if phase is phase_merge:
                    nc.clear_and_free_semaphores(sems)
                    nc.all_engine_barrier()
                    sems.clear()
        if dbg:
            dbg(nc, k, io)


ARENA_KB = 194
PHASES = [phase_norm_and_rwkv_in, phase_rwkv_prepare, phase_delta_rule, phase_rwkv_out,
          phase_mla_project, phase_attention, phase_merge,
          phase_route_scores, phase_route_picks, phase_gate_matrix, phase_experts]




def kernel(**inputs):
    import concourse.bacc as bacc
    from concourse.bass_utils import run_bass_kernel_spmd

    nc = bacc.Bacc("TRN2", target_bir_lowering=False, num_devices=1)
    arrays, io = {}, {}
    for name, a in laid_out(inputs).items():
        arrays[f"in_{name}_dram"] = a
        io[name] = nc.dram_tensor(f"in_{name}_dram", a.shape, mybir.dt.from_np(a.dtype), kind="ExternalInput").ap()
    io["outT"] = nc.dram_tensor("out_0_dram", (D, T), F32, kind="ExternalOutput").ap()
    build(nc, io)
    r = run_bass_kernel_spmd(nc, [arrays], core_ids=[0])
    return np.ascontiguousarray(r.results[0]["out_0_dram"].T)[None]
```

```python
from contextlib import ExitStack

import numpy as np
import concourse.bass as bass
from concourse import mybir

F32 = mybir.dt.float32
F16 = mybir.dt.float16
I32 = mybir.dt.int32
U32 = mybir.dt.uint32
ALU = mybir.AluOpType
ACT = mybir.ActivationFunctionType
AX = mybir.AxisListType

P = 128
T = 512
D = 1024
KT = D // P
EPS = 1e-6
RW = 512
RT = RW // P
C = 64
NCH = T // C
NPR = NCH * RT
HALF = [slice(0, 64), slice(64, 128)]
GN_EPS = 64e-5
Q_LORA, KV_LORA, ROPE = 384, 256, 32
HEADS, NOPE, QK = 8, 64, 96
TT = T // P
PH, NK, TOPK = 8, 128, 16
PICKS = PH * TOPK
NE = NK * NK

RW_COLS = [(P * n, P) for n in range(13)] + [(1664, P), (1792, 32)]
Q_COL = 1824
KV_COL = Q_COL + Q_LORA
KPE_COL = KV_COL + KV_LORA
GA_COL = KPE_COL + ROPE
GB_COL = GA_COL + D

VECS = [("norm1_w", P, 8), ("rw_mu", P, 14), ("rw_mu_tail", 32, 1), ("rw_w0", P, 4), ("rw_a0", P, 4),
        ("rw_k_k", P, 4), ("rw_k_a", P, 4), ("rw_r_k", P, 4), ("rw_ln_w", P, 4), ("rw_ln_b", P, 4),
        ("mla_q_norm_w", P, 3), ("mla_kv_norm_w", P, 2), ("qn_w", QK, 1), ("kn_w", QK, 1),
        ("norm2_w", P, 8), ("inv_freq", QK, 1)]
VEC_AT = {name: sum(t for _, _, t in VECS[:n]) for n, (name, _, _) in enumerate(VECS)}
NV = sum(t for _, _, t in VECS)

LEVELS = [1, 2, 4, 8, 16, 32]
CONSTS = [("ones", P), ("head_ones", P), ("ident", P), ("qk_ones", QK), ("rope_swap", QK), ("iota", P),
          ("causal", P), ("chunk_start", T), ("strict", C), ("upto", C), ("fold", C), ("level1_t", C)] + \
         [(f"level{m}", C) for m in LEVELS[1:]]
CONST_AT = {name: (sum(c for _, c in CONSTS[:n]), cols) for n, (name, cols) in enumerate(CONSTS)}
NCONST = sum(c for _, c in CONSTS)


def constant_array():
    a = np.zeros((P, NCONST), np.float32)

    def put(name, m):
        at, cols = CONST_AT[name]
        a[:m.shape[0], at:at + cols] = m

    i, j = np.arange(P)[:, None], np.arange(P)[None, :]
    put("ones", np.ones((P, P)))
    put("head_ones", (i // 64 == j // 64) * 1.0)
    put("ident", (i == j) * 1.0)
    q, r = np.arange(QK)[:, None], np.arange(QK)[None, :]
    put("qk_ones", np.where((q < NOPE) & (r < NOPE), 1 / NOPE, 0) + np.where((q >= NOPE) & (r >= NOPE), 1 / ROPE, 0))
    half = ROPE // 2
    put("rope_swap", np.where((r >= NOPE) & (r < NOPE + half) & (q == r + half), -1.0, 0)
        + np.where((r >= NOPE + half) & (q == r - half), 1.0, 0))
    put("iota", np.broadcast_to(j, (P, P)) * 1.0)
    put("causal", np.where(j <= i, 0.0, -1e30))
    put("chunk_start", np.broadcast_to(np.arange(T)[None] % C != 0, (P, T)) * 1.0)
    s, t = np.arange(P)[:, None] % C, np.arange(C)[None, :]
    put("strict", (s < t) * 1.0)
    put("upto", (s <= t) * 1.0)
    put("fold", (s == t) * 1.0)
    put("level1_t", ((t // 2 == s // 2) & (t % 2 == 1) & (s % 2 == 0)) * 1.0)
    for m in LEVELS[1:]:
        put(f"level{m}", ((t // (2 * m) == s // (2 * m)) & (s // m % 2 == 1) & (t // m % 2 == 0)) * 1.0)
    return a


class Kit:
    pass


def chained(eng, sem):
    n = [0]

    def link(ins):
        n[0] += 1
        ins.then_inc(sem, 1)
        eng.wait_ge(sem, n[0])
    return link


def diagonal(bd, e, other=False):
    return bd[HALF[e], :, HALF[1 - e if other else e]]


def by_chunk(x):
    return x.rearrange("p j (c t) -> p c j t", t=C)


def phase_norm_and_rwkv_in(nc, k, io):
    x = k.view(64, [KT, T])
    sq = k.view(80, [KT, T])
    ring = [k.view(96 + 4 * s, [KT, P]) for s in range(4)]
    raw = [k.view(112 + 3 * s, [T + 1]) for s in range(2)]
    diff = k.view(118, [T])
    rt, rstd = k.view(120, [T]), k.view(122, [T])
    xn, mix = k.view(0, [KT, T]), k.view(32, [15, T])
    w_in = io["w_in"].rearrange("(k p) n -> p k n", p=P)
    NB = 3
    with nc.Block() as block:
        x_ld = [k.sem(f"x_ld{n}") for n in range(KT)]
        small_ld, sq_ready, ss_done, rt_ready, rstd_ready = map(k.sem, ("small_ld", "sq_ready", "ss_done", "rt_ready", "rstd_ready"))
        w_ld = [k.sem(f"w_in_ld{s}") for s in range(4)]
        xn_ready, proj_done, raw_ready, pad_ready, diff_ready, mix_done = map(
            k.sem, ("xn_ready", "proj_done", "raw_ready", "pad_ready", "diff_ready", "mix_done"))

        @block.sync
        def _(sp):
            for n in range(KT):
                sp.dma_start(x[:, n], io["xT"][n * P:(n + 1) * P, :]).then_inc(x_ld[n], 16)
                if n == 0:
                    sp.dma_start(k.consts[:, :], io["consts"]).then_inc(small_ld, 16)
                    sp.dma_start(k.vecs[:, :], io["vecs"]).then_inc(small_ld, 16)
            for n, (col, m) in enumerate(RW_COLS):
                if n >= 4:
                    sp.wait_ge(proj_done, n - 3)
                sp.dma_start(ring[n % 4][:, :, 0:m], w_in[:, :, col:col + m]).then_inc(w_ld[n % 4], 16)

        @block.scalar
        def _(act):
            for n in range(KT):
                act.wait_ge(x_ld[n], 16)
                act.activation(sq[:, n], x[:, n], ACT.Square).then_inc(sq_ready, 1)
            act.wait_ge(ss_done, 1)
            act.wait_ge(pad_ready, 3)
            act.activation(rt, k.ps[:, 0], ACT.Sqrt, scale=1.0 / D, bias=k.eps[:, 0:1]).then_inc(rt_ready, 1)
            for n, (_, m) in enumerate(RW_COLS):
                act.wait_ge(proj_done, n + 1)
                act.wait_ge(pad_ready, 3)
                if n >= 2:
                    act.wait_ge(mix_done, n - 1)
                act.activation(raw[n % 2][0:m, 1:T + 1], k.ps[0:m, 1 + n % NB], ACT.Copy).then_inc(raw_ready, 1)

        @block.vector
        def _(dve):
            dve.memset(raw[0][:, 0:1], 0.0).then_inc(pad_ready, 1)
            dve.memset(raw[1][:, 0:1], 0.0).then_inc(pad_ready, 1)
            dve.memset(k.eps[:, 0:1], EPS).then_inc(pad_ready, 1)
            dve.memset(k.eps[:, 1:2], GN_EPS)
            dve.wait_ge(small_ld, 32)
            dve.wait_ge(rt_ready, 1)
            dve.reciprocal(rstd, rt).then_inc(rstd_ready, 1)
            dve.wait_ge(rstd_ready, 1)
            for n in range(KT):
                dve.scalar_tensor_tensor(xn[:, n], x[:, n], k.vec("norm1_w", n), rstd,
                                         ALU.mult, ALU.mult).then_inc(xn_ready, 1)
            for n, (_, m) in enumerate(RW_COLS):
                dve.wait_ge(raw_ready, n + 1)
                if n:
                    dve.wait_ge(mix_done, n)
                prev, cur = raw[n % 2][0:m, 0:T], raw[n % 2][0:m, 1:T + 1]
                dve.tensor_tensor(diff[0:m], prev, cur, ALU.subtract).then_inc(diff_ready, 1)
                dve.wait_ge(diff_ready, n + 1)
                dve.scalar_tensor_tensor(mix[0:m, n], diff[0:m], k.vec("rw_mu", n)[0:m], cur,
                                         ALU.mult, ALU.add).then_inc(mix_done, 1)

        @block.tensor
        def _(pe):
            pe.wait_ge(small_ld, 32)
            for n in range(KT):
                pe.wait_ge(sq_ready, n + 1)
                last = pe.matmul(k.ps[:, 0], k.const("ones"), sq[:, n], start=n == 0, stop=n == KT - 1)
            last.then_inc(ss_done, 1)
            for n, (_, m) in enumerate(RW_COLS):
                pe.wait_ge(w_ld[n % 4], 16 * (n // 4 + 1))
                if n >= NB:
                    pe.wait_ge(raw_ready, n - NB + 1)
                for f in range(KT):
                    if n == 0:
                        pe.wait_ge(xn_ready, f + 1)
                    last = pe.matmul(k.ps[0:m, 1 + n % NB], ring[n % 4][:, f, 0:m], xn[:, f],
                                     start=f == 0, stop=f == KT - 1)
                last.then_inc(proj_done, 1)


def phase_rwkv_prepare(nc, k, io):
    mix = k.view(32, [15, T])
    r, key, v = mix[:, 0:4], mix[:, 4:8], mix[:, 8:12]
    g, bonus = k.view(16, [RT, T]), k.view(24, [RT, T])
    at, rt_ = k.view(32, [RT, T]), k.view(40, [RT, T])
    at_bd, bt_bd, kt_bd = (k.view(64 + 16 * n, [NPR, P]) for n in range(3))
    lw, L, ex, ea, a, kk, kp, inv_n = (k.view(112 + 8 * n, [RT, T]) for n in range(8))
    w2a2 = k.view(176, [RW])
    g2a, g2b = k.view(178, [RW]), k.view(180, [RW])
    tw, sg = k.view(182, [T]), k.view(184, [2, T])
    b = inv_n
    ps = k.ps
    with nc.Block() as block:
        at_ready = k.sem("at_ready")
        lora_ld, tw_ready, sg_ready, z_done, za_done, g_done, kk2_done, rk_done = map(
            k.sem, ("lora_ld", "tw_ready", "sg_ready", "z_done", "za_done", "g_done", "kk2_done", "rk_done"))
        sw_ready, a_ready, g_ready, kk2_ready, norm_ready = map(
            k.sem, ("sw_ready", "a_ready", "g_ready", "kk2_ready", "norm_ready"))
        ss_ready, ex_in, L_ready, rk_ready, dve_chain, ea_ready, en_ready, ex_ready = map(
            k.sem, ("ss_ready", "ex_in", "L_ready", "rk_ready", "dve_chain2", "ea_ready", "en_ready", "ex_ready"))

        @block.sync
        def _(sp):
            sp.dma_start(w2a2[0:64], io["rw_w2"]).then_inc(lora_ld, 16)
            sp.dma_start(w2a2[64:128], io["rw_a2"]).then_inc(lora_ld, 16)
            sp.dma_start(g2a, io["rw_g2"][0:P, :]).then_inc(lora_ld, 16)
            sp.dma_start(g2b[0:32], io["rw_g2"][P:160, :]).then_inc(lora_ld, 16)

        @block.scalar
        def _(act):
            act.activation(tw[0:64], mix[0:64, 12], ACT.Tanh).then_inc(tw_ready, 1)
            act.activation(sg[:, 0], mix[:, 13], ACT.Sigmoid).then_inc(sg_ready, 1)
            act.activation(sg[0:32, 1], mix[0:32, 14], ACT.Sigmoid).then_inc(sg_ready, 1)
            for j in range(RT):
                act.wait_ge(z_done, j + 1)
                act.activation(lw[:, j], ps[:, j], ACT.Sigmoid, bias=k.vec("rw_w0", j)).then_inc(sw_ready, 1)
            for j in range(RT):
                act.wait_ge(za_done, j + 1)
                act.activation(a[:, j], ps[:, 4 + j], ACT.Sigmoid, bias=k.vec("rw_a0", j)).then_inc(a_ready, 1)
            for j in range(RT):
                act.wait_ge(g_done, j + 1)
                act.activation(g[:, j], ps[:, j], ACT.Copy).then_inc(g_ready, 1)
            for j in range(RT):
                act.activation(kp[:, j], key[:, j], ACT.Square, scale=k.vec("rw_k_k", j)).then_inc(kk2_ready, 1)
            act.wait_ge(ss_ready, 1)
            act.activation(inv_n[:, :], inv_n[:, :], ACT.Sqrt).then_inc(norm_ready, 1)
            act.wait_ge(L_ready, RT)
            act.activation(ea[:, :], L[:, :], ACT.Exp).then_inc(ea_ready, 1)
            act.wait_ge(ex_in, 1)
            act.activation(ex[:, :], ex[:, :], ACT.Exp).then_inc(ex_ready, 1)
            act.wait_ge(ea_ready, 1)
            act.activation(L[:, :], L[:, :], ACT.Exp, scale=-1.0).then_inc(en_ready, 1)
            act.wait_ge(at_ready, 1)
            for e in range(2):
                act.activation(diagonal(at_bd, e), by_chunk(at[HALF[e]]), ACT.Copy)

        @block.gpsimd
        def _(pool):
            for bd in (at_bd, bt_bd, kt_bd):
                for e in range(2):
                    pool.memset(diagonal(bd, e, other=True), 0.0)

        @block.vector
        def _(dve):
            link = chained(dve, dve_chain)
            for j in range(RT):
                dve.wait_ge(sw_ready, j + 1)
                link(dve.tensor_scalar(lw[:, j], lw[:, j], -float(np.exp(-0.5)), None, ALU.mult))
                dve.tensor_tensor_scan(L[:, j], k.const("chunk_start"), lw[:, j], 0.0,
                                       ALU.mult, ALU.add).then_inc(L_ready, 1)
            dve.wait_ge(L_ready, RT)
            dve.tensor_tensor(ex[:, :], L[:, :], lw[:, :], ALU.subtract).then_inc(ex_in, 1)
            dve.wait_ge(kk2_done, RT)
            dve.tensor_scalar(inv_n[:, :], ps[:, 4:8], 1e-24, None, ALU.max).then_inc(ss_ready, 1)
            dve.wait_ge(norm_ready, 1)
            link(dve.reciprocal(inv_n[:, :], inv_n[:, :]))
            for j in range(RT):
                last = dve.scalar_tensor_tensor(kk[:, j], key[:, j], k.vec("rw_k_k", j), inv_n[:, j], ALU.mult, ALU.mult)
            link(last)
            dve.wait_ge(a_ready, RT)
            link(dve.tensor_tensor(b[:, :], kk[:, :], a[:, :], ALU.mult))
            for j in range(RT):
                last = dve.tensor_scalar(a[:, j], a[:, j], 1.0, k.vec("rw_k_a", j), ALU.subtract, ALU.mult)
            link(last)
            link(dve.scalar_tensor_tensor(kp[:, :], a[:, :], 1.0, key[:, :], ALU.add, ALU.mult))
            for j in range(RT):
                dve.scalar_tensor_tensor(a[:, j], r[:, j], k.vec("rw_r_k", j), kp[:, j],
                                         ALU.mult, ALU.mult).then_inc(rk_ready, 1)
            dve.wait_ge(ea_ready, 1)
            link(dve.tensor_tensor(rt_[:, :], r[:, :], ea[:, :], ALU.mult))
            dve.wait_ge(rk_ready, RT)
            dve.wait_ge(ex_ready, 1)
            dve.scalar_tensor_tensor(at[:, :], kk[:, :], -1.0, ex[:, :], ALU.mult, ALU.mult).then_inc(at_ready, 1)
            dve.wait_ge(en_ready, 1)
            for e in range(2):
                dve.tensor_tensor(diagonal(bt_bd, e), by_chunk(b[HALF[e]]), by_chunk(L[HALF[e]]), ALU.mult)
                dve.tensor_tensor(diagonal(kt_bd, e), by_chunk(kp[HALF[e]]), by_chunk(L[HALF[e]]), ALU.mult)
            dve.tensor_copy(k.chunk_decay[:, :, :], ea.rearrange("p j (c t) -> p j c t", t=C)[:, :, :, C - 1])
            dve.wait_ge(rk_done, RT)
            dve.tensor_tensor(bonus[:, :], ps[:, 0:4], v[:, :], ALU.mult)

        @block.tensor
        def _(pe):
            pe.wait_ge(lora_ld, 64)
            pe.wait_ge(tw_ready, 1)
            for j in range(RT):
                pe.matmul(ps[:, j], w2a2[0:64, j * P:(j + 1) * P], tw[0:64], start=True, stop=True).then_inc(z_done, 1)
            for j in range(RT):
                pe.matmul(ps[:, 4 + j], w2a2[64:128, j * P:(j + 1) * P], mix[64:128, 12],
                          start=True, stop=True).then_inc(za_done, 1)
            pe.wait_ge(sg_ready, 2)
            for j in range(RT):
                pe.wait_ge(sw_ready, j + 1)
                pe.matmul(ps[:, j], g2a[:, j * P:(j + 1) * P], sg[:, 0], start=True, stop=False)
                pe.matmul(ps[:, j], g2b[0:32, j * P:(j + 1) * P], sg[0:32, 1], start=False, stop=True).then_inc(g_done, 1)
            for j in range(RT):
                pe.wait_ge(kk2_ready, j + 1)
                pe.wait_ge(a_ready, j + 1)
                pe.matmul(ps[:, 4 + j], k.const("head_ones"), kp[:, j], start=True, stop=True).then_inc(kk2_done, 1)
            for j in range(RT):
                pe.wait_ge(rk_ready, j + 1)
                pe.wait_ge(g_ready, j + 1)
                pe.matmul(ps[:, j], k.const("head_ones"), a[:, j], start=True, stop=True).then_inc(rk_done, 1)



def phase_delta_rule(nc, k, io):
    rt_, v = k.view(40, [RT, T]), k.view(48, [RT, T])
    ar = k.view(32, [2, RT, T])
    RV = k.view(56, [NPR, C])
    at_bd, bt_bd, kt_bd, v_bd, AabT_bd, Bt_bd = (k.view(64 + 16 * n, [NPR, P]) for n in range(6))
    ArbT, y, KV = k.view(160, [NPR, C]), k.view(168, [RT, T]), k.view(176, [NPR, C])
    GR = 4
    GP = NPR // GR
    AakT_bd, Kt_bd, Vt_bd = (k.view(184 + 4 * n, [GP, P]) for n in range(3))
    Vt, ArkT = k.view(48, [GP, C]), k.view(50, [GP, C])
    Tm, TmT, X, X_bd, TmT_bd = k.view(80, [NPR, C]), k.view(88, [NPR, C]), k.view(32, [NPR, C]), kt_bd, v_bd
    ST, W, R, SA, tmp = (k.view(at_kb, [RT, C]) for at_kb in (48, 49, 50, 51, 184))
    ST_bd, SA_bd = k.view(52, [RT, P]), k.view(54, [RT, P])
    ps = k.ps
    fold = k.const("fold")
    fold_wide = k.consts[:, CONST_AT["fold"][0]:CONST_AT["fold"][0] + 2 * C]

    def mask(name, rows, n):
        m = k.const(name)[rows]
        return m.unsqueeze(1).to_broadcast([m.shape[0], n, C])

    def group(x, g):
        return x[:, g * GP:(g + 1) * GP]

    def bank(n, rows=slice(0, P), cols=GP * C):
        return ps[rows, n, 0:cols].rearrange("p (n t) -> p n t", t=C)

    def wide_product(pe, out, stationary, moving, n, q, last=RT - 1, stop=True):
        if q == last:
            return pe.matmul(ps[:, out, q * C:(q + 1) * C], stationary, moving[:, n], start=True, stop=stop)
        return pe.matmul(ps[:, out, q * C:(q + 2) * C], stationary, moving[:, n:n + 2].rearrange("p n t -> p (n t)"),
                         start=True, stop=stop)

    def group_products(pe, out, stationary, moving, at=0):
        for q in range(GP):
            last = wide_product(pe, out, stationary[:, at + q], moving, at + q, q, GP - 1)
        return last

    KINDS = [("k0", "dve"), ("V", "act"), ("k1", "dve"), ("K", "act"), ("b0", "dve"), ("B", "act"),
             ("b1", "dve"), ("RV", "dve"), ("KV", "act"), ("YV", "act")]
    units = [(name, by, g) for g in range(GR) for name, by in KINDS]

    def done(by, name, g):
        return sum(b == by for _, b, _ in units[:units.index((name, by, g)) + 1])

    LV = len(LEVELS) - 1
    NX = LV * GR
    with nc.Block() as block:
        zero_ready, zero2_ready, v_ready, product_done, dve_out, act_out = map(
            k.sem, ("zero_ready", "zero2_ready", "v_ready", "product_done", "dve_out", "act_out"))
        first_in, first_ready, first_bd, first_done, first_out = map(k.sem, ("first_in", "first_ready", "first_bd", "first_done", "first_out"))
        x_done, x_out, xb_out, t_done, t_out, tt_done, tt_out, tb_out = map(
            k.sem, ("x_done", "x_out", "xb_out", "t_done", "t_out", "tt_done", "tt_out", "tb_out"))
        r_done, r_out, sa_done, sa_out, sab_out, s_done, s_in, s_out, stb_out, w_out, y_done, y_out = map(
            k.sem, ("r_done", "r_out", "sa_done", "sa_out", "sab_out", "s_done", "s_in", "s_out", "stb_out", "w_out", "y_done", "y_out"))

        @block.gpsimd
        def _(pool):
            for bd in (v_bd, Bt_bd, AabT_bd):
                for e in range(2):
                    last = pool.memset(diagonal(bd, e, other=True), 0.0)
                last.then_inc(zero_ready, 1)
            pool.wait_ge(v_ready, 1)
            for bd in (ST_bd, SA_bd):
                for e in range(2):
                    last = pool.memset(diagonal(bd, e, other=True), 0.0)
            last.then_inc(zero_ready, 1)

        @block.tensor
        def _(pe):
            transposed = {"V": v_bd, "K": kt_bd, "B": bt_bd}
            inner = {"RV": (AakT_bd, Vt), "KV": (Kt_bd, Vt), "YV": (Vt_bd, ArkT)}
            for u, (name, _, g) in enumerate(units):
                if u >= 8:
                    before = units[u - 8]
                    pe.wait_ge(dve_out if before[1] == "dve" else act_out, done(before[1], before[0], before[2]))
                if name == "V" and g == 0:
                    pe.wait_ge(v_ready, 1)
                    pe.wait_ge(zero_ready, 1)
                if name == "RV":
                    pe.wait_ge(dve_out, done("dve", "k1", g))
                    pe.wait_ge(act_out, done("act", "V", g))
                    pe.wait_ge(zero2_ready, 1)
                if name == "KV":
                    pe.wait_ge(act_out, done("act", "K", g))
                if name == "YV":
                    pe.wait_ge(dve_out, done("dve", "k1", g))
                if name in inner:
                    last = group_products(pe, u % 8, *inner[name])
                for q in range(GP) if name in transposed else ():
                    n = C if q == GP - 1 else 2 * C
                    last = pe.matmul(ps[:, u % 8, q * C:q * C + n], transposed[name][:, g * GP + q], fold_wide[:, 0:n],
                                     start=True, stop=True)
                for q in range(GP // 2) if name[0] in "kb" else ():
                    n = g * GP + int(name[1]) * GP // 2 + q
                    c, j = divmod(n, RT)
                    last = pe.matmul(ps[:, u % 8, q * 2 * C:(q + 1) * 2 * C], (kt_bd if name[0] == "k" else bt_bd)[:, n],
                                     ar[:, :, j, c * C:(c + 1) * C], start=True, stop=True)
                last.then_inc(product_done, 1)
            pe.wait_ge(act_out, done("act", "YV", GR - 1))
            pe.wait_ge(dve_out, done("dve", "RV", GR - 1))
            for g in range(GR):
                pe.wait_ge(first_bd, g + 1)
                for q in range(GP):
                    last = pe.matmul(bank(g)[:, q], TmT_bd[:, g * GP + q], fold, start=True, stop=True)
                last.then_inc(first_done, 1)
            pe.wait_ge(zero_ready, 4)
            for n in range(NX + 2):
                if n < NX:
                    g = n % GR
                    if n < GR:
                        pe.wait_ge(first_out, GR)
                    else:
                        pe.wait_ge(t_out, n - GR + 1)
                    if n >= 2:
                        pe.wait_ge(x_out, n - 1)
                    group_products(pe, n % 2, AabT_bd, Tm, g * GP).then_inc(x_done, 1)
                m = n - 1
                if 0 <= m < NX - GR:
                    g = m % GR
                    pe.wait_ge(x_out, m + 1)
                    if m >= GR:
                        pe.wait_ge(tb_out, m - GR + 1)
                    if m >= 2:
                        pe.wait_ge(t_out, m - 1)
                    group_products(pe, 2 + m % 2, TmT_bd, X, g * GP).then_inc(t_done, 1)
                m = n - 2
                if m >= 0:
                    g = m % GR
                    pe.wait_ge(xb_out, m + 1)
                    if m >= GR:
                        pe.wait_ge(tt_out, m - GR + 1)
                    if m >= 2:
                        pe.wait_ge(tt_out, m - 1)
                    group_products(pe, 4 + m % 2, X_bd, TmT, g * GP).then_inc(tt_done, 1)
            pe.wait_ge(tb_out, NX)
            for c in range(NCH):
                if c:
                    pe.wait_ge(s_out, c)
                    for j in range(RT):
                        last = wide_product(pe, 0, at_bd[:, c * RT + j], ST, j, j)
                    last.then_inc(r_done, 1)
                    pe.wait_ge(r_out, c)
                for j in range(RT):
                    last = wide_product(pe, 1, TmT_bd[:, c * RT + j], R if c else RV, j, j)
                last.then_inc(sa_done, 1)
                pe.wait_ge(sa_out, c + 1)
                if c < NCH - 1:
                    for j in range(RT):
                        last = wide_product(pe, 2, Bt_bd[:, c * RT + j], SA, j, j)
                    last.then_inc(s_done, 1)
                pe.wait_ge(sab_out, c + 1)
                if c:
                    pe.wait_ge(stb_out, c)
                if c >= 2:
                    pe.wait_ge(y_out, c - 1)
                for j in range(RT):
                    last = wide_product(pe, 6 + c % 2, SA_bd[:, j], ArbT, c * RT + j, j, stop=not c)
                    if c:
                        last = pe.matmul(bank(6 + c % 2)[:, j], ST_bd[:, j], rt_[:, j, c * C:(c + 1) * C], start=False, stop=True)
                last.then_inc(y_done, 1)

        @block.scalar
        def _(act):
            for e in range(2):
                last = act.activation(diagonal(v_bd, e), by_chunk(v[HALF[e]]), ACT.Copy)
            last.then_inc(v_ready, 1)
            act.wait_ge(v_ready, 1)
            act.wait_ge(zero2_ready, 1)
            for u, (name, by, g) in enumerate(units):
                if by != "act":
                    continue
                act.wait_ge(product_done, u + 1)
                if name == "V":
                    if g:
                        act.wait_ge(product_done, units.index(("YV", "act", g - 1)) + 1)
                    act.activation(Vt, bank(u % 8), ACT.Copy)
                if name in ("V", "K", "B"):
                    dst = {"V": Vt_bd, "K": Kt_bd, "B": group(Bt_bd, g)}[name]
                    for e in range(2):
                        last = act.activation(diagonal(dst, e), bank(u % 8, HALF[e]), ACT.Copy)
                elif name == "KV":
                    last = act.activation(group(KV, g), bank(u % 8), ACT.Copy)
                else:
                    per = GP // RT
                    last = act.activation(by_chunk(y)[:, g * per:(g + 1) * per],
                                          ps[:, u % 8].rearrange("p (c j t) -> p c j t", j=RT, t=C), ACT.Copy)
                last.then_inc(act_out, 1)
            for g in range(GR):
                act.wait_ge(first_ready, g + 1)
                for e in range(2):
                    last = act.activation(diagonal(group(TmT_bd, g), e), group(TmT, g)[HALF[e]], ACT.Copy)
                last.then_inc(first_bd, 1)
            for g in range(GR):
                act.wait_ge(first_done, g + 1)
                act.activation(group(Tm, g), bank(g), ACT.Copy).then_inc(first_out, 1)
            for n in range(NX + 2):
                if n < NX:
                    act.wait_ge(x_out, n + 1)
                    if n >= GR:
                        act.wait_ge(tt_done, n - GR + 1)
                    for e in range(2):
                        last = act.activation(diagonal(group(X_bd, n % GR), e), group(X, n % GR)[HALF[e]], ACT.Copy)
                    last.then_inc(xb_out, 1)
                m = n - 2
                if m >= 0:
                    act.wait_ge(tt_out, m + 1)
                    for e in range(2):
                        last = act.activation(diagonal(group(TmT_bd, m % GR), e), group(TmT, m % GR)[HALF[e]], ACT.Copy)
                    last.then_inc(tb_out, 1)
            for c in range(NCH):
                act.wait_ge(sa_out, c + 1)
                if c:
                    act.wait_ge(y_done, c)
                for e in range(2):
                    last = act.activation(diagonal(SA_bd, e), SA[HALF[e]], ACT.Copy)
                last.then_inc(sab_out, 1)
                if c < NCH - 1:
                    act.wait_ge(s_out, c + 1)
                    act.wait_ge(y_done, c + 1)
                    for e in range(2):
                        last = act.activation(diagonal(ST_bd, e), ST[HALF[e]], ACT.Copy)
                    last.then_inc(stb_out, 1)

        @block.vector
        def _(dve):
            for bd in (AakT_bd, Kt_bd, Vt_bd):
                for e in range(2):
                    last = dve.memset(diagonal(bd, e, other=True), 0.0)
            last.then_inc(zero2_ready, 1)
            dve.wait_ge(v_ready, 1)
            for u, (name, by, g) in enumerate(units):
                if by != "dve":
                    continue
                dve.wait_ge(product_done, u + 1)
                if name == "k0" and g:
                    dve.wait_ge(product_done, units.index(("YV", "act", g - 1)) + 1)
                if name[0] in "kb":
                    half = slice(int(name[1]) * GP // 2, (int(name[1]) + 1) * GP // 2)
                    A_bd, A_r = (AakT_bd, ArkT) if name[0] == "k" else (group(AabT_bd, g), group(ArbT, g))
                    both = ps[:, u % 8].rearrange("p (n x t) -> p n x t", x=2, t=C)
                    for e in range(2):
                        dve.tensor_tensor(diagonal(A_bd[:, half], e), both[HALF[e], :, 0], mask("strict", HALF[e], GP // 2), ALU.mult)
                    last = dve.tensor_tensor(A_r[:, half], both[:, :, 1], mask("upto", slice(0, P), GP // 2), ALU.mult)
                else:
                    last = dve.tensor_copy(group(RV, g), bank(u % 8))
                last.then_inc(dve_out, 1)
            dve.wait_ge(product_done, len(units))
            dve.wait_ge(dve_out, done("dve", "RV", GR - 1))
            for g in range(GR):
                for e in range(2):
                    last = dve.tensor_tensor(group(TmT, g)[HALF[e]], diagonal(group(AabT_bd, g), e), mask("level1_t", HALF[e], GP), ALU.mult)
                last.then_inc(first_in, 1)
            for g in range(GR):
                dve.wait_ge(first_in, g + 1)
                dve.tensor_tensor(group(TmT, g), group(TmT, g), mask("fold", slice(0, P), GP), ALU.add).then_inc(first_ready, 1)
            for n in range(NX + 2):
                if n < NX:
                    dve.wait_ge(x_done, n + 1)
                    if n >= GR:
                        dve.wait_ge(t_done, min(n - GR + 1, NX - GR))
                        dve.wait_ge(xb_out, n - GR + 1)
                    dve.tensor_tensor(group(X, n % GR), bank(n % 2), mask(f"level{LEVELS[n // GR + 1]}", slice(0, P), GP),
                                      ALU.mult).then_inc(x_out, 1)
                m = n - 1
                if 0 <= m < NX - GR:
                    dve.wait_ge(t_done, m + 1)
                    if m >= GR:
                        dve.wait_ge(t_out, m - GR + 1)
                    dve.tensor_tensor(group(Tm, m % GR), group(Tm, m % GR), bank(2 + m % 2), ALU.add).then_inc(t_out, 1)
                m = n - 2
                if m >= 0:
                    dve.wait_ge(tt_done, m + 1)
                    if m >= GR:
                        dve.wait_ge(tb_out, m - GR + 1)
                        dve.wait_ge(tt_out, m - GR + 1)
                    else:
                        dve.wait_ge(first_ready, m + 1)
                    dve.tensor_tensor(group(TmT, m % GR), group(TmT, m % GR), bank(4 + m % 2), ALU.add).then_inc(tt_out, 1)
            for c in range(NCH):
                now = slice(c * RT, (c + 1) * RT)
                if c:
                    dve.wait_ge(r_done, c)
                    dve.tensor_tensor(R, bank(0, cols=RT * C), RV[:, now], ALU.add).then_inc(r_out, 1)
                dve.wait_ge(sa_done, c + 1)
                if c:
                    dve.wait_ge(s_done, c)
                    dve.wait_ge(sab_out, c)
                dve.tensor_copy(SA, bank(1, cols=RT * C)).then_inc(sa_out, 1)
                if c < NCH - 1:
                    dve.wait_ge(s_done, c + 1)
                    if c:
                        dve.wait_ge(w_out, c)
                        dve.wait_ge(s_out, c)
                    dve.tensor_tensor(tmp, bank(2, cols=RT * C), W if c else KV[:, now], ALU.add).then_inc(s_in, 1)
                    dve.wait_ge(s_in, c + 1)
                    if c:
                        dve.wait_ge(stb_out, c)
                    dve.tensor_tensor(ST, tmp, k.chunk_decay[:, :, c:c + 1].to_broadcast([P, RT, C]), ALU.mult).then_inc(s_out, 1)
                    dve.wait_ge(s_out, c + 1)
                    dve.tensor_tensor(W, ST, KV[:, (c + 1) * RT:(c + 2) * RT], ALU.add).then_inc(w_out, 1)
                dve.wait_ge(y_done, c + 1)
                own = y[:, :, c * C:(c + 1) * C]
                dve.tensor_tensor(own, own, bank(6 + c % 2, cols=RT * C), ALU.add).then_inc(y_out, 1)


def phase_rwkv_out(nc, k, io):
    g, bonus, y = k.view(16, [RT, T]), k.view(24, [RT, T]), k.view(168, [RT, T])
    d, sq, s, yg = k.view(112, [RT, T]), k.view(120, [RT, T]), k.view(128, [RT, T]), g
    ps = k.ps
    with nc.Block() as block:
        mean_done, dev_ready, dev2_ready, var_done, sd_ready, gn_chain = map(
            k.sem, ("mean_done", "dev_ready", "dev2_ready", "var_done", "sd_ready", "gn_chain"))

        @block.tensor
        def _(pe):
            for j in range(RT):
                pe.matmul(ps[:, j], k.const("head_ones"), y[:, j], start=True, stop=True).then_inc(mean_done, 1)
            for j in range(RT):
                pe.wait_ge(dev2_ready, j + 1)
                pe.matmul(ps[:, 4 + j], k.const("head_ones"), sq[:, j], start=True, stop=True).then_inc(var_done, 1)

        @block.scalar
        def _(act):
            for j in range(RT):
                act.wait_ge(dev_ready, j + 1)
                act.activation(sq[:, j], d[:, j], ACT.Square).then_inc(dev2_ready, 1)
            for j in range(RT):
                act.wait_ge(var_done, j + 1)
                act.activation(s[:, j], ps[:, 4 + j], ACT.Sqrt, scale=1.0 / 64, bias=k.eps[:, 1:2]).then_inc(sd_ready, 1)

        @block.vector
        def _(dve):
            link = chained(dve, gn_chain)
            for j in range(RT):
                dve.wait_ge(mean_done, j + 1)
                dve.scalar_tensor_tensor(d[:, j], ps[:, j], -1.0 / 64, y[:, j], ALU.mult, ALU.add).then_inc(dev_ready, 1)
            dve.wait_ge(sd_ready, RT)
            dve.wait_ge(dev_ready, RT)
            link(dve.reciprocal(s[:, :], s[:, :]))
            link(dve.tensor_tensor(d[:, :], d[:, :], s[:, :], ALU.mult))
            for j in range(RT):
                last = dve.tensor_scalar(d[:, j], d[:, j], k.vec("rw_ln_w", j), k.vec("rw_ln_b", j), ALU.mult, ALU.add)
            link(last)
            link(dve.tensor_tensor(d[:, :], d[:, :], bonus[:, :], ALU.add))
            link(dve.tensor_tensor(yg[:, :], d[:, :], g[:, :], ALU.mult))


def phase_mla_project(nc, k, io):
    xn = k.view(0, [KT, T])
    ring = [k.view(32 + 4 * s, [KT, P]) for s in range(4)]
    down = k.view(48, [5, T])
    sq = k.view(58, [5, T])
    rstd = k.view(68, [2, T])
    w_uq, w_ukv = k.view(72, [3, HEADS * QK]), k.view(81, [2, HEADS * 2 * NOPE])
    Q, K, V = k.view(90, [HEADS, T]), k.view(106, [HEADS, T]), k.view(122, [TT, HEADS * NOPE])
    cos, sin = k.view(130, [T]), k.view(132, [T])
    turned = k.view(134, [T])
    hsq, hsd = k.view(136, [2, T]), k.view(140, [2, T])
    pos, ang, turns, red = k.view(144, [T], I32), k.view(146, [T]), k.view(148, [T]), k.view(150, [T])
    w_in = io["w_in"].rearrange("(k p) n -> p k n", p=P)
    cols = [(Q_COL + n * P, P) for n in range(5)] + [(KPE_COL, ROPE)]
    rope = slice(NOPE, QK)
    items = [("q", h) for h in range(HEADS)] + [("k", h) for h in range(HEADS)]
    rows = [QK if kind == "q" or h == 0 else NOPE for kind, h in items]
    roped = [i for i in range(16) if rows[i] == QK]
    ps = k.ps
    TWO_PI = 2 * np.pi
    C1 = 6.28125
    C2 = float(np.float32(np.round((TWO_PI - C1) * 2 ** 20) / 2 ** 20))
    C3 = float(TWO_PI - C1 - C2)
    MAGIC = 1.5 * 2 ** 23
    with nc.Block() as block:
        w_ld = [k.sem(f"mla_w_ld{s}") for s in range(6)]
        up_ld, pos_ld, down_done, down_ready, dsq_ready, dss_done, dsd_ready, down_normed = map(
            k.sem, ("up_ld", "pos_ld", "down_done", "down_ready", "dsq_ready", "dss_done", "dsd_ready", "down_normed"))
        ang_ready, sin_ready, cos_in, head_done, head_ready, hsq_ready, hss_done, hsd_ready, head_normed = map(
            k.sem, ("ang_ready", "sin_ready", "cos_in", "head_done", "head_ready", "hsq_ready", "hss_done", "hsd_ready", "head_normed"))
        swap_done, roped_ready, mla_chain, v_done, v_ready, kpe_copied = map(
            k.sem, ("swap_done", "roped_ready", "mla_chain", "v_done", "v_ready", "kpe_copied"))

        @block.sync
        def _(sp):
            sp.dma_start(pos[0:QK], io["positions"].to_broadcast([QK, T])).then_inc(pos_ld, 16)
            for n, (col, m) in enumerate(cols):
                if n >= 4:
                    sp.wait_ge(down_done, n - 3)
                sp.dma_start(ring[n % 4][:, :, 0:m], w_in[:, :, col:col + m]).then_inc(w_ld[n], 16)
                if n == 3:
                    sp.dma_start(w_uq, io["mla_w_uq"].rearrange("(k p) n -> p k n", p=P)).then_inc(up_ld, 16)
                    sp.dma_start(w_ukv, io["mla_w_ukv"].rearrange("(k p) n -> p k n", p=P)).then_inc(up_ld, 16)

        @block.tensor
        def _(pe):
            for n in range(5):
                pe.wait_ge(w_ld[n], 16)
                for f in range(KT):
                    last = pe.matmul(ps[:, n], ring[n % 4][:, f], xn[:, f], start=f == 0, stop=f == KT - 1)
                last.then_inc(down_done, 1)
            for n in range(5):
                pe.wait_ge(dsq_ready, n + 1)
                last = pe.matmul(ps[:, 5 + n // 3], k.const("ones"), sq[:, n], start=n in (0, 3), stop=n in (2, 4))
                if n in (2, 4):
                    last.then_inc(dss_done, 1)
            pe.wait_ge(w_ld[5], 16)
            pe.wait_ge(up_ld, 32)

            def main(i):
                kind, h = items[i]
                if i == 0:
                    pe.wait_ge(down_normed, 3)
                    pe.wait_ge(down_ready, 5)
                if i == HEADS:
                    pe.wait_ge(down_normed, 5)
                if i >= 2:
                    pe.wait_ge(head_ready, i - 1)
                out = ps[:, i % 2]
                if kind == "q":
                    for f in range(3):
                        last = pe.matmul(out[0:QK], w_uq[:, f, h * QK:(h + 1) * QK], down[:, f], start=f == 0, stop=f == 2)
                else:
                    if h == 0:
                        for f in range(KT):
                            pe.matmul(out[rope], ring[1][:, f, 0:ROPE], xn[:, f], start=f == 0, stop=f == KT - 1)
                    for f in range(2):
                        last = pe.matmul(out[0:NOPE], w_ukv[:, f, h * P:h * P + NOPE], down[:, 3 + f], start=f == 0, stop=f == 1)
                last.then_inc(head_done, 1)

            def squares(i):
                pe.wait_ge(hsq_ready, i + 1)
                if i >= 2:
                    pe.wait_ge(hsd_ready, i - 1)
                m = rows[i]
                pe.matmul(ps[0:m, 2 + i % 2], k.const("qk_ones")[0:m, 0:m], hsq[0:m, i % 2], start=True, stop=True).then_inc(hss_done, 1)

            def swap(i):
                kind, h = items[i]
                n = roped.index(i)
                pe.wait_ge(head_normed, i + 1)
                if n >= 2:
                    pe.wait_ge(roped_ready, n - 1)
                pe.matmul(ps[0:QK, 4 + n % 2], k.const("rope_swap")[0:QK], (Q if kind == "q" else K)[0:QK, h],
                          start=True, stop=True).then_inc(swap_done, 1)

            pe.wait_ge(dsd_ready, 2)
            for i in range(18):
                if i < 16:
                    main(i)
                if 1 <= i <= 16:
                    squares(i - 1)
                if i >= 2 and i - 2 in roped:
                    swap(i - 2)
            for t in range(TT):
                if t >= 2:
                    pe.wait_ge(v_ready, t - 1)
                for f in range(2):
                    last = pe.matmul(ps[:, 6 + t % 2], down[:, 3 + f, t * P:(t + 1) * P],
                                     w_ukv[:, f].rearrange("p (h c) -> p h c", h=HEADS)[:, :, NOPE:], start=f == 0, stop=f == 1)
                last.then_inc(v_done, 1)

        @block.scalar
        def _(act):
            for n in range(5):
                act.wait_ge(down_done, n + 1)
                act.activation(sq[:, n], ps[:, n], ACT.Square).then_inc(dsq_ready, 1)
                act.activation(down[:, n], ps[:, n], ACT.Copy).then_inc(down_ready, 1)
            for n in range(2):
                act.wait_ge(dss_done, n + 1)
                act.activation(rstd[:, n], ps[:, 5 + n], ACT.Sqrt, scale=1.0 / (Q_LORA, KV_LORA)[n],
                               bias=k.eps[:, 0:1]).then_inc(dsd_ready, 1)
            act.wait_ge(ang_ready, 1)
            act.activation(sin[0:QK], sin[0:QK], ACT.Sin).then_inc(sin_ready, 1)
            act.wait_ge(cos_in, 1)
            act.activation(cos[0:QK], cos[0:QK], ACT.Sin).then_inc(sin_ready, 1)
            for i in range(17):
                if i < 16:
                    kind, h = items[i]
                    m = rows[i]
                    act.wait_ge(head_done, i + 1)
                    if i >= 2:
                        act.wait_ge(hss_done, i - 1)
                    act.activation(hsq[0:m, i % 2], ps[0:m, i % 2], ACT.Square).then_inc(hsq_ready, 1)
                    act.activation((Q if kind == "q" else K)[0:m, h], ps[0:m, i % 2], ACT.Copy).then_inc(head_ready, 1)
                if i:
                    m = rows[i - 1]
                    act.wait_ge(hss_done, i)
                    if i >= 3:
                        act.wait_ge(head_normed, i - 2)
                    act.activation(hsd[0:m, (i - 1) % 2], ps[0:m, 2 + (i - 1) % 2], ACT.Sqrt, bias=k.eps[0:m, 0:1]).then_inc(hsd_ready, 1)
            for t in range(TT):
                act.wait_ge(v_done, t + 1)
                act.activation(V[:, t], ps[:, 6 + t % 2], ACT.Copy).then_inc(v_ready, 1)

        @block.vector
        def _(dve):
            link = chained(dve, mla_chain)
            dve.wait_ge(pos_ld, 16)
            link(dve.tensor_copy(ang[0:QK], pos[0:QK]))
            link(dve.tensor_scalar(ang[0:QK], ang[0:QK], k.vec("inv_freq")[0:QK], None, ALU.mult))
            for table, quarter, ready in ((sin, 0.0, ang_ready), (cos, 0.25, cos_in)):
                link(dve.tensor_scalar(turns[0:QK], ang[0:QK], 1 / TWO_PI, quarter, ALU.mult, ALU.add))
                link(dve.tensor_scalar(turns[0:QK], turns[0:QK], MAGIC, None, ALU.add))
                link(dve.tensor_scalar(turns[0:QK], turns[0:QK], MAGIC, None, ALU.subtract))
                link(dve.scalar_tensor_tensor(red[0:QK], turns[0:QK], -C1, ang[0:QK], ALU.mult, ALU.add))
                link(dve.scalar_tensor_tensor(red[0:QK], turns[0:QK], -C2, red[0:QK], ALU.mult, ALU.add))
                link(dve.scalar_tensor_tensor(red[0:QK], turns[0:QK], -C3, red[0:QK], ALU.mult, ALU.add))
                link(dve.tensor_scalar(red[0:QK], red[0:QK], quarter * TWO_PI, None, ALU.add))
                dve.tensor_scalar(table[0:QK], red[0:QK], float(np.float32(3.1415925)), -float(np.float32(3.1415925)),
                                  ALU.min, ALU.max).then_inc(ready, 1)
                dve.wait_ge(ready, 1)
            for n in range(2):
                dve.wait_ge(dsd_ready, n + 1)
                link(dve.reciprocal(rstd[:, n], rstd[:, n]))
                for f in ((0, 1, 2), (3, 4))[n]:
                    dve.wait_ge(down_ready, f + 1)
                    dve.scalar_tensor_tensor(down[:, f], down[:, f], k.vec("mla_q_norm_w", f), rstd[:, n],
                                             ALU.mult, ALU.mult).then_inc(down_normed, 1)
            dve.wait_ge(sin_ready, 2)

            def turn(i):
                kind, h = items[i]
                n = roped.index(i)
                x = (Q if kind == "q" else K)[rope, h]
                dve.wait_ge(swap_done, n + 1)
                link(dve.tensor_tensor(turned[rope], ps[rope, 4 + n % 2], sin[rope], ALU.mult))
                link(dve.tensor_tensor(x, x, cos[rope], ALU.mult))
                dve.tensor_tensor(x, x, turned[rope], ALU.add).then_inc(roped_ready, 1)
                dve.wait_ge(roped_ready, n + 1)

            for i in range(17):
                if i < 16:
                    kind, h = items[i]
                    m = rows[i]
                    x = (Q if kind == "q" else K)[0:m, h]
                    dve.wait_ge(hsd_ready, i + 1)
                    dve.wait_ge(head_ready, i + 1)
                    link(dve.reciprocal(hsd[0:m, i % 2], hsd[0:m, i % 2]))
                    dve.scalar_tensor_tensor(x, x, k.vec("qn_w" if kind == "q" else "kn_w")[0:m], hsd[0:m, i % 2],
                                             ALU.mult, ALU.mult).then_inc(head_normed, 1)
                if i and i - 1 in roped:
                    turn(i - 1)

        @block.gpsimd
        def _(pool):
            pool.wait_ge(roped_ready, len(roped))
            for h in range(1, HEADS):
                pool.tensor_copy(K[rope, h], K[rope, 0]).then_inc(kpe_copied, 1)


def phase_attention(nc, k, io):
    Q, K, V = k.view(90, [HEADS, T]), k.view(106, [HEADS, T]), k.view(122, [TT, HEADS * NOPE])
    oT = k.view(24, [RT, T])
    probs, probsT, diag = k.view(130, [2, T]), k.view(134, [2, TT, P]), k.view(138, [2, P])
    mx, nb, rs, ri = (k.view(140 + n, [32]) for n in range(4))
    scale = float(1.0 / np.sqrt(QK))
    units = [(h, q) for h in range(HEADS) for q in range(TT)]
    ps = k.ps
    with nc.Block() as block:
        s_done, masked, max_ready, nb_ready, exp_ready, diag_ready, pt_done, pt_out, o_done, o_out, rinv_ready = map(
            k.sem, ("s_done", "masked", "max_ready", "nb_ready", "exp_ready", "diag_ready", "pt_done", "pt_out", "o_done2", "o_out", "rinv_ready"))

        @block.tensor
        def _(pe):
            def scores(u):
                h, q = units[u]
                if u >= 2:
                    pe.wait_ge(exp_ready, u - 1)
                n = (q + 1) * P
                pe.matmul(ps[:, u % 2, 0:n], Q[0:QK, h, q * P:n], K[0:QK, h, 0:n], start=True, stop=True).then_inc(s_done, 1)

            def weighted(u):
                h, q = units[u]
                half = slice(64 * (h % 2), 64 * (h % 2) + 64)
                pe.wait_ge(diag_ready, u + 1)
                if u >= 2:
                    pe.wait_ge(pt_out, u - 1)
                for t in range(q + 1):
                    last = pe.matmul(ps[:, 2 + u % 2, t * P:(t + 1) * P], probs[:, u % 2, t * P:(t + 1) * P],
                                     diag[:, u % 2], start=True, stop=True)
                last.then_inc(pt_done, 1)

            def values(u):
                h, q = units[u]
                half = slice(64 * (h % 2), 64 * (h % 2) + 64)
                pe.wait_ge(pt_out, u + 1)
                if q == 0 and h >= 2:
                    pe.wait_ge(o_out, h - 1)
                for t in range(q + 1):
                    last = pe.matmul(ps[half, 4 + h % 2, q * P:(q + 1) * P], V[:, t, h * NOPE:(h + 1) * NOPE],
                                     probsT[:, u % 2, t], start=t == 0, stop=t == q)
                last.then_inc(o_done, 1)

            for u in range(len(units) + 2):
                if u < len(units):
                    scores(u)
                if 1 <= u <= len(units):
                    weighted(u - 1)
                if u >= 2:
                    values(u - 2)

        @block.vector
        def _(dve):
            def top(u):
                h, q = units[u]
                dve.wait_ge(s_done, u + 1)
                own = ps[:, u % 2, q * P:(q + 1) * P]
                dve.tensor_tensor(own, own, k.const("causal"), ALU.add).then_inc(masked, 1)
                dve.wait_ge(masked, u + 1)
                dve.reduce_max(mx[:, u:u + 1], ps[:, u % 2, 0:(q + 1) * P], AX.X).then_inc(max_ready, 1)
                dve.wait_ge(max_ready, u + 1)
                dve.tensor_scalar(nb[:, u:u + 1], mx[:, u:u + 1], -scale, None, ALU.mult).then_inc(nb_ready, 1)

            def bottom(u):
                dve.wait_ge(exp_ready, u + 1)
                if u >= 2:
                    dve.wait_ge(pt_done, u - 1)
                dve.reciprocal(ri[:, u:u + 1], rs[:, u:u + 1]).then_inc(rinv_ready, 1)
                dve.wait_ge(rinv_ready, u + 1)
                dve.tensor_scalar(diag[:, u % 2], k.const("ident"), ri[:, u:u + 1], None, ALU.mult).then_inc(diag_ready, 1)

            def turned(u):
                h, q = units[u]
                dve.wait_ge(pt_done, u + 1)
                if u >= 2:
                    dve.wait_ge(o_done, u - 1)
                dve.tensor_copy(probsT[:, u % 2, 0:q + 1], ps[:, 2 + u % 2, 0:(q + 1) * P].rearrange("p (t c) -> p t c", c=P)).then_inc(pt_out, 1)

            for u in range(len(units) + 1):
                if u < len(units):
                    top(u)
                    bottom(u)
                if u:
                    turned(u - 1)

        @block.scalar
        def _(act):
            def copy_out(h):
                half = slice(64 * (h % 2), 64 * (h % 2) + 64)
                act.wait_ge(o_done, TT * (h + 1))
                act.activation(oT[half, h // 2], ps[half, 4 + h % 2], ACT.Copy).then_inc(o_out, 1)

            for u, (h, q) in enumerate(units):
                act.wait_ge(nb_ready, u + 1)
                if u >= 2:
                    act.wait_ge(pt_done, u - 1)
                n = (q + 1) * P
                act.activation(probs[:, u % 2, 0:n], ps[:, u % 2, 0:n], ACT.Exp, scale=scale, bias=nb[:, u:u + 1],
                               accum_out=rs[:, u:u + 1]).then_inc(exp_ready, 1)
                if q == 1 and h:
                    copy_out(h - 1)
            copy_out(HEADS - 1)


def phase_merge(nc, k, io):
    xn, yg, oT = k.view(0, [KT, T]), k.view(16, [RT, T]), k.view(24, [RT, T])
    hT = k.view(32, [KT, T])
    mixed = k.view(48, [KT, T])
    gate_ring = [k.view(64 + 4 * s, [KT, P]) for s in range(6)]
    out_ring = [k.view(88 + 2 * s, [RT, P]) for s in range(6)]
    xres = k.view(100, [KT, T])
    ga, gb = k.view(116, [2, T]), k.view(120, [2, T])
    ps = k.ps
    part = lambda w: w.rearrange("(k p) n -> p k n", p=P)
    w_in, w_a, w_b, w_out = (part(io[n]) for n in ("w_in", "rw_w_o", "mla_w_o", "w_out"))
    with nc.Block() as block:
        gate_ld = [k.sem(f"gate_ld{s}") for s in range(6)]
        out_ld = [k.sem(f"out_ld{s}") for s in range(6)]
        x_ld, g_done, y_done, gate_ready, part_ready, mixed_ready, h_done, h_ready = map(
            k.sem, ("xres_ld", "mg_done", "my_done", "gate_ready", "part_ready", "mixed_ready", "h_done", "h_ready"))
        loads = [(w_in, col + n * P) for n in range(KT) for col in (GA_COL, GB_COL)] + [(w_out, n * P) for n in range(KT)]

        @block.sync
        def _(sp):
            sp.dma_start(xres, io["xT"].rearrange("(k p) n -> p k n", p=P)).then_inc(x_ld, 16)
            for n, (w, col) in enumerate(loads):
                if n >= 6:
                    old = n - 6
                    if old < 2 * KT:
                        sp.wait_ge(g_done, old + 1)
                    else:
                        sp.wait_ge(h_done, old - 2 * KT + 1)
                sp.dma_start(gate_ring[n % 6], w[:, :, col:col + P]).then_inc(gate_ld[n % 6], 16)
                if n < 2 * KT:
                    if n >= 6:
                        sp.wait_ge(y_done, n - 5)
                    sp.dma_start(out_ring[n % 6], (w_a, w_b)[n % 2][:, :, n // 2 * P:(n // 2 + 1) * P]).then_inc(out_ld[n % 6], 16)

        @block.tensor
        def _(pe):
            for n in range(2 * KT):
                pe.wait_ge(gate_ld[n % 6], 16 * (n // 6 + 1))
                if n >= 4:
                    pe.wait_ge(gate_ready, n - 3)
                for f in range(KT):
                    last = pe.matmul(ps[:, n % 4], gate_ring[n % 6][:, f], xn[:, f], start=f == 0, stop=f == KT - 1)
                last.then_inc(g_done, 1)
                pe.wait_ge(out_ld[n % 6], 16 * (n // 6 + 1))
                if n >= 4:
                    pe.wait_ge(part_ready, n - 3)
                for f in range(RT):
                    last = pe.matmul(ps[:, 4 + n % 4], out_ring[n % 6][:, f], (yg, oT)[n % 2][:, f], start=f == 0, stop=f == RT - 1)
                last.then_inc(y_done, 1)
            for n in range(KT):
                m = 2 * KT + n
                pe.wait_ge(gate_ld[m % 6], 16 * (m // 6 + 1))
                if n == 0:
                    pe.wait_ge(gate_ready, 2 * KT)
                if n >= 4:
                    pe.wait_ge(h_ready, n - 3)
                for f in range(KT):
                    if n == 0:
                        pe.wait_ge(mixed_ready, f + 1)
                    last = pe.matmul(ps[:, n % 4], gate_ring[m % 6][:, f], mixed[:, f], start=f == 0, stop=f == KT - 1)
                last.then_inc(h_done, 1)

        @block.scalar
        def _(act):
            for n in range(2 * KT):
                act.wait_ge(g_done, n + 1)
                if n >= 4:
                    act.wait_ge(mixed_ready, n // 2 - 1)
                act.activation((ga, gb)[n % 2][:, n // 2 % 2], ps[:, n % 4], ACT.Sigmoid).then_inc(gate_ready, 1)

        @block.vector
        def _(dve):
            for n in range(2 * KT):
                dve.wait_ge(gate_ready, n + 1)
                dve.wait_ge(y_done, n + 1)
                g = (ga, gb)[n % 2][:, n // 2 % 2]
                dve.tensor_tensor(g, g, ps[:, 4 + n % 4], ALU.mult).then_inc(part_ready, 1)
                if n % 2:
                    dve.wait_ge(part_ready, n + 1)
                    dve.tensor_tensor(mixed[:, n // 2], ga[:, n // 2 % 2], g, ALU.add).then_inc(mixed_ready, 1)
            dve.wait_ge(x_ld, 16)
            for n in range(KT):
                dve.wait_ge(h_done, n + 1)
                dve.tensor_tensor(hT[:, n], ps[:, n % 4], xres[:, n], ALU.add).then_inc(h_ready, 1)


def phase_route_scores(nc, k, io):
    hT, hn, h_hi, h_lo = k.view(32, [KT, T]), k.view(0, [KT, T]), k.view(16, [KT, T], F16), k.view(24, [KT, T], F16)
    ring = [k.view(48 + 4 * s, [KT, P]) for s in range(4)]
    qT = k.view(64, [2, T])
    subk = k.view(68, [2 * PH, NK])
    sq, rstd = k.view(76, [KT, T]), k.view(92, [T])
    sc = k.view(96, [TT, 2 * PH, NK])
    top, top_i = k.top, k.top_i
    rest = k.view(94, [2, NK])
    w_q = io["peer_w_query"].rearrange("(k p) n -> p k n", p=P)
    ps = k.ps
    with nc.Block() as block:
        w_ld = [k.sem(f"w_ld{s}") for s in range(4)]
        subk_ld, sq_ready, ss_done, rt_ready, rstd_ready, hn_ready, hi_ready, lo_ready = map(
            k.sem, ("subk_ld", "sq_ready", "ss_done", "rt_ready", "rstd_ready", "hn_ready", "hi_ready", "lo_ready"))
        q_done, q_out, sc_done, sc_out, top_step = map(k.sem, ("q_done", "q_out", "sc_done", "sc_out", "top_step"))

        @block.sync
        def _(sp):
            sp.dma_start(subk, io["sub_keysT"]).then_inc(subk_ld, 16)
            for n in range(2 * PH):
                if n >= 4:
                    sp.wait_ge(q_done, n - 3)
                sp.dma_start(ring[n % 4], w_q[:, :, n * P:(n + 1) * P]).then_inc(w_ld[n % 4], 16)

        @block.tensor
        def _(pe):
            for n in range(KT):
                pe.wait_ge(sq_ready, n + 1)
                last = pe.matmul(ps[:, 0], k.const("ones"), sq[:, n], start=n == 0, stop=n == KT - 1)
            last.then_inc(ss_done, 1)

            def scores(n):
                pe.wait_ge(q_out, n + 1)
                if n >= 2:
                    pe.wait_ge(sc_out, n - 1)
                for t in range(TT):
                    last = pe.matmul(ps[:, 3 + n % 2, t * P:(t + 1) * P], qT[:, n % 2, t * P:(t + 1) * P], subk[:, n],
                                     start=True, stop=True)
                last.then_inc(sc_done, 1)

            pe.wait_ge(subk_ld, 16)
            for n in range(2 * PH):
                pe.wait_ge(w_ld[n % 4], 16 * (n // 4 + 1))
                if n >= 2:
                    pe.wait_ge(q_out, n - 1)
                for f in range(KT):
                    if n == 0:
                        pe.wait_ge(hn_ready, f + 1)
                    last = pe.matmul(ps[:, 1 + n % 2], ring[n % 4][:, f], hn[:, f], start=f == 0, stop=f == KT - 1)
                last.then_inc(q_done, 1)
                if n:
                    scores(n - 1)
            scores(2 * PH - 1)

        @block.scalar
        def _(act):
            for n in range(KT):
                act.activation(sq[:, n], hT[:, n], ACT.Square).then_inc(sq_ready, 1)
            act.wait_ge(ss_done, 1)
            act.activation(rstd, ps[:, 0], ACT.Sqrt, scale=1.0 / D, bias=k.eps[:, 0:1]).then_inc(rt_ready, 1)
            for n in range(KT):
                act.wait_ge(hn_ready, n + 1)
                act.activation(h_hi[:, n], hn[:, n], ACT.Copy).then_inc(hi_ready, 1)

            def score_copy(n):
                act.wait_ge(sc_done, n + 1)
                act.activation(sc[:, :, n], ps[:, 3 + n % 2].rearrange("p (t n) -> p t n", t=TT), ACT.Copy).then_inc(sc_out, 1)

            for n in range(2 * PH):
                act.wait_ge(q_done, n + 1)
                if n >= 2:
                    act.wait_ge(sc_done, n - 1)
                act.activation(qT[:, n % 2], ps[:, 1 + n % 2], ACT.Copy).then_inc(q_out, 1)
                if n:
                    score_copy(n - 1)
            score_copy(2 * PH - 1)

        @block.vector
        def _(dve):
            dve.wait_ge(rt_ready, 1)
            dve.reciprocal(rstd, rstd).then_inc(rstd_ready, 1)
            dve.wait_ge(rstd_ready, 1)
            for n in range(KT):
                dve.scalar_tensor_tensor(hn[:, n], hT[:, n], k.vec("norm2_w", n), rstd, ALU.mult, ALU.mult).then_inc(hn_ready, 1)
            for n in range(KT):
                dve.wait_ge(hi_ready, n + 1)
                dve.tensor_tensor(h_lo[:, n], hn[:, n], h_hi[:, n], ALU.subtract).then_inc(lo_ready, 1)
            steps = 0
            for n in range(2 * PH):
                dve.wait_ge(sc_out, n + 1)
                for t in range(0, TT, 2):
                    two = [(sc[:, t + b, n], top[:, t + b, n], top_i[:, t + b, n], rest[:, b]) for b in range(2)]
                    if steps:
                        dve.wait_ge(top_step, steps)
                    for stage in (lambda s, v, i, r: dve.max(v[:, 0:8], s),
                                  lambda s, v, i, r: dve.max_index(i[:, 0:8], v[:, 0:8], s),
                                  lambda s, v, i, r: dve.match_replace(r, v[:, 0:8], s, -3.0e38),
                                  lambda s, v, i, r: dve.max(v[:, 8:16], r),
                                  lambda s, v, i, r: dve.max_index(i[:, 8:16], v[:, 8:16], r)):
                        for b in range(2):
                            stage(*two[b]).then_inc(top_step, 1)
                        steps += 2
                        dve.wait_ge(top_step, steps)


AHEAD_PICKS, AHEAD_PER_ROUND = 24, 4


class Ahead:

    def __init__(self, k, io):
        self.k, self.uT, self.acts = k, io["uT"], io["acts"]
        self.hn = k.view(0, [KT, T])
        self.u = [k.view(120 + 4 * s, [KT, P]) for s in range(4)]
        self.out = k.view(152, [4, T])
        self.u_ld = [k.sem(f"ahead_u_ld{s}") for s in range(4)]
        self.stored = [k.sem(f"ahead_stored{s}") for s in range(4)]
        self.done, self.ready = k.sem("ahead_done"), k.sem("ahead_ready")

    def load(self, eng, m, s):
        eng.dma_start(self.u[s], self.uT[bass.ds(m, 1)].rearrange("i p f e -> (i p) f e")).then_inc(self.u_ld[s], 16)

    def products(self, pe, m, s, fours, features):
        if features[0] == 0:
            pe.wait_ge(self.u_ld[s], (fours + 1) * 16)
            if not isinstance(m, int) or m >= 2:
                pe.wait_ge(self.ready, m - 1)
        for f in features:
            last = pe.matmul(self.k.ps[:, 6 + s % 2], self.u[s][:, f], self.hn[:, f], start=f == 0, stop=f == KT - 1)
        if features[-1] == KT - 1:
            last.then_inc(self.done, 1)

    def finish(self, act, m, s, fours):
        act.wait_ge(self.done, m + 1)
        self.load(act, m + 4, s)
        if not isinstance(m, int) or m >= 4:
            act.wait_ge(self.stored[s], fours * 16)
        act.activation(self.out[:, s], self.k.ps[:, 6 + s % 2], ACT.Gelu).then_inc(self.ready, 1)
        act.wait_ge(self.ready, m + 1)
        act.dma_start(self.acts[bass.ds(m, 1)].rearrange("i p t -> (i p) t"), self.out[:, s]).then_inc(self.stored[s], 16)


def phase_route_picks(nc, k, io):
    top, top_i = k.top, k.top_i
    cand, rest = k.view(48, [PH, 256]), k.view(56, [2, 256])
    best, best_i = k.view(58, [PH, TOPK]), k.view(59, [PH, TOPK], U32)
    pos = k.view(60, [2, PICKS], U32)
    posf, keyf = k.view(61, [2, PICKS]), k.view(62, [2 * PH, TOPK])
    hit = k.view(64, [PICKS, TOPK])
    picked = k.view(72, [3, PICKS])
    gsum = k.view(74, [PH])
    picksT = k.picksT
    iota16 = k.const("iota")[:, 0:TOPK].unsqueeze(1).to_broadcast([P, PICKS, TOPK])
    ps = k.ps
    with nc.Block() as block:
        step, gate_in, gate_exp, picked_ready, turn_done, turn_out = map(
            k.sem, ("step", "gate_in", "gate_exp", "picked_ready", "turn_done", "turn_out"))
        ahead = k.ahead = Ahead(k, io)
        AT = AHEAD_PICKS // TT

        @block.sync
        def _(sp):
            for m in range(4):
                ahead.load(sp, m, m)

        @block.tensor
        def _(pe):
            for t in range(TT):
                for m in range(t * AT, (t + 1) * AT):
                    ahead.products(pe, m, m % 4, m // 4, range(KT))
                pe.wait_ge(picked_ready, t + 1)
                for n in range(3):
                    last = pe.matmul(ps[:, n, t * P:(t + 1) * P], picked[:, n], k.const("ident"), start=True, stop=True)
                last.then_inc(turn_done, 1)

        @block.scalar
        def _(act):
            for t in range(TT):
                for m in range(t * AT, (t + 1) * AT):
                    ahead.finish(act, m, m % 4, m // 4)
                act.wait_ge(gate_in, t + 1)
                act.activation(picked[:, 2], picked[:, 2], ACT.Exp).then_inc(gate_exp, 1)
            act.wait_ge(turn_done, TT)
            for n in range(3):
                act.activation(picksT[:, n], ps[:, n], ACT.Copy).then_inc(turn_out, 1)

        @block.vector
        def _(dve):
            link = chained(dve, step)
            for t in range(TT):
                pair = top[:, t].rearrange("p (h s) a -> p s h a", s=2)
                first, second = pair[:, 0], pair[:, 1]
                link(dve.tensor_copy(keyf[:, :, :], top_i[:, t]))
                link(dve.tensor_tensor(cand.rearrange("p h (a b) -> p h a b", a=TOPK),
                                       first.unsqueeze(3).to_broadcast([P, PH, TOPK, TOPK]),
                                       second.unsqueeze(2).to_broadcast([P, PH, TOPK, TOPK]), ALU.add))
                for h in range(0, PH, 2):
                    two = [(cand[:, h + b], best[:, h + b], best_i[:, h + b], rest[:, b]) for b in range(2)]
                    for stage in (lambda s, v, i, r: dve.max(v[:, 0:8], s),
                                  lambda s, v, i, r: dve.max_index(i[:, 0:8], v[:, 0:8], s),
                                  lambda s, v, i, r: dve.match_replace(r, v[:, 0:8], s, -3.0e38),
                                  lambda s, v, i, r: dve.max(v[:, 8:16], r),
                                  lambda s, v, i, r: dve.max_index(i[:, 8:16], v[:, 8:16], r)):
                        for b in range(2):
                            link(stage(*two[b]))
                if t:
                    dve.wait_ge(turn_done, t)
                flat_i = best_i.rearrange("p h a -> p (h a)")
                link(dve.tensor_scalar(pos[:, 0], flat_i, 4, None, ALU.logical_shift_right))
                link(dve.tensor_scalar(pos[:, 1], flat_i, 15, None, ALU.bitwise_and))
                link(dve.tensor_copy(posf[:, :, :], pos[:, :, :]))
                dve.tensor_tensor(picked[:, 2].rearrange("p (h a) -> p h a", h=PH), best[:, :, :],
                                  best[:, :, 0:1].to_broadcast([P, PH, TOPK]), ALU.subtract).then_inc(gate_in, 1)
                keys = keyf.rearrange("p (h s) a -> p s h a", s=2)
                for n in range(2):
                    link(dve.tensor_tensor(hit[:, :, :], posf[:, n].unsqueeze(2).to_broadcast([P, PICKS, TOPK]), iota16, ALU.is_equal))
                    link(dve.tensor_tensor(hit.rearrange("p (h q) a -> p h q a", h=PH), hit.rearrange("p (h q) a -> p h q a", h=PH),
                                           keys[:, n].unsqueeze(2).to_broadcast([P, PH, TOPK, TOPK]), ALU.mult))
                    link(dve.tensor_reduce(picked[:, n], hit[:, :, :], AX.X, ALU.add))
                dve.wait_ge(gate_exp, t + 1)
                gates = picked[:, 2].rearrange("p (h a) -> p h a", h=PH)
                link(dve.tensor_reduce(gsum, gates, AX.X, ALU.add))
                link(dve.reciprocal(gsum, gsum))
                dve.tensor_tensor(gates, gates, gsum.unsqueeze(2).to_broadcast([P, PH, TOPK]), ALU.mult).then_inc(picked_ready, 1)
                dve.wait_ge(picked_ready, t + 1)


STAGE = 64
BANKS = 4
NAHEAD = AHEAD_PICKS + AHEAD_PER_ROUND * T // (2 * STAGE)


def phase_gate_matrix(nc, k, io):
    key1, key2, gate = (k.picksT[:, n] for n in range(3))
    SL, FEW = 16, 8
    one_j, gated_i = k.view(48, [SL, NK]), k.view(160, [SL, NK])
    stage = [k.view(56 + 32 * s, [NK, STAGE]) for s in range(2)]
    Gd = io["gates"]
    ps = k.ps
    with nc.Block() as block:
        hot_ready, g_done, staged = map(k.sem, ("hot_ready", "g_done", "staged"))
        stored = k.gates_stored = [k.sem(f"stored{s}") for s in range(2)]
        ROUNDS = T // (2 * STAGE)
        ahead = k.ahead

        def ahead_tile(it, t):
            s = t * AHEAD_PER_ROUND // (2 * STAGE)
            return AHEAD_PICKS + it * AHEAD_PER_ROUND + s, s, AHEAD_PICKS // 4 + it

        def rounds(eng, body):
            body(0)
            with eng.Fori(1, ROUNDS) as it:
                body(it)

        def wait(eng, sem, value):
            if not isinstance(value, int) or value > 0:
                eng.wait_ge(sem, value)

        @block.vector
        def _(dve):
            def body(it):
                for t in range(0, 2 * STAGE, FEW):
                    at = it * 2 * STAGE + t
                    if t >= SL:
                        dve.wait_ge(g_done, at - FEW)
                    else:
                        wait(dve, g_done, it * 2 * STAGE - SL + FEW + t if not isinstance(it, int) or it else 0)
                    few = slice(t % SL, t % SL + FEW)
                    dve.tensor_tensor(one_j[:, few], k.const("iota").unsqueeze(1).to_broadcast([P, FEW, NK]),
                                      key2[:, bass.ds(at, FEW)].unsqueeze(2).to_broadcast([P, FEW, NK]), ALU.is_equal)
                    for b in range(FEW):
                        dve.tensor_scalar(gated_i[:, (t + b) % SL], k.const("iota"), key1[:, bass.ds(at + b, 1)],
                                          gate[:, bass.ds(at + b, 1)], ALU.is_equal, ALU.mult).then_inc(hot_ready, 1)
            rounds(dve, body)

        @block.tensor
        def _(pe):
            def body(it):
                for t in range(2 * STAGE):
                    if t % 4 == 0:
                        before = it * (2 * STAGE // 4) + t // 4 - BANKS + 1
                        if not isinstance(it, int) or before > 0:
                            pe.wait_ge(staged, before)
                    pe.wait_ge(hot_ready, it * 2 * STAGE + t + 1)
                    pe.matmul(ps[:, t // 4 % BANKS, t % 4 * P:(t % 4 + 1) * P], one_j[:, t % SL], gated_i[:, t % SL],
                              start=True, stop=True).then_inc(g_done, 1)
                    if t % FEW == FEW - 1:
                        part = t // FEW % 4
                        ahead.products(pe, *ahead_tile(it, t), range(part * KT // 4, (part + 1) * KT // 4))
            rounds(pe, body)

        @block.scalar
        def _(act):
            def body(it):
                for q in range(2 * STAGE // 4):
                    s, at = divmod(4 * q, STAGE)
                    if at == 0:
                        wait(act, stored[s], it * 16)
                    act.wait_ge(g_done, it * 2 * STAGE + 4 * q + 4)
                    act.activation(stage[s][:, :, at:at + 4].rearrange("p i t -> p t i"),
                                   ps[:, q % BANKS].rearrange("p (t i) -> p t i", t=4), ACT.Copy).then_inc(staged, 1)
                    if q % 8 == 7:
                        ahead.finish(act, *ahead_tile(it, 4 * q))
            rounds(act, body)
            for s in range(4):
                act.wait_ge(ahead.stored[s], NAHEAD // 4 * 16)

        @block.sync
        def _(sp):
            def body(it):
                for s in range(2):
                    sp.wait_ge(staged, it * (2 * STAGE // 4) + (s + 1) * (STAGE // 4))
                    sp.dma_start(Gd[bass.ds(it * 2 + s, 1)].rearrange("s j i t -> (s j) i t"), stage[s]).then_inc(stored[s], 16)
            rounds(sp, body)


SCALE = 256.0
GROUP = 4


def phase_experts(nc, k, io):
    h_hi, h_lo, y = k.view(16, [KT, T], F16), k.view(24, [KT, T], F16), k.view(32, [KT, T])
    u_raw, v_raw = k.view(120, [4, KT, P]), k.view(64, [4, D])
    u_hi, u_lo = k.view(48, [4, KT, P], F16), k.view(188, [4, KT, P], F16)
    v_hi, v_lo = k.view(0, [8, D], F16), k.view(172, [8, D], F16)
    a_hi, a_lo = k.view(80, [8, T], F16), k.view(136, [8, T], F16)
    G = k.view(144, [8, T])
    acts, loaded = k.view(160, [2, T]), k.view(164, [4, T])
    OWN = NK - NAHEAD
    uT, v, Gd = io["uT"], io["peer_v"].rearrange("(i j) d -> i j d", j=NK), io["gates"]
    out = io["outT"].rearrange("(k p) t -> p k t", p=P)
    ps = k.ps
    N = NK
    with nc.Block() as block:
        u_ld = k.ahead.u_ld
        v_ld = [k.sem(f"v_ld{s}") for s in range(4)]
        g_ld = [k.sem(f"g_ld{s}") for s in range(8)]
        acts_ld = [k.sem(f"acts_ld{s}") for s in range(4)]
        u_hi_ready, u_lo_ready, v_hi_ready, v_lo_ready, act_ready, weighted, a_hi_ready, a_ready = map(
            k.sem, ("u_hi_ready", "u_lo_ready", "v_hi_ready", "v_lo_ready", "act_ready", "weighted", "a_hi_ready", "a_ready"))
        act_done, out_done, y_added, stored = map(k.sem, ("act_done", "out_done", "y_added", "stored"))

        def wait(eng, sem, value):
            if not isinstance(value, int) or value > 0:
                eng.wait_ge(sem, value)

        def steps(eng, step):
            def eights(first, end, own):
                def eight(it):
                    for r in range(8):
                        step(it, r, it * 8 + r, own)
                eight(first)
                with eng.Fori(first + 1, end - 1) as it:
                    eight(it)
                eight(end - 1)

            eights(0, OWN // 8, True)
            eights(OWN // 8, N // 8, False)
            for r in range(GROUP):
                step(N // 8, r, N + r, False)

        def tile_of(n, end=N):
            return not isinstance(n, int) or n < end

        @block.sync
        def _(sp):
            def step(it, r, n, own):
                if tile_of(n):
                    if not own:
                        wait(sp, a_ready, n - 3)
                        sp.dma_start(loaded[:, r % 4], io["acts"][bass.ds(n - OWN, 1)].rearrange("i p t -> (i p) t")).then_inc(acts_ld[r % 4], 16)
                    elif not (isinstance(n, int) and n < 4):
                        sp.wait_ge(u_lo_ready, n - 3)
                        sp.dma_start(u_raw[:, r % 4], uT[bass.ds(n + NAHEAD, 1)].rearrange("i p f e -> (i p) f e")).then_inc(u_ld[r % 4], 16)
                    tile = n + NAHEAD if own else n - OWN
                    if isinstance(n, int) and n == 0:
                        sp.wait_ge(k.gates_stored[0], 16 * T // (2 * STAGE))
                    wait(sp, v_lo_ready, n - 3)
                    sp.dma_start(v_raw[:, r % 4], v[bass.ds(tile, 1)].rearrange("i j d -> (i j) d")).then_inc(v_ld[r % 4], 16)
                    wait(sp, weighted, n - 7)
                    if isinstance(n, int) and n == 0:
                        sp.wait_ge(k.gates_stored[1], 16 * T // (2 * STAGE))
                    sp.dma_start(G[:, r].rearrange("p (s t) -> p s t", t=STAGE),
                                 Gd[:, :, bass.ds(tile, 1)].rearrange("s j i t -> j s (i t)")).then_inc(g_ld[r], 16)
            steps(sp, step)
            sp.wait_ge(y_added, N // GROUP * KT)
            sp.dma_start(out, y).then_inc(stored, 16)
            sp.wait_ge(stored, 16)

        @block.scalar
        def _(act):
            def split_u(it, r, m):
                act.wait_ge(u_ld[r % 4], (NAHEAD // 4 + it * 2 + r // 4 + 1) * 16)
                wait(act, act_done, m - 3)
                act.activation(u_hi[:, r % 4], u_raw[:, r % 4], ACT.Copy, scale=SCALE).then_inc(u_hi_ready, 1)

            def step(it, r, n, own):
                if isinstance(n, int) and n == 0:
                    split_u(0, 0, 0)
                    split_u(0, 1, 1)
                if own and tile_of(n + 2, OWN):
                    split_u(it + (r + 2) // 8, (r + 2) % 8, n + 2)
                if tile_of(n):
                    act.wait_ge(v_ld[r % 4], (it * 2 + r // 4 + 1) * 16)
                    wait(act, out_done, ((it * 2) + r // 4 - 1) * KT)
                    act.activation(v_hi[:, r], v_raw[:, r % 4], ACT.Copy, scale=SCALE).then_inc(v_hi_ready, 1)
                if own:
                    act.wait_ge(act_done, n + 1)
                    wait(act, a_ready, n - 1)
                    act.activation(acts[:, r % 2], ps[:, r % 2], ACT.Gelu, scale=1 / SCALE).then_inc(act_ready, 1)
            steps(act, step)

        @block.vector
        def _(dve):
            def split_u(r, m):
                dve.wait_ge(u_hi_ready, m + 1)
                dve.scalar_tensor_tensor(u_lo[:, r % 4], u_raw[:, r % 4], SCALE, u_hi[:, r % 4],
                                         ALU.mult, ALU.subtract).then_inc(u_lo_ready, 1)

            def step(it, r, n, own):
                if isinstance(n, int) and n == 0:
                    split_u(0, 0)
                    split_u(1, 1)
                if own and tile_of(n + 2, OWN):
                    split_u(r + 2, n + 2)
                if tile_of(n):
                    dve.wait_ge(v_hi_ready, n + 1)
                    dve.scalar_tensor_tensor(v_lo[:, r], v_raw[:, r % 4], SCALE, v_hi[:, r],
                                             ALU.mult, ALU.subtract).then_inc(v_lo_ready, 1)
                    if own:
                        x = acts[:, r % 2]
                        dve.wait_ge(act_ready, n + 1)
                    else:
                        x = loaded[:, r % 4]
                        dve.wait_ge(acts_ld[r % 4], ((it - OWN // 8) * 2 + r // 4 + 1) * 16)
                    dve.wait_ge(g_ld[r], (it + 1) * 16)
                    dve.tensor_tensor(x, x, G[:, r], ALU.mult).then_inc(weighted, 1)
                    dve.wait_ge(weighted, n + 1)
                    wait(dve, out_done, ((it * 2) + r // 4 - 1) * KT)
                    dve.tensor_copy(a_hi[:, r], x).then_inc(a_hi_ready, 1)
                    dve.wait_ge(a_hi_ready, n + 1)
                    dve.tensor_tensor(a_lo[:, r], x, a_hi[:, r], ALU.subtract).then_inc(a_ready, 1)
                if not (isinstance(n, int) and n < GROUP):
                    for b in range(2):
                        d = 2 * (r % 4) + b
                        nth = (it * 2 + r // 4 - 1) * KT + d
                        dve.wait_ge(out_done, nth + 1)
                        wait(dve, y_added, nth + 1 - KT)
                        dve.scalar_tensor_tensor(y[:, d], ps[:, 2 + d % 4], 1 / SCALE, y[:, d], ALU.mult, ALU.add).then_inc(y_added, 1)
            steps(dve, step)

        @block.tensor
        def _(pe):
            def step(it, r, n, own):
                if own:
                    pe.wait_ge(u_lo_ready, n + 1)
                    wait(pe, act_ready, n - 1)
                    for f in range(KT):
                        for w, x in ((u_hi, h_hi), (u_hi, h_lo), (u_lo, h_hi)):
                            last = pe.matmul(ps[:, r % 2], w[:, r % 4, f], x[:, f],
                                             start=f == 0 and x is h_hi and w is u_hi, stop=f == KT - 1 and w is u_lo)
                    last.then_inc(act_done, 1)
                if not (isinstance(n, int) and n < GROUP):
                    group = it * 2 + r // 4 - 1
                    if r % 4 == 0:
                        pe.wait_ge(a_ready, (group + 1) * GROUP)
                        pe.wait_ge(v_lo_ready, (group + 1) * GROUP)
                    for b in range(2):
                        d = 2 * (r % 4) + b
                        wait(pe, y_added, group * KT + d - 3)
                        for q in range(GROUP):
                            s = (r // 4 + 1) % 2 * 4 + q
                            for w, x in ((v_hi, a_hi), (v_hi, a_lo), (v_lo, a_hi)):
                                last = pe.matmul(ps[:, 2 + d % 4], w[:, s, d * P:(d + 1) * P], x[:, s],
                                                 start=q == 0 and x is a_hi and w is v_hi, stop=q == GROUP - 1 and w is v_lo)
                        last.then_inc(out_done, 1)
            steps(pe, step)


def laid_out(inputs):
    get = lambda n: np.asarray(inputs[n])
    q_w = np.concatenate([get("mla_qn_nope_w"), get("mla_qn_pe_w")])
    k_w = np.concatenate([get("mla_kn_nope_w"), get("mla_kn_pe_w")])
    half = ROPE // 2
    freq = (np.float32(10000.0) ** (-np.arange(half, dtype=np.float32) / np.float32(half))).astype(np.float32)
    given = {"qn_w": q_w, "kn_w": k_w, "rw_mu": get("rw_mu")[:14 * P], "rw_mu_tail": get("rw_mu")[14 * P:],
             "inv_freq": np.concatenate([np.zeros(NOPE, np.float32), freq, freq])}
    columns = []
    for name, rows, tiles in VECS:
        v = given[name] if name in given else get(name).reshape(-1)
        padded = np.zeros((P, tiles), np.float32)
        padded[:rows] = v.reshape(tiles, rows).T
        columns.append(padded)
    out = {"xT": get("x")[0].T, "positions": get("positions"), "vecs": np.concatenate(columns, axis=1),
           "consts": constant_array()}
    for name in ("w_in", "rw_w2", "rw_a2", "rw_g2", "rw_w_o", "mla_w_uq", "mla_w_ukv", "mla_w_o", "w_out",
                 "peer_w_query", "peer_v"):
        out[name] = get(name)
    out["sub_keysT"] = get("peer_sub_keys").reshape(2 * PH, NK, P).transpose(2, 0, 1)
    out["uT"] = get("peer_u").reshape(NK, NK, KT, P).transpose(0, 3, 2, 1)
    return {name: np.ascontiguousarray(a) for name, a in out.items()}




def build(nc, io, upto=99, dbg=None):
    with ExitStack() as ctx:
        k = Kit()
        arena = ctx.enter_context(nc.sbuf_tensor("arena", [P, ARENA_KB * 256], F32))
        k.consts = ctx.enter_context(nc.sbuf_tensor("consts", [P, NCONST], F32))
        k.vecs = ctx.enter_context(nc.sbuf_tensor("vecs", [P, NV], F32))
        k.eps = ctx.enter_context(nc.sbuf_tensor("eps", [P, 2], F32))
        k.chunk_decay = ctx.enter_context(nc.sbuf_tensor("chunk_decay", [P, RT, NCH], F32))
        k.ps = ctx.enter_context(nc.psum_tensor("ps", [P, 8, 512], F32))

        io = dict(io, gates=nc.dram_tensor("gates", (T // STAGE, NK, NK, STAGE), F32, kind="Internal").ap(),
                  acts=nc.dram_tensor("acts", (NAHEAD, P, T), F32, kind="Internal").ap())

        def view(at_kb, shape, dtype=F32):
            words = int(np.prod(shape)) * mybir.dt.size(dtype) // 4
            a = arena[:, at_kb * 256:at_kb * 256 + words]
            if dtype != F32:
                a = a.bitcast(dtype)
            if len(shape) > 1:
                names = "abcd"[:len(shape)]
                a = a.rearrange(f"p ({' '.join(names)}) -> p {' '.join(names)}", **dict(zip(names[1:], shape[1:])))
            return a

        k.view = view
        k.top, k.top_i = view(136, [TT, 2 * PH, TOPK]), view(140, [TT, 2 * PH, TOPK], U32)
        k.picksT = view(144, [3, T])
        sems = []

        def sem(name):
            sems.append(nc.alloc_semaphore(name=f"{k.phase}_{name}"))
            return sems[-1]

        k.sem = sem
        k.vec = lambda name, n=0: k.vecs[:, VEC_AT[name] + n:VEC_AT[name] + n + 1]
        k.const = lambda name: k.consts[:, CONST_AT[name][0]:sum(CONST_AT[name])]
        for n, phase in enumerate(PHASES):
            if n < upto:
                k.phase = phase.__name__.removeprefix("phase_")
                phase(nc, k, io)
                if phase is phase_merge:
                    nc.clear_and_free_semaphores(sems)
                    nc.all_engine_barrier()
                    sems.clear()
        if dbg:
            dbg(nc, k, io)


ARENA_KB = 196
PHASES = [phase_norm_and_rwkv_in, phase_rwkv_prepare, phase_delta_rule, phase_rwkv_out,
          phase_mla_project, phase_attention, phase_merge,
          phase_route_scores, phase_route_picks, phase_gate_matrix, phase_experts]




def kernel(**inputs):
    import concourse.bacc as bacc
    from concourse.bass_utils import run_bass_kernel_spmd

    nc = bacc.Bacc("TRN2", target_bir_lowering=False, num_devices=1)
    arrays, io = {}, {}
    for name, a in laid_out(inputs).items():
        arrays[f"in_{name}_dram"] = a
        io[name] = nc.dram_tensor(f"in_{name}_dram", a.shape, mybir.dt.from_np(a.dtype), kind="ExternalInput").ap()
    io["outT"] = nc.dram_tensor("out_0_dram", (D, T), F32, kind="ExternalOutput").ap()
    build(nc, io)
    r = run_bass_kernel_spmd(nc, [arrays], core_ids=[0])
    return np.ascontiguousarray(r.results[0]["out_0_dram"].T)[None]
```

```python
from contextlib import ExitStack

import numpy as np
import concourse.bass as bass
from concourse import mybir

F32 = mybir.dt.float32
F16 = mybir.dt.float16
I32 = mybir.dt.int32
U32 = mybir.dt.uint32
ALU = mybir.AluOpType
ACT = mybir.ActivationFunctionType
AX = mybir.AxisListType

P = 128
T = 512
D = 1024
KT = D // P
EPS = 1e-6
RW = 512
RT = RW // P
C = 64
NCH = T // C
NPR = NCH * RT
HALF = [slice(0, 64), slice(64, 128)]
GN_EPS = 64e-5
Q_LORA, KV_LORA, ROPE = 384, 256, 32
HEADS, NOPE, QK = 8, 64, 96
TT = T // P
PH, NK, TOPK = 8, 128, 16
PICKS = PH * TOPK
NE = NK * NK

SCALE = 256.0

RW_COLS = [(P * n, P) for n in range(13)] + [(1664, P), (1792, 32)]
Q_COL = 1824
KV_COL = Q_COL + Q_LORA
KPE_COL = KV_COL + KV_LORA
GA_COL = KPE_COL + ROPE
GB_COL = GA_COL + D

VECS = [("norm1_w", P, 8), ("rw_mu", P, 14), ("rw_mu_tail", 32, 1), ("rw_w0", P, 4), ("rw_a0", P, 4),
        ("rw_k_k", P, 4), ("rw_k_a", P, 4), ("rw_r_k", P, 4), ("rw_ln_w", P, 4), ("rw_ln_b", P, 4),
        ("mla_q_norm_w", P, 3), ("mla_kv_norm_w", P, 2), ("qn_w", QK, 1), ("kn_w", QK, 1),
        ("norm2_w", P, 8), ("inv_freq", QK, 1)]
VEC_AT = {name: sum(t for _, _, t in VECS[:n]) for n, (name, _, _) in enumerate(VECS)}
NV = sum(t for _, _, t in VECS)

LEVELS = [1, 2, 4, 8, 16, 32]
CONSTS = [("ones", P), ("head_ones", P), ("ident", P), ("qk_ones", QK), ("rope_swap", QK), ("iota", P),
          ("causal", P), ("chunk_start", T), ("strict", C), ("upto", C), ("fold", C), ("level1_t", C)] + \
         [(f"level{m}", C) for m in LEVELS[1:]]
CONST_AT = {name: (sum(c for _, c in CONSTS[:n]), cols) for n, (name, cols) in enumerate(CONSTS)}
NCONST = sum(c for _, c in CONSTS)


def constant_array():
    a = np.zeros((P, NCONST), np.float32)

    def put(name, m):
        at, cols = CONST_AT[name]
        a[:m.shape[0], at:at + cols] = m

    i, j = np.arange(P)[:, None], np.arange(P)[None, :]
    put("ones", np.ones((P, P)))
    put("head_ones", (i // 64 == j // 64) * 1.0)
    put("ident", (i == j) * 1.0)
    q, r = np.arange(QK)[:, None], np.arange(QK)[None, :]
    put("qk_ones", np.where((q < NOPE) & (r < NOPE), 1 / NOPE, 0) + np.where((q >= NOPE) & (r >= NOPE), 1 / ROPE, 0))
    half = ROPE // 2
    put("rope_swap", np.where((r >= NOPE) & (r < NOPE + half) & (q == r + half), -1.0, 0)
        + np.where((r >= NOPE + half) & (q == r - half), 1.0, 0))
    put("iota", np.broadcast_to(j, (P, P)) * 1.0)
    put("causal", np.where(j <= i, 0.0, -1e30))
    put("chunk_start", np.broadcast_to(np.arange(T)[None] % C != 0, (P, T)) * 1.0)
    s, t = np.arange(P)[:, None] % C, np.arange(C)[None, :]
    put("strict", (s < t) * 1.0)
    put("upto", (s <= t) * 1.0)
    put("fold", (s == t) * 1.0)
    put("level1_t", ((t // 2 == s // 2) & (t % 2 == 1) & (s % 2 == 0)) * 1.0)
    for m in LEVELS[1:]:
        put(f"level{m}", ((t // (2 * m) == s // (2 * m)) & (s // m % 2 == 1) & (t // m % 2 == 0)) * 1.0)
    return a


class Kit:
    pass


def chained(eng, sem):
    n = [0]

    def link(ins):
        n[0] += 1
        ins.then_inc(sem, 1)
        eng.wait_ge(sem, n[0])
    return link


def diagonal(bd, e, other=False):
    return bd[HALF[e], :, HALF[1 - e if other else e]]


def by_chunk(x):
    return x.rearrange("p j (c t) -> p c j t", t=C)


GATES_IN_PREPARE = 4


class Split:

    def __init__(self, k, name, raw, parts_kb, x_hi, x_lo):
        self.k, self.raw, self.x_hi, self.x_lo = k, raw, x_hi, x_lo
        self.hi, self.lo = k.view(parts_kb, [4, KT, P], F16), k.view(parts_kb + 8, [4, KT, P], F16)
        self.ld = [k.sem(f"{name}_ld{s}") for s in range(4)]
        self.hi_ready, self.lo_ready, self.done = (k.sem(f"{name}_{x}") for x in ("hi_ready", "lo_ready", "done"))

    def load(self, sp, n, columns):
        if n >= 4:
            sp.wait_ge(self.lo_ready, n - 3)
        m = columns.shape[-1]
        sp.dma_start(self.raw[n % 4][:, :, 0:m], columns).then_inc(self.ld[n % 4], 16)

    def split_hi(self, act, n, m=P):
        act.wait_ge(self.ld[n % 4], 16 * (n // 4 + 1))
        if n >= 4:
            act.wait_ge(self.done, n - 3)
        act.activation(self.hi[:, n % 4, :, 0:m], self.raw[n % 4][:, :, 0:m], ACT.Copy, scale=SCALE).then_inc(self.hi_ready, 1)

    def split_lo(self, dve, n, m=P):
        dve.wait_ge(self.hi_ready, n + 1)
        dve.scalar_tensor_tensor(self.lo[:, n % 4, :, 0:m], self.raw[n % 4][:, :, 0:m], SCALE, self.hi[:, n % 4, :, 0:m],
                                 ALU.mult, ALU.subtract).then_inc(self.lo_ready, 1)

    def products(self, pe, n, out, m=P, x_ready=None):
        pe.wait_ge(self.lo_ready, n + 1)
        for f in range(KT):
            if x_ready:
                for ready in x_ready:
                    pe.wait_ge(ready, f + 1)
            for w, x in ((self.hi, self.x_hi), (self.hi, self.x_lo), (self.lo, self.x_hi)):
                last = pe.matmul(out, w[:, n % 4, f, 0:m], x[:, f], start=f == 0 and w is self.hi and x is self.x_hi,
                                 stop=f == KT - 1 and w is self.lo)
        last.then_inc(self.done, 1)


class Gates:

    def __init__(self, k, io):
        self.k, self.w_in, self.store_to = k, io["w_in"].rearrange("(k p) n -> p k n", p=P), io["gate_acts"]
        self.stored = [k.sem(f"gates_stored{s}") for s in range(4)]
        self.ready = k.sem("gates_ready")

    def place(self, split, first, out_kb):
        self.split, self.first, self.out = split, first, self.k.view(out_kb, [4, T])

    def tile(self, m):
        return self.first + m

    def columns(self, m):
        col = (GA_COL, GB_COL)[m % 2] + m // 2 * P
        return self.w_in[:, :, col:col + P]

    def finish(self, act, m, bank):
        act.wait_ge(self.split.done, self.tile(m) + 1)
        if m >= 4:
            act.wait_ge(self.stored[m % 4], m // 4 * 16)
        act.activation(self.out[:, m % 4], self.k.ps[:, bank], ACT.Sigmoid, scale=1 / SCALE).then_inc(self.ready, 1)
        act.wait_ge(self.ready, m + 1)
        act.dma_start(self.store_to[m], self.out[:, m % 4]).then_inc(self.stored[m % 4], 16)


def phase_norm_and_rwkv_in(nc, k, io):
    x, sq, xn = k.view(112, [KT, T]), k.view(128, [KT, T]), k.view(144, [KT, T])
    ring = [k.view(64 + 4 * s, [KT, P]) for s in range(4)]
    raw = [k.view(96 + 3 * s, [T + 1]) for s in range(2)]
    diff = k.view(102, [T])
    rt, rstd = k.view(104, [T]), k.view(106, [T])
    mix, g = k.view(32, [15, T]), k.view(16, [RT, T])
    key = mix[:, 4:8]
    lw, L, ex, ea, a, _, kp, inv_n = (k.view(112 + 8 * n, [RT, T]) for n in range(8))
    w2a2, g2a, g2b = k.view(176, [RW]), k.view(178, [RW]), k.view(180, [RW])
    tw, sg = k.view(182, [T]), k.view(184, [2, T])
    ps = k.ps
    ORDER = [12, 13, 14] + list(range(4, 8)) + list(range(4)) + list(range(8, 12))
    COLS = [RW_COLS[t] for t in ORDER]
    x_hi, x_lo = k.xn_parts
    w_in = io["w_in"].rearrange("(k p) n -> p k n", p=P)
    NB = 3
    with nc.Block() as block:
        x_ld = [k.sem(f"x_ld{n}") for n in range(KT)]
        small_ld, sq_ready, ss_done, rt_ready, rstd_ready = map(k.sem, ("small_ld", "sq_ready", "ss_done", "rt_ready", "rstd_ready"))
        w = Split(k, "w_in", ring, 80, x_hi, x_lo)
        proj_done = w.done
        xn_ready, hi_ready, lo_ready, raw_ready, pad_ready, diff_ready, mix_done = map(
            k.sem, ("xn_ready", "xn_hi_ready", "xn_lo_ready", "raw_ready", "pad_ready", "diff_ready", "mix_done"))

        lora_ld, tw_ready, sg_ready, z_done, za_done, g_done, kk2_done = map(
            k.sem, ("lora_ld", "tw_ready", "sg_ready", "z_done", "za_done", "g_done", "kk2_done"))
        sw_ready, a_ready, g_ready, kk2_ready, norm_ready, ss_ready, ex_in, L_ready, ea_ready, chain = map(
            k.sem, ("sw_ready", "a_ready", "g_ready", "kk2_ready", "norm_ready", "ss_ready", "ex_in", "L_ready", "ea_ready", "chain"))

        @block.sync
        def _(sp):
            for n in range(KT):
                sp.dma_start(x[:, n], io["xT"][n * P:(n + 1) * P, :]).then_inc(x_ld[n], 16)
                if n == 0:
                    sp.dma_start(k.consts[:, :], io["consts"]).then_inc(small_ld, 16)
                    sp.dma_start(k.vecs[:, :], io["vecs"]).then_inc(small_ld, 16)
            for n, (col, m) in enumerate(COLS):
                w.load(sp, n, w_in[:, :, col:col + m])
                if n == 2:
                    sp.dma_start(w2a2[0:64], io["rw_w2"]).then_inc(lora_ld, 16)
                    sp.dma_start(w2a2[64:128], io["rw_a2"]).then_inc(lora_ld, 16)
                    sp.dma_start(g2a, io["rw_g2"][0:P, :]).then_inc(lora_ld, 16)
                    sp.dma_start(g2b[0:32], io["rw_g2"][P:160, :]).then_inc(lora_ld, 16)

        @block.scalar
        def _(act):
            def beside(n):
                if n == 1:
                    act.wait_ge(mix_done, 1)
                    act.activation(tw[0:64], mix[0:64, 12], ACT.Tanh).then_inc(tw_ready, 1)
                if n == 3:
                    act.wait_ge(mix_done, 3)
                    act.activation(sg[:, 0], mix[:, 13], ACT.Sigmoid).then_inc(sg_ready, 1)
                    act.activation(sg[0:32, 1], mix[0:32, 14], ACT.Sigmoid).then_inc(sg_ready, 1)
                    for j in range(RT):
                        act.wait_ge(z_done, j + 1)
                        act.activation(lw[:, j], ps[:, 4 + j], ACT.Sigmoid, bias=k.vec("rw_w0", j)).then_inc(sw_ready, 1)
                for j in range(RT) if n == 5 else ():
                    act.wait_ge(za_done, j + 1)
                    act.activation(a[:, j], ps[:, 4 + j], ACT.Sigmoid, bias=k.vec("rw_a0", j)).then_inc(a_ready, 1)
                for j in range(RT) if n == 7 else ():
                    act.wait_ge(g_done, j + 1)
                    act.activation(g[:, j], ps[:, 4 + j], ACT.Copy).then_inc(g_ready, 1)
                if n == 8:
                    act.wait_ge(mix_done, 7)
                    for j in range(RT):
                        act.activation(kp[:, j], key[:, j], ACT.Square, scale=k.vec("rw_k_k", j)).then_inc(kk2_ready, 1)
                if n == 9:
                    act.wait_ge(L_ready, RT)
                    act.activation(ea[:, :], L[:, :], ACT.Exp).then_inc(ea_ready, 1)
                if n == 10:
                    act.wait_ge(ex_in, 1)
                    act.activation(ex[:, :], ex[:, :], ACT.Exp)
                if n == 11:
                    act.wait_ge(ea_ready, 1)
                    act.activation(L[:, :], L[:, :], ACT.Exp, scale=-1.0)
                if n == 12:
                    act.wait_ge(ss_ready, 1)
                    act.activation(inv_n[:, :], inv_n[:, :], ACT.Sqrt).then_inc(norm_ready, 1)

            for n in range(KT):
                act.wait_ge(x_ld[n], 16)
                act.activation(sq[:, n], x[:, n], ACT.Square).then_inc(sq_ready, 1)
            for n in range(2):
                w.split_hi(act, n)
            act.wait_ge(ss_done, 1)
            act.wait_ge(pad_ready, 3)
            act.activation(rt, k.ps[:, 0], ACT.Sqrt, scale=1.0 / D, bias=k.eps[:, 0:1]).then_inc(rt_ready, 1)
            for n in range(KT):
                act.wait_ge(xn_ready, n + 1)
                act.activation(x_hi[:, n], xn[:, n], ACT.Copy).then_inc(hi_ready, 1)
            for n, (_, m) in enumerate(COLS):
                if n + 2 < len(COLS):
                    w.split_hi(act, n + 2, COLS[n + 2][1])
                act.wait_ge(proj_done, n + 1)
                act.wait_ge(pad_ready, 3)
                if n >= 2:
                    act.wait_ge(mix_done, n - 1)
                act.activation(raw[n % 2][0:m, 1:T + 1], k.ps[0:m, 1 + n % NB], ACT.Copy, scale=1 / SCALE).then_inc(raw_ready, 1)
                beside(n)

        @block.vector
        def _(dve):
            link = chained(dve, chain)

            def beside(n):
                if n == 4:
                    for j in range(RT):
                        dve.wait_ge(sw_ready, j + 1)
                        link(dve.tensor_scalar(lw[:, j], lw[:, j], -float(np.exp(-0.5)), None, ALU.mult))
                        dve.tensor_tensor_scan(L[:, j], k.const("chunk_start"), lw[:, j], 0.0,
                                               ALU.mult, ALU.add).then_inc(L_ready, 1)
                if n == 5:
                    dve.wait_ge(L_ready, RT)
                    dve.tensor_tensor(ex[:, :], L[:, :], lw[:, :], ALU.subtract).then_inc(ex_in, 1)
                if n == 11:
                    dve.wait_ge(kk2_done, RT)
                    dve.tensor_scalar(inv_n[:, :], ps[:, 4:8], 1e-24, None, ALU.max).then_inc(ss_ready, 1)
                for j in {13: (0, 1), 14: (2, 3)}.get(n, ()):
                    dve.wait_ge(norm_ready, 1)
                    dve.reciprocal(inv_n[:, j], inv_n[:, j])

            dve.memset(raw[0][:, 0:1], 0.0).then_inc(pad_ready, 1)
            dve.memset(raw[1][:, 0:1], 0.0).then_inc(pad_ready, 1)
            dve.memset(k.eps[:, 0:1], EPS).then_inc(pad_ready, 1)
            dve.memset(k.eps[:, 1:2], GN_EPS)
            dve.wait_ge(small_ld, 32)
            for n in range(2):
                w.split_lo(dve, n)
            dve.wait_ge(rt_ready, 1)
            dve.reciprocal(rstd, rt).then_inc(rstd_ready, 1)
            dve.wait_ge(rstd_ready, 1)
            for n in range(KT):
                dve.scalar_tensor_tensor(xn[:, n], x[:, n], k.vec("norm1_w", n), rstd,
                                         ALU.mult, ALU.mult).then_inc(xn_ready, 1)
            for n in range(KT):
                dve.wait_ge(hi_ready, n + 1)
                dve.tensor_tensor(x_lo[:, n], xn[:, n], x_hi[:, n], ALU.subtract).then_inc(lo_ready, 1)
            for n, (_, m) in enumerate(COLS):
                if n + 2 < len(COLS):
                    w.split_lo(dve, n + 2, COLS[n + 2][1])
                dve.wait_ge(raw_ready, n + 1)
                if n:
                    dve.wait_ge(mix_done, n)
                prev, cur = raw[n % 2][0:m, 0:T], raw[n % 2][0:m, 1:T + 1]
                dve.tensor_tensor(diff[0:m], prev, cur, ALU.subtract).then_inc(diff_ready, 1)
                dve.wait_ge(diff_ready, n + 1)
                dve.scalar_tensor_tensor(mix[0:m, ORDER[n]], diff[0:m], k.vec("rw_mu", ORDER[n])[0:m], cur,
                                         ALU.mult, ALU.add).then_inc(mix_done, 1)
                beside(n)

        @block.tensor
        def _(pe):
            pe.wait_ge(small_ld, 32)
            for n in range(KT):
                pe.wait_ge(sq_ready, n + 1)
                last = pe.matmul(k.ps[:, 0], k.const("ones"), sq[:, n], start=n == 0, stop=n == KT - 1)
            last.then_inc(ss_done, 1)
            for n, (_, m) in enumerate(COLS):
                if n >= NB:
                    pe.wait_ge(raw_ready, n - NB + 1)
                w.products(pe, n, k.ps[0:m, 1 + n % NB], m, x_ready=None if n else (hi_ready, lo_ready))
                if n == 2:
                    pe.wait_ge(lora_ld, 64)
                    pe.wait_ge(tw_ready, 1)
                if n == 6:
                    pe.wait_ge(sg_ready, 2)
                for j in range(RT):
                    cols, out = slice(j * P, (j + 1) * P), ps[:, 4 + j]
                    if n == 2:
                        pe.matmul(out, w2a2[0:64, cols], tw[0:64], start=True, stop=True).then_inc(z_done, 1)
                    if n == 4:
                        pe.wait_ge(sw_ready, j + 1)
                        pe.matmul(out, w2a2[64:128, cols], mix[64:128, 12], start=True, stop=True).then_inc(za_done, 1)
                    if n == 6:
                        pe.wait_ge(a_ready, j + 1)
                        pe.matmul(out, g2a[:, cols], sg[:, 0], start=True, stop=False)
                        pe.matmul(out, g2b[0:32, cols], sg[0:32, 1], start=False, stop=True).then_inc(g_done, 1)
                    if n == 10:
                        pe.wait_ge(g_ready, j + 1)
                        pe.wait_ge(kk2_ready, j + 1)
                        pe.matmul(out, k.const("head_ones"), kp[:, j], start=True, stop=True).then_inc(kk2_done, 1)


def phase_rwkv_prepare(nc, k, io):
    mix = k.view(32, [15, T])
    r, key, v = mix[:, 0:4], mix[:, 4:8], mix[:, 8:12]
    bonus = k.view(24, [RT, T])
    at, rt_ = k.view(32, [RT, T]), k.view(40, [RT, T])
    at_bd, bt_bd, kt_bd = (k.view(64 + 16 * n, [NPR, P]) for n in range(3))
    lw, L, ex, ea, a, kk, kp, inv_n = (k.view(112 + 8 * n, [RT, T]) for n in range(8))
    b = inv_n
    ps = k.ps
    gates = k.gates = Gates(k, io)
    with nc.Block() as block:
        w = Split(k, "w_gates", [k.view(64 + 4 * s, [KT, P]) for s in range(4)], 88, *k.xn_parts)
        gates.place(w, 0, 80)
        at_ready = k.sem("at_ready")
        rk_done, rk_ready, chain = map(k.sem, ("rk_done", "rk_ready", "chain"))

        @block.sync
        def _(sp):
            for m in range(GATES_IN_PREPARE):
                w.load(sp, m, gates.columns(m))

        @block.scalar
        def _(act):
            for m in range(GATES_IN_PREPARE):
                w.split_hi(act, m)
            for m in range(GATES_IN_PREPARE):
                gates.finish(act, m, m)
            act.wait_ge(at_ready, 1)
            for e in range(2):
                act.activation(diagonal(at_bd, e), by_chunk(at[HALF[e]]), ACT.Copy)

        @block.gpsimd
        def _(pool):
            pool.wait_ge(w.done, GATES_IN_PREPARE)
            for bd in (kt_bd, at_bd, bt_bd):
                if bd is bt_bd:
                    for m in range(GATES_IN_PREPARE):
                        pool.wait_ge(gates.stored[m], 16)
                for e in range(2):
                    pool.memset(diagonal(bd, e, other=True), 0.0)

        @block.vector
        def _(dve):
            link = chained(dve, chain)
            w.split_lo(dve, 0)
            for j in range(RT):
                last = dve.scalar_tensor_tensor(kk[:, j], key[:, j], k.vec("rw_k_k", j), inv_n[:, j], ALU.mult, ALU.mult)
            link(last)
            w.split_lo(dve, 1)
            link(dve.tensor_tensor(b[:, :], kk[:, :], a[:, :], ALU.mult))
            w.split_lo(dve, 2)
            for j in range(RT):
                last = dve.tensor_scalar(a[:, j], a[:, j], 1.0, k.vec("rw_k_a", j), ALU.subtract, ALU.mult)
            link(last)
            link(dve.scalar_tensor_tensor(kp[:, :], a[:, :], 1.0, key[:, :], ALU.add, ALU.mult))
            w.split_lo(dve, 3)
            for j in range(RT):
                dve.scalar_tensor_tensor(a[:, j], r[:, j], k.vec("rw_r_k", j), kp[:, j],
                                         ALU.mult, ALU.mult).then_inc(rk_ready, 1)
            link(dve.tensor_tensor(rt_[:, :], r[:, :], ea[:, :], ALU.mult))
            dve.wait_ge(rk_ready, RT)
            dve.scalar_tensor_tensor(at[:, :], kk[:, :], -1.0, ex[:, :], ALU.mult, ALU.mult).then_inc(at_ready, 1)
            for m in range(GATES_IN_PREPARE):
                dve.wait_ge(gates.stored[m], 16)
            for e in range(2):
                dve.tensor_tensor(diagonal(bt_bd, e), by_chunk(b[HALF[e]]), by_chunk(L[HALF[e]]), ALU.mult)
                dve.tensor_tensor(diagonal(kt_bd, e), by_chunk(kp[HALF[e]]), by_chunk(L[HALF[e]]), ALU.mult)
            dve.tensor_copy(k.chunk_decay[:, :, :], ea.rearrange("p j (c t) -> p j c t", t=C)[:, :, :, C - 1])
            dve.wait_ge(rk_done, RT)
            dve.tensor_tensor(bonus[:, :], ps[:, 0:4], v[:, :], ALU.mult)

        @block.tensor
        def _(pe):
            for m in range(GATES_IN_PREPARE):
                w.products(pe, m, ps[:, m])
            for j in range(RT):
                pe.wait_ge(rk_ready, j + 1)
                pe.wait_ge(gates.ready, GATES_IN_PREPARE)
                pe.matmul(ps[:, j], k.const("head_ones"), a[:, j], start=True, stop=True).then_inc(rk_done, 1)



def phase_delta_rule(nc, k, io):
    rt_, v = k.view(40, [RT, T]), k.view(48, [RT, T])
    ar = k.view(32, [2, RT, T])
    RV = k.view(56, [NPR, C])
    at_bd, bt_bd, kt_bd, v_bd, AabT_bd, Bt_bd = (k.view(64 + 16 * n, [NPR, P]) for n in range(6))
    ArbT, y, KV = k.view(160, [NPR, C]), k.view(168, [RT, T]), k.view(176, [NPR, C])
    GR = 4
    GP = NPR // GR
    AakT_bd, Kt_bd, Vt_bd = (k.view(184 + 4 * n, [GP, P]) for n in range(3))
    Vt, ArkT = k.view(48, [GP, C]), k.view(50, [GP, C])
    Tm, TmT, X, X_bd, TmT_bd = k.view(80, [NPR, C]), k.view(88, [NPR, C]), k.view(32, [NPR, C]), kt_bd, v_bd
    ST, W, R, SA, tmp = (k.view(at_kb, [RT, C]) for at_kb in (48, 49, 50, 51, 184))
    ST_bd, SA_bd = k.view(52, [RT, P]), k.view(54, [RT, P])
    ps = k.ps
    fold = k.const("fold")
    fold_wide = k.consts[:, CONST_AT["fold"][0]:CONST_AT["fold"][0] + 2 * C]

    def mask(name, rows, n):
        m = k.const(name)[rows]
        return m.unsqueeze(1).to_broadcast([m.shape[0], n, C])

    def group(x, g):
        return x[:, g * GP:(g + 1) * GP]

    def bank(n, rows=slice(0, P), cols=GP * C):
        return ps[rows, n, 0:cols].rearrange("p (n t) -> p n t", t=C)

    def wide_product(pe, out, stationary, moving, n, q, last=RT - 1, stop=True):
        if q == last:
            return pe.matmul(ps[:, out, q * C:(q + 1) * C], stationary, moving[:, n], start=True, stop=stop)
        return pe.matmul(ps[:, out, q * C:(q + 2) * C], stationary, moving[:, n:n + 2].rearrange("p n t -> p (n t)"),
                         start=True, stop=stop)

    def group_products(pe, out, stationary, moving, at=0):
        for q in range(GP):
            last = wide_product(pe, out, stationary[:, at + q], moving, at + q, q, GP - 1)
        return last

    KINDS = [("k0", "dve"), ("V", "act"), ("k1", "dve"), ("K", "act"), ("b0", "dve"), ("B", "act"),
             ("b1", "dve"), ("RV", "dve"), ("KV", "act"), ("YV", "act")]
    units = [(name, by, g) for g in range(GR) for name, by in KINDS]

    def done(by, name, g):
        return sum(b == by for _, b, _ in units[:units.index((name, by, g)) + 1])

    LV = len(LEVELS) - 1
    NX = LV * GR
    with nc.Block() as block:
        zero_ready, zero2_ready, v_ready, product_done, dve_out, act_out = map(
            k.sem, ("zero_ready", "zero2_ready", "v_ready", "product_done", "dve_out", "act_out"))
        first_in, first_ready, first_bd, first_done, first_out = map(k.sem, ("first_in", "first_ready", "first_bd", "first_done", "first_out"))
        x_done, x_out, xb_out, t_done, t_out, tt_done, tt_out, tb_out = map(
            k.sem, ("x_done", "x_out", "xb_out", "t_done", "t_out", "tt_done", "tt_out", "tb_out"))
        r_done, r_out, sa_done, sa_out, sab_out, s_done, s_in, s_out, stb_out, w_out, y_done, y_out = map(
            k.sem, ("r_done", "r_out", "sa_done", "sa_out", "sab_out", "s_done", "s_in", "s_out", "stb_out", "w_out", "y_done", "y_out"))

        @block.gpsimd
        def _(pool):
            for bd in (v_bd, Bt_bd, AabT_bd):
                for e in range(2):
                    last = pool.memset(diagonal(bd, e, other=True), 0.0)
                last.then_inc(zero_ready, 1)
            pool.wait_ge(v_ready, 1)
            for bd in (ST_bd, SA_bd):
                for e in range(2):
                    last = pool.memset(diagonal(bd, e, other=True), 0.0)
            last.then_inc(zero_ready, 1)

        @block.tensor
        def _(pe):
            transposed = {"V": v_bd, "K": kt_bd, "B": bt_bd}
            inner = {"RV": (AakT_bd, Vt), "KV": (Kt_bd, Vt), "YV": (Vt_bd, ArkT)}
            for u, (name, _, g) in enumerate(units):
                if u >= 8:
                    before = units[u - 8]
                    pe.wait_ge(dve_out if before[1] == "dve" else act_out, done(before[1], before[0], before[2]))
                if name == "V" and g == 0:
                    pe.wait_ge(v_ready, 1)
                    pe.wait_ge(zero_ready, 1)
                if name == "RV":
                    pe.wait_ge(dve_out, done("dve", "k1", g))
                    pe.wait_ge(act_out, done("act", "V", g))
                    pe.wait_ge(zero2_ready, 1)
                if name == "KV":
                    pe.wait_ge(act_out, done("act", "K", g))
                if name == "YV":
                    pe.wait_ge(dve_out, done("dve", "k1", g))
                if name in inner:
                    last = group_products(pe, u % 8, *inner[name])
                for q in range(GP) if name in transposed else ():
                    n = C if q == GP - 1 else 2 * C
                    last = pe.matmul(ps[:, u % 8, q * C:q * C + n], transposed[name][:, g * GP + q], fold_wide[:, 0:n],
                                     start=True, stop=True)
                for q in range(GP // 2) if name[0] in "kb" else ():
                    n = g * GP + int(name[1]) * GP // 2 + q
                    c, j = divmod(n, RT)
                    last = pe.matmul(ps[:, u % 8, q * 2 * C:(q + 1) * 2 * C], (kt_bd if name[0] == "k" else bt_bd)[:, n],
                                     ar[:, :, j, c * C:(c + 1) * C], start=True, stop=True)
                last.then_inc(product_done, 1)
            pe.wait_ge(act_out, done("act", "YV", GR - 1))
            pe.wait_ge(dve_out, done("dve", "RV", GR - 1))
            for g in range(GR):
                pe.wait_ge(first_bd, g + 1)
                for q in range(GP):
                    last = pe.matmul(bank(g)[:, q], TmT_bd[:, g * GP + q], fold, start=True, stop=True)
                last.then_inc(first_done, 1)
            pe.wait_ge(zero_ready, 4)
            for n in range(NX + 2):
                if n < NX:
                    g = n % GR
                    if n < GR:
                        pe.wait_ge(first_out, GR)
                    else:
                        pe.wait_ge(t_out, n - GR + 1)
                    if n >= 2:
                        pe.wait_ge(x_out, n - 1)
                    group_products(pe, n % 2, AabT_bd, Tm, g * GP).then_inc(x_done, 1)
                m = n - 1
                if 0 <= m < NX - GR:
                    g = m % GR
                    pe.wait_ge(x_out, m + 1)
                    if m >= GR:
                        pe.wait_ge(tb_out, m - GR + 1)
                    if m >= 2:
                        pe.wait_ge(t_out, m - 1)
                    group_products(pe, 2 + m % 2, TmT_bd, X, g * GP).then_inc(t_done, 1)
                m = n - 2
                if m >= 0:
                    g = m % GR
                    pe.wait_ge(xb_out, m + 1)
                    if m >= GR:
                        pe.wait_ge(tt_out, m - GR + 1)
                    if m >= 2:
                        pe.wait_ge(tt_out, m - 1)
                    group_products(pe, 4 + m % 2, X_bd, TmT, g * GP).then_inc(tt_done, 1)
            pe.wait_ge(tb_out, NX)
            for c in range(NCH):
                if c:
                    pe.wait_ge(s_out, c)
                    for j in range(RT):
                        last = wide_product(pe, 0, at_bd[:, c * RT + j], ST, j, j)
                    last.then_inc(r_done, 1)
                    pe.wait_ge(r_out, c)
                for j in range(RT):
                    last = wide_product(pe, 1, TmT_bd[:, c * RT + j], R if c else RV, j, j)
                last.then_inc(sa_done, 1)
                pe.wait_ge(sa_out, c + 1)
                if c < NCH - 1:
                    for j in range(RT):
                        last = wide_product(pe, 2, Bt_bd[:, c * RT + j], SA, j, j)
                    last.then_inc(s_done, 1)
                pe.wait_ge(sab_out, c + 1)
                if c:
                    pe.wait_ge(stb_out, c)
                if c >= 2:
                    pe.wait_ge(y_out, c - 1)
                for j in range(RT):
                    last = wide_product(pe, 6 + c % 2, SA_bd[:, j], ArbT, c * RT + j, j, stop=not c)
                    if c:
                        last = pe.matmul(bank(6 + c % 2)[:, j], ST_bd[:, j], rt_[:, j, c * C:(c + 1) * C], start=False, stop=True)
                last.then_inc(y_done, 1)

        @block.scalar
        def _(act):
            for e in range(2):
                last = act.activation(diagonal(v_bd, e), by_chunk(v[HALF[e]]), ACT.Copy)
            last.then_inc(v_ready, 1)
            act.wait_ge(v_ready, 1)
            act.wait_ge(zero2_ready, 1)
            for u, (name, by, g) in enumerate(units):
                if by != "act":
                    continue
                act.wait_ge(product_done, u + 1)
                if name == "V":
                    if g:
                        act.wait_ge(product_done, units.index(("YV", "act", g - 1)) + 1)
                    act.activation(Vt, bank(u % 8), ACT.Copy)
                if name in ("V", "K", "B"):
                    dst = {"V": Vt_bd, "K": Kt_bd, "B": group(Bt_bd, g)}[name]
                    for e in range(2):
                        last = act.activation(diagonal(dst, e), bank(u % 8, HALF[e]), ACT.Copy)
                elif name == "KV":
                    last = act.activation(group(KV, g), bank(u % 8), ACT.Copy)
                else:
                    per = GP // RT
                    last = act.activation(by_chunk(y)[:, g * per:(g + 1) * per],
                                          ps[:, u % 8].rearrange("p (c j t) -> p c j t", j=RT, t=C), ACT.Copy)
                last.then_inc(act_out, 1)
            for g in range(GR):
                act.wait_ge(first_ready, g + 1)
                for e in range(2):
                    last = act.activation(diagonal(group(TmT_bd, g), e), group(TmT, g)[HALF[e]], ACT.Copy)
                last.then_inc(first_bd, 1)
            for g in range(GR):
                act.wait_ge(first_done, g + 1)
                act.activation(group(Tm, g), bank(g), ACT.Copy).then_inc(first_out, 1)
            for n in range(NX + 2):
                if n < NX:
                    act.wait_ge(x_out, n + 1)
                    if n >= GR:
                        act.wait_ge(tt_done, n - GR + 1)
                    for e in range(2):
                        last = act.activation(diagonal(group(X_bd, n % GR), e), group(X, n % GR)[HALF[e]], ACT.Copy)
                    last.then_inc(xb_out, 1)
                m = n - 2
                if m >= 0:
                    act.wait_ge(tt_out, m + 1)
                    for e in range(2):
                        last = act.activation(diagonal(group(TmT_bd, m % GR), e), group(TmT, m % GR)[HALF[e]], ACT.Copy)
                    last.then_inc(tb_out, 1)
            for c in range(NCH):
                act.wait_ge(sa_out, c + 1)
                if c:
                    act.wait_ge(y_done, c)
                for e in range(2):
                    last = act.activation(diagonal(SA_bd, e), SA[HALF[e]], ACT.Copy)
                last.then_inc(sab_out, 1)
                if c < NCH - 1:
                    act.wait_ge(s_out, c + 1)
                    act.wait_ge(y_done, c + 1)
                    for e in range(2):
                        last = act.activation(diagonal(ST_bd, e), ST[HALF[e]], ACT.Copy)
                    last.then_inc(stb_out, 1)

        @block.vector
        def _(dve):
            for bd in (AakT_bd, Kt_bd, Vt_bd):
                for e in range(2):
                    last = dve.memset(diagonal(bd, e, other=True), 0.0)
            last.then_inc(zero2_ready, 1)
            dve.wait_ge(v_ready, 1)
            for u, (name, by, g) in enumerate(units):
                if by != "dve":
                    continue
                dve.wait_ge(product_done, u + 1)
                if name == "k0" and g:
                    dve.wait_ge(product_done, units.index(("YV", "act", g - 1)) + 1)
                if name[0] in "kb":
                    half = slice(int(name[1]) * GP // 2, (int(name[1]) + 1) * GP // 2)
                    A_bd, A_r = (AakT_bd, ArkT) if name[0] == "k" else (group(AabT_bd, g), group(ArbT, g))
                    both = ps[:, u % 8].rearrange("p (n x t) -> p n x t", x=2, t=C)
                    for e in range(2):
                        dve.tensor_tensor(diagonal(A_bd[:, half], e), both[HALF[e], :, 0], mask("strict", HALF[e], GP // 2), ALU.mult)
                    last = dve.tensor_tensor(A_r[:, half], both[:, :, 1], mask("upto", slice(0, P), GP // 2), ALU.mult)
                else:
                    last = dve.tensor_copy(group(RV, g), bank(u % 8))
                last.then_inc(dve_out, 1)
            dve.wait_ge(product_done, len(units))
            dve.wait_ge(dve_out, done("dve", "RV", GR - 1))
            for g in range(GR):
                for e in range(2):
                    last = dve.tensor_tensor(group(TmT, g)[HALF[e]], diagonal(group(AabT_bd, g), e), mask("level1_t", HALF[e], GP), ALU.mult)
                last.then_inc(first_in, 1)
            for g in range(GR):
                dve.wait_ge(first_in, g + 1)
                dve.tensor_tensor(group(TmT, g), group(TmT, g), mask("fold", slice(0, P), GP), ALU.add).then_inc(first_ready, 1)
            for n in range(NX + 2):
                if n < NX:
                    dve.wait_ge(x_done, n + 1)
                    if n >= GR:
                        dve.wait_ge(t_done, min(n - GR + 1, NX - GR))
                        dve.wait_ge(xb_out, n - GR + 1)
                    dve.tensor_tensor(group(X, n % GR), bank(n % 2), mask(f"level{LEVELS[n // GR + 1]}", slice(0, P), GP),
                                      ALU.mult).then_inc(x_out, 1)
                m = n - 1
                if 0 <= m < NX - GR:
                    dve.wait_ge(t_done, m + 1)
                    if m >= GR:
                        dve.wait_ge(t_out, m - GR + 1)
                    dve.tensor_tensor(group(Tm, m % GR), group(Tm, m % GR), bank(2 + m % 2), ALU.add).then_inc(t_out, 1)
                m = n - 2
                if m >= 0:
                    dve.wait_ge(tt_done, m + 1)
                    if m >= GR:
                        dve.wait_ge(tb_out, m - GR + 1)
                        dve.wait_ge(tt_out, m - GR + 1)
                    else:
                        dve.wait_ge(first_ready, m + 1)
                    dve.tensor_tensor(group(TmT, m % GR), group(TmT, m % GR), bank(4 + m % 2), ALU.add).then_inc(tt_out, 1)
            for c in range(NCH):
                now = slice(c * RT, (c + 1) * RT)
                if c:
                    dve.wait_ge(r_done, c)
                    dve.tensor_tensor(R, bank(0, cols=RT * C), RV[:, now], ALU.add).then_inc(r_out, 1)
                dve.wait_ge(sa_done, c + 1)
                if c:
                    dve.wait_ge(s_done, c)
                    dve.wait_ge(sab_out, c)
                dve.tensor_copy(SA, bank(1, cols=RT * C)).then_inc(sa_out, 1)
                if c < NCH - 1:
                    dve.wait_ge(s_done, c + 1)
                    if c:
                        dve.wait_ge(w_out, c)
                        dve.wait_ge(s_out, c)
                    dve.tensor_tensor(tmp, bank(2, cols=RT * C), W if c else KV[:, now], ALU.add).then_inc(s_in, 1)
                    dve.wait_ge(s_in, c + 1)
                    if c:
                        dve.wait_ge(stb_out, c)
                    dve.tensor_tensor(ST, tmp, k.chunk_decay[:, :, c:c + 1].to_broadcast([P, RT, C]), ALU.mult).then_inc(s_out, 1)
                    dve.wait_ge(s_out, c + 1)
                    dve.tensor_tensor(W, ST, KV[:, (c + 1) * RT:(c + 2) * RT], ALU.add).then_inc(w_out, 1)
                dve.wait_ge(y_done, c + 1)
                own = y[:, :, c * C:(c + 1) * C]
                dve.tensor_tensor(own, own, bank(6 + c % 2, cols=RT * C), ALU.add).then_inc(y_out, 1)


def rwkv_out(block, k, io, early_vector):
    g, bonus, y = k.view(16, [RT, T]), k.view(24, [RT, T]), k.view(168, [RT, T])
    d, sq, s, yg = k.view(122, [RT, T]), k.view(152, [RT, T]), k.view(160, [RT, T]), g
    ps = k.ps
    mean_done, dev_ready, dev2_ready, var_done, sd_ready, gn_chain = map(
        k.sem, ("mean_done", "dev_ready", "dev2_ready", "var_done", "sd_ready", "gn_chain"))

    @block.tensor
    def _(pe):
        for j in range(RT):
            pe.matmul(ps[:, j], k.const("head_ones"), y[:, j], start=True, stop=True).then_inc(mean_done, 1)
        for j in range(RT):
            pe.wait_ge(dev2_ready, j + 1)
            pe.matmul(ps[:, 4 + j], k.const("head_ones"), sq[:, j], start=True, stop=True).then_inc(var_done, 1)

    @block.scalar
    def _(act):
        for j in range(RT):
            act.wait_ge(dev_ready, j + 1)
            act.activation(sq[:, j], d[:, j], ACT.Square).then_inc(dev2_ready, 1)
        for j in range(RT):
            act.wait_ge(var_done, j + 1)
            act.activation(s[:, j], ps[:, 4 + j], ACT.Sqrt, scale=1.0 / 64, bias=k.eps[:, 1:2]).then_inc(sd_ready, 1)

    @block.vector
    def _(dve):
        link = chained(dve, gn_chain)
        for j in range(RT):
            dve.wait_ge(mean_done, j + 1)
            dve.scalar_tensor_tensor(d[:, j], ps[:, j], -1.0 / 64, y[:, j], ALU.mult, ALU.add).then_inc(dev_ready, 1)
        early_vector(dve)
        dve.wait_ge(sd_ready, RT)
        dve.wait_ge(dev_ready, RT)
        link(dve.reciprocal(s[:, :], s[:, :]))
        link(dve.tensor_tensor(d[:, :], d[:, :], s[:, :], ALU.mult))
        for j in range(RT):
            last = dve.tensor_scalar(d[:, j], d[:, j], k.vec("rw_ln_w", j), k.vec("rw_ln_b", j), ALU.mult, ALU.add)
        link(last)
        link(dve.tensor_tensor(d[:, :], d[:, :], bonus[:, :], ALU.add))
        link(dve.tensor_tensor(yg[:, :], d[:, :], g[:, :], ALU.mult))
    return dev_ready, sd_ready


def phase_rwkv_out_and_mla_project(nc, k, io):
    down = k.view(48, [5, T])
    sq = k.view(58, [5, T])
    rstd = k.view(68, [2, T])
    w_uq, w_ukv = k.view(72, [3, HEADS * QK]), k.view(81, [2, HEADS * 2 * NOPE])
    Q, K, V = k.view(90, [HEADS, T]), k.view(106, [HEADS, T]), k.view(122, [TT, HEADS * NOPE])
    cos, sin = k.view(130, [T]), k.view(132, [T])
    turned = k.view(134, [T])
    hsq, hsd = k.view(136, [2, T]), k.view(140, [2, T])
    pos, ang, turns, red = k.view(144, [T], I32), k.view(146, [T]), k.view(148, [T]), k.view(150, [T])
    w_in = io["w_in"].rearrange("(k p) n -> p k n", p=P)
    cols = [(Q_COL + n * P, P) for n in range(5)] + [(KPE_COL, ROPE)]
    rope = slice(NOPE, QK)
    items = [("k", 0)] + [("q", h) for h in range(HEADS)] + [("k", h) for h in range(1, HEADS)]
    rows = [QK if kind == "q" or h == 0 else NOPE for kind, h in items]
    roped = [i for i in range(16) if rows[i] == QK]
    ps = k.ps
    G_MLA = 2 * KT - GATES_IN_PREPARE
    TWO_PI = 2 * np.pi
    C1 = 6.28125
    C2 = float(np.float32(np.round((TWO_PI - C1) * 2 ** 20) / 2 ** 20))
    C3 = float(TWO_PI - C1 - C2)
    MAGIC = 1.5 * 2 ** 23
    gates = k.gates
    with nc.Block() as block:
        w = Split(k, "mla_w", [k.view(176 + 4 * s, [KT, P]) for s in range(4)], 32, *k.xn_parts)
        gates.place(w, len(cols) - GATES_IN_PREPARE, 152)
        m_of = [m for _, m in cols] + [P] * G_MLA
        dev_ready, sd_ready = rwkv_out(block, k, io, lambda dve: [w.split_lo(dve, n) for n in range(4)])
        up_ld, pos_ld, down_ready, dsq_ready, dss_done, dsd_ready, down_normed = map(
            k.sem, ("up_ld", "pos_ld", "down_ready", "dsq_ready", "dss_done", "dsd_ready", "down_normed"))
        ang_ready, sin_ready, cos_in, head_done, head_ready, hsq_ready, hss_done, hsd_ready, head_normed = map(
            k.sem, ("ang_ready", "sin_ready", "cos_in", "head_done", "head_ready", "hsq_ready", "hss_done", "hsd_ready", "head_normed"))
        swap_done, roped_ready, mla_chain, v_done, v_ready, kpe_copied = map(
            k.sem, ("swap_done", "roped_ready", "mla_chain", "v_done", "v_ready", "kpe_copied"))

        @block.sync
        def _(sp):
            sp.dma_start(pos[0:QK], io["positions"].to_broadcast([QK, T])).then_inc(pos_ld, 16)
            for n, (col, m) in enumerate(cols):
                w.load(sp, n, w_in[:, :, col:col + m])
                if n == 3:
                    sp.dma_start(w_uq, io["mla_w_uq"].rearrange("(k p) n -> p k n", p=P)).then_inc(up_ld, 16)
                    sp.dma_start(w_ukv, io["mla_w_ukv"].rearrange("(k p) n -> p k n", p=P)).then_inc(up_ld, 16)
            for m in range(GATES_IN_PREPARE, 2 * KT):
                w.load(sp, gates.tile(m), gates.columns(m))

        @block.tensor
        def _(pe):
            pe.wait_ge(dev_ready, RT)
            pe.wait_ge(sd_ready, RT)
            for n in range(5):
                w.products(pe, n, ps[:, n])
            for n in range(5):
                pe.wait_ge(dsq_ready, n + 1)
                last = pe.matmul(ps[:, 5 + n // 3], k.const("ones"), sq[:, n], start=n in (0, 3), stop=n in (2, 4))
                if n in (2, 4):
                    last.then_inc(dss_done, 1)
            pe.wait_ge(up_ld, 32)

            def main(i):
                kind, h = items[i]
                if i == 0:
                    pe.wait_ge(down_normed, 5)
                    pe.wait_ge(down_ready, 5)
                if i >= 2:
                    pe.wait_ge(head_ready, i - 1)
                out = ps[:, i % 2]
                if kind == "q":
                    for f in range(3):
                        last = pe.matmul(out[0:QK], w_uq[:, f, h * QK:(h + 1) * QK], down[:, f], start=f == 0, stop=f == 2)
                else:
                    if h == 0:
                        w.products(pe, 5, out[rope], ROPE)
                    for f in range(2):
                        last = pe.matmul(out[0:NOPE], w_ukv[:, f, h * P:h * P + NOPE], down[:, 3 + f], start=f == 0, stop=f == 1)
                last.then_inc(head_done, 1)

            def squares(i):
                pe.wait_ge(hsq_ready, i + 1)
                if i >= 2:
                    pe.wait_ge(hsd_ready, i - 1)
                m = rows[i]
                pe.matmul(ps[0:m, 2 + i % 2], k.const("qk_ones")[0:m, 0:m], hsq[0:m, i % 2], start=True, stop=True).then_inc(hss_done, 1)

            def swap(i):
                kind, h = items[i]
                n = roped.index(i)
                pe.wait_ge(head_normed, i + 1)
                if n >= 2:
                    pe.wait_ge(roped_ready, n - 1)
                pe.matmul(ps[0:QK, 4 + n % 2], k.const("rope_swap")[0:QK], (Q if kind == "q" else K)[0:QK, h],
                          start=True, stop=True).then_inc(swap_done, 1)

            pe.wait_ge(dsd_ready, 2)
            for i in range(18):
                if i < 16:
                    main(i)
                if 1 <= i <= 16:
                    squares(i - 1)
                if i >= 2 and i - 2 in roped:
                    swap(i - 2)
                if i < G_MLA:
                    m = GATES_IN_PREPARE + i
                    if i >= 2:
                        pe.wait_ge(gates.ready, m - 1)
                    w.products(pe, gates.tile(m), ps[:, 6 + i % 2])
            for t in range(TT):
                if t >= 2:
                    pe.wait_ge(v_ready, t - 1)
                else:
                    pe.wait_ge(gates.ready, 2 * KT)
                for f in range(2):
                    last = pe.matmul(ps[:, 6 + t % 2], down[:, 3 + f, t * P:(t + 1) * P],
                                     w_ukv[:, f].rearrange("p (h c) -> p h c", h=HEADS)[:, :, NOPE:], start=f == 0, stop=f == 1)
                last.then_inc(v_done, 1)

        @block.scalar
        def _(act):
            for n in range(4):
                w.split_hi(act, n, m_of[n])
            for n in range(5):
                act.wait_ge(w.done, n + 1)
                act.activation(sq[:, n], ps[:, n], ACT.Square, scale=1 / SCALE).then_inc(dsq_ready, 1)
                act.activation(down[:, n], ps[:, n], ACT.Copy, scale=1 / SCALE).then_inc(down_ready, 1)
                if n < 4:
                    w.split_hi(act, n + 4, m_of[n + 4])
            for n in range(2):
                act.wait_ge(dss_done, n + 1)
                act.activation(rstd[:, n], ps[:, 5 + n], ACT.Sqrt, scale=1.0 / (Q_LORA, KV_LORA)[n],
                               bias=k.eps[:, 0:1]).then_inc(dsd_ready, 1)
            act.wait_ge(ang_ready, 1)
            act.activation(sin[0:QK], sin[0:QK], ACT.Sin).then_inc(sin_ready, 1)
            act.wait_ge(cos_in, 1)
            act.activation(cos[0:QK], cos[0:QK], ACT.Sin).then_inc(sin_ready, 1)
            for i in range(17):
                if i < 16:
                    kind, h = items[i]
                    m = rows[i]
                    act.wait_ge(head_done, i + 1)
                    if i >= 2:
                        act.wait_ge(hss_done, i - 1)
                    parts = [(slice(0, m), 1.0)] if i else [(slice(0, NOPE), 1.0), (rope, 1 / SCALE)]
                    for at, scale in parts:
                        last = act.activation(hsq[at, i % 2], ps[at, i % 2], ACT.Square, scale=scale)
                    last.then_inc(hsq_ready, 1)
                    for at, scale in parts:
                        last = act.activation((Q if kind == "q" else K)[at, h], ps[at, i % 2], ACT.Copy, scale=scale)
                    last.then_inc(head_ready, 1)
                if i:
                    m = rows[i - 1]
                    act.wait_ge(hss_done, i)
                    if i >= 3:
                        act.wait_ge(head_normed, i - 2)
                    act.activation(hsd[0:m, (i - 1) % 2], ps[0:m, 2 + (i - 1) % 2], ACT.Sqrt, bias=k.eps[0:m, 0:1]).then_inc(hsd_ready, 1)
                if 1 <= i <= G_MLA:
                    gates.finish(act, GATES_IN_PREPARE + i - 1, 6 + (i - 1) % 2)
                if len(cols) + 2 + i < len(m_of):
                    w.split_hi(act, len(cols) + 2 + i)
            for s in range(4):
                act.wait_ge(gates.stored[s], 2 * KT // 4 * 16)
            for t in range(TT):
                act.wait_ge(v_done, t + 1)
                act.activation(V[:, t], ps[:, 6 + t % 2], ACT.Copy).then_inc(v_ready, 1)

        @block.vector
        def _(dve):
            link = chained(dve, mla_chain)
            for n in range(4, 6):
                w.split_lo(dve, n, m_of[n])
            dve.wait_ge(pos_ld, 16)
            link(dve.tensor_copy(ang[0:QK], pos[0:QK]))
            link(dve.tensor_scalar(ang[0:QK], ang[0:QK], k.vec("inv_freq")[0:QK], None, ALU.mult))
            for table, quarter, ready in ((sin, 0.0, ang_ready), (cos, 0.25, cos_in)):
                link(dve.tensor_scalar(turns[0:QK], ang[0:QK], 1 / TWO_PI, quarter, ALU.mult, ALU.add))
                link(dve.tensor_scalar(turns[0:QK], turns[0:QK], MAGIC, None, ALU.add))
                link(dve.tensor_scalar(turns[0:QK], turns[0:QK], MAGIC, None, ALU.subtract))
                link(dve.scalar_tensor_tensor(red[0:QK], turns[0:QK], -C1, ang[0:QK], ALU.mult, ALU.add))
                link(dve.scalar_tensor_tensor(red[0:QK], turns[0:QK], -C2, red[0:QK], ALU.mult, ALU.add))
                link(dve.scalar_tensor_tensor(red[0:QK], turns[0:QK], -C3, red[0:QK], ALU.mult, ALU.add))
                link(dve.tensor_scalar(red[0:QK], red[0:QK], quarter * TWO_PI, None, ALU.add))
                dve.tensor_scalar(table[0:QK], red[0:QK], float(np.float32(3.1415925)), -float(np.float32(3.1415925)),
                                  ALU.min, ALU.max).then_inc(ready, 1)
                dve.wait_ge(ready, 1)
            for n in range(6, 8):
                w.split_lo(dve, n)
            for n in range(2):
                dve.wait_ge(dsd_ready, n + 1)
                link(dve.reciprocal(rstd[:, n], rstd[:, n]))
                for f in ((0, 1, 2), (3, 4))[n]:
                    dve.wait_ge(down_ready, f + 1)
                    dve.scalar_tensor_tensor(down[:, f], down[:, f], k.vec("mla_q_norm_w", f), rstd[:, n],
                                             ALU.mult, ALU.mult).then_inc(down_normed, 1)
            dve.wait_ge(sin_ready, 2)

            def turn(i):
                kind, h = items[i]
                n = roped.index(i)
                x = (Q if kind == "q" else K)[rope, h]
                dve.wait_ge(swap_done, n + 1)
                link(dve.tensor_tensor(turned[rope], ps[rope, 4 + n % 2], sin[rope], ALU.mult))
                link(dve.tensor_tensor(x, x, cos[rope], ALU.mult))
                dve.tensor_tensor(x, x, turned[rope], ALU.add).then_inc(roped_ready, 1)
                dve.wait_ge(roped_ready, n + 1)

            for i in range(17):
                if i < 16:
                    kind, h = items[i]
                    m = rows[i]
                    x = (Q if kind == "q" else K)[0:m, h]
                    dve.wait_ge(hsd_ready, i + 1)
                    dve.wait_ge(head_ready, i + 1)
                    link(dve.reciprocal(hsd[0:m, i % 2], hsd[0:m, i % 2]))
                    dve.scalar_tensor_tensor(x, x, k.vec("qn_w" if kind == "q" else "kn_w")[0:m], hsd[0:m, i % 2],
                                             ALU.mult, ALU.mult).then_inc(head_normed, 1)
                if i and i - 1 in roped:
                    turn(i - 1)
                if len(cols) + 2 + i < len(m_of):
                    w.split_lo(dve, len(cols) + 2 + i)

        @block.gpsimd
        def _(pool):
            pool.wait_ge(roped_ready, len(roped))
            for h in range(1, HEADS):
                pool.tensor_copy(K[rope, h], K[rope, 0]).then_inc(kpe_copied, 1)


def phase_attention_and_merge(nc, k, io):
    Q, K, V = k.view(90, [HEADS, T]), k.view(106, [HEADS, T]), k.view(122, [TT, HEADS * NOPE])
    oT = k.view(24, [RT, T])
    probs, probsT, diag = k.view(130, [2, T]), k.view(134, [2, TT, P]), k.view(138, [2, P])
    mx, nb, rs, ri = (k.view(140 + n, [32]) for n in range(4))
    scale = float(1.0 / np.sqrt(QK))
    units = [(h, q) for h in range(HEADS) for q in range(TT)]
    yg, hT, mixed = k.view(16, [RT, T]), k.view(32, [KT, T]), k.view(48, [KT, T])
    w_a, w_b = k.view(64, [RT, D]), k.view(0, [RT, D])
    gates = k.view(152, [2 * KT, T])
    ring = [k.view(at_kb, [KT, P]) for at_kb in (184, 188, 192, 80)]
    squares, total = k.view(130, [2, T]), k.view(150, [T])
    part = lambda w: w.rearrange("(k p) n -> p k n", p=P)
    w_out = part(io["w_out"])
    PER = len(units) // KT
    ps = k.ps
    with nc.Block() as block:
        s_done, masked, max_ready, nb_ready, exp_ready, diag_ready, pt_done, pt_out, o_done, o_out, rinv_ready = map(
            k.sem, ("s_done", "masked", "max_ready", "nb_ready", "exp_ready", "diag_ready", "pt_done", "pt_out", "o_done2", "o_out", "rinv_ready"))
        ring_ld = [k.sem(f"ring_ld{s}") for s in range(4)]
        w_a_ld, w_b_ld, x_ld, gates_ld = map(k.sem, ("w_a_ld", "w_b_ld", "x_ld", "gates_ld"))
        branch_done, part_ready, mixed_ready, h_done, h_ready, squared, summed = map(
            k.sem, ("branch_done", "part_ready", "mixed_ready", "h_done", "h_ready", "squared", "summed"))

        @block.sync
        def _(sp):
            sp.dma_start(w_a, part(io["rw_w_o"])).then_inc(w_a_ld, 16)
            sp.dma_start(gates, io["gate_acts"].rearrange("m p t -> p m t")).then_inc(gates_ld, 16)
            sp.dma_start(w_b, part(io["mla_w_o"])).then_inc(w_b_ld, 16)
            for n in range(KT):
                if n == 4:
                    sp.dma_start(hT, io["xT"].rearrange("(k p) n -> p k n", p=P)).then_inc(x_ld, 16)
                if n >= 4:
                    sp.wait_ge(h_done, n - 3)
                sp.dma_start(ring[n % 4], w_out[:, :, n * P:(n + 1) * P]).then_inc(ring_ld[n % 4], 16)

        @block.tensor
        def _(pe):
            def branch(n, f, w, x):
                if f == 0 and n >= 2:
                    pe.wait_ge(part_ready, n - 1)
                d = n % KT
                last = pe.matmul(ps[:, 6 + n % 2], w[:, f, d * P:(d + 1) * P], x[:, f], start=f == 0, stop=f == RT - 1)
                if f == RT - 1:
                    last.then_inc(branch_done, 1)

            def scores(u):
                h, q = units[u]
                if u >= 2:
                    pe.wait_ge(exp_ready, u - 1)
                n = (q + 1) * P
                pe.matmul(ps[:, u % 2, 0:n], Q[0:QK, h, q * P:n], K[0:QK, h, 0:n], start=True, stop=True).then_inc(s_done, 1)

            def weighted(u):
                h, q = units[u]
                half = slice(64 * (h % 2), 64 * (h % 2) + 64)
                pe.wait_ge(diag_ready, u + 1)
                if u >= 2:
                    pe.wait_ge(pt_out, u - 1)
                for t in range(q + 1):
                    last = pe.matmul(ps[:, 2 + u % 2, t * P:(t + 1) * P], probs[:, u % 2, t * P:(t + 1) * P],
                                     diag[:, u % 2], start=True, stop=True)
                last.then_inc(pt_done, 1)

            def values(u):
                h, q = units[u]
                half = slice(64 * (h % 2), 64 * (h % 2) + 64)
                pe.wait_ge(pt_out, u + 1)
                if q == 0 and h >= 2:
                    pe.wait_ge(o_out, h - 1)
                for t in range(q + 1):
                    last = pe.matmul(ps[half, 4 + h % 2, q * P:(q + 1) * P], V[:, t, h * NOPE:(h + 1) * NOPE],
                                     probsT[:, u % 2, t], start=t == 0, stop=t == q)
                last.then_inc(o_done, 1)

            for u in range(len(units) + 2):
                if u < len(units):
                    scores(u)
                if 1 <= u <= len(units):
                    weighted(u - 1)
                if u < len(units):
                    if u == 0:
                        pe.wait_ge(w_a_ld, 16)
                    branch(u // PER, u % PER, w_a, yg)
                if u >= 2:
                    values(u - 2)
            pe.wait_ge(w_b_ld, 16)
            pe.wait_ge(o_out, HEADS)
            for n in range(KT, 2 * KT):
                for f in range(RT):
                    branch(n, f, w_b, oT)
            for n in range(KT):
                pe.wait_ge(ring_ld[n % 4], 16 * (n // 4 + 1))
                if n >= 4:
                    pe.wait_ge(h_ready, n - 3)
                for f in range(KT):
                    if n == 0:
                        pe.wait_ge(mixed_ready, f + 1)
                    last = pe.matmul(ps[:, n % 4], ring[n % 4][:, f], mixed[:, f], start=f == 0, stop=f == KT - 1)
                last.then_inc(h_done, 1)

        @block.vector
        def _(dve):
            def top(u):
                h, q = units[u]
                dve.wait_ge(s_done, u + 1)
                own = ps[:, u % 2, q * P:(q + 1) * P]
                dve.tensor_tensor(own, own, k.const("causal"), ALU.add).then_inc(masked, 1)
                dve.wait_ge(masked, u + 1)
                dve.reduce_max(mx[:, u:u + 1], ps[:, u % 2, 0:(q + 1) * P], AX.X).then_inc(max_ready, 1)
                dve.wait_ge(max_ready, u + 1)
                dve.tensor_scalar(nb[:, u:u + 1], mx[:, u:u + 1], -scale, None, ALU.mult).then_inc(nb_ready, 1)

            def bottom(u):
                dve.wait_ge(exp_ready, u + 1)
                if u >= 2:
                    dve.wait_ge(pt_done, u - 1)
                dve.reciprocal(ri[:, u:u + 1], rs[:, u:u + 1]).then_inc(rinv_ready, 1)
                dve.wait_ge(rinv_ready, u + 1)
                dve.tensor_scalar(diag[:, u % 2], k.const("ident"), ri[:, u:u + 1], None, ALU.mult).then_inc(diag_ready, 1)

            def turned(u):
                h, q = units[u]
                dve.wait_ge(pt_done, u + 1)
                if u >= 2:
                    dve.wait_ge(o_done, u - 1)
                dve.tensor_copy(probsT[:, u % 2, 0:q + 1], ps[:, 2 + u % 2, 0:(q + 1) * P].rearrange("p (t c) -> p t c", c=P)).then_inc(pt_out, 1)

            for u in range(len(units) + 1):
                if u < len(units):
                    top(u)
                    bottom(u)
                if u:
                    turned(u - 1)
                if u >= PER and u % PER == 0:
                    n = u // PER - 1
                    dve.wait_ge(gates_ld, 16)
                    dve.wait_ge(branch_done, n + 1)
                    dve.tensor_tensor(mixed[:, n], gates[:, 2 * n], ps[:, 6 + n % 2], ALU.mult).then_inc(part_ready, 1)

            def add(n):
                dve.wait_ge(part_ready, KT + n + 1)
                dve.tensor_tensor(mixed[:, n], mixed[:, n], gates[:, 2 * n + 1], ALU.add).then_inc(mixed_ready, 1)

            for n in range(KT):
                dve.wait_ge(branch_done, KT + n + 1)
                g = gates[:, 2 * n + 1]
                dve.tensor_tensor(g, g, ps[:, 6 + n % 2], ALU.mult).then_inc(part_ready, 1)
                if n:
                    add(n - 1)
            add(KT - 1)

            def sum_up(n):
                dve.wait_ge(squared, n + 1)
                if n:
                    dve.wait_ge(summed, n)
                    dve.tensor_tensor(total, total, squares[:, n % 2], ALU.add).then_inc(summed, 1)
                else:
                    dve.tensor_copy(total, squares[:, 0]).then_inc(summed, 1)

            dve.wait_ge(x_ld, 16)
            for n in range(KT):
                dve.wait_ge(h_done, n + 1)
                dve.tensor_tensor(hT[:, n], ps[:, n % 4], hT[:, n], ALU.add).then_inc(h_ready, 1)
                if n:
                    sum_up(n - 1)
            sum_up(KT - 1)

        @block.scalar
        def _(act):
            def copy_out(h):
                half = slice(64 * (h % 2), 64 * (h % 2) + 64)
                act.wait_ge(o_done, TT * (h + 1))
                act.activation(oT[half, h // 2], ps[half, 4 + h % 2], ACT.Copy).then_inc(o_out, 1)

            for u, (h, q) in enumerate(units):
                act.wait_ge(nb_ready, u + 1)
                if u >= 2:
                    act.wait_ge(pt_done, u - 1)
                n = (q + 1) * P
                act.activation(probs[:, u % 2, 0:n], ps[:, u % 2, 0:n], ACT.Exp, scale=scale, bias=nb[:, u:u + 1],
                               accum_out=rs[:, u:u + 1]).then_inc(exp_ready, 1)
                if q == 1 and h:
                    copy_out(h - 1)
            copy_out(HEADS - 1)
            for n in range(KT):
                act.wait_ge(h_ready, n + 1)
                if n >= 2:
                    act.wait_ge(summed, n - 1)
                act.activation(squares[:, n % 2], hT[:, n], ACT.Square).then_inc(squared, 1)


def route_scores(block, k, io):
    hT, hn, h_hi, h_lo = k.view(32, [KT, T]), k.view(0, [KT, T]), k.view(16, [KT, T], F16), k.view(24, [KT, T], F16)
    ring = [k.view(48 + 4 * s, [KT, P]) for s in range(4)]
    qT = k.view(64, [2, T])
    subk = k.view(68, [2 * PH, NK])
    total, rstd = k.view(150, [T]), k.view(108, [T])
    sc = k.view(76, [TT, 2 * PH, NK])
    top, top_i = k.top, k.top_i
    rest = k.view(110, [2, NK])
    w_q = io["peer_w_query"].rearrange("(k p) n -> p k n", p=P)
    ps = k.ps
    query = Split(k, "w_q", ring, 152, h_hi, h_lo)
    subk_ld, ss_done, rt_ready, rstd_ready, hn_ready, hi_ready, lo_ready = map(
        k.sem, ("subk_ld", "ss_done", "rt_ready", "rstd_ready", "hn_ready", "hi_ready", "lo_ready"))
    q_done = query.done
    q_out, sc_done, sc_out, top_step = map(k.sem, ("q_out", "sc_done", "sc_out", "top_step"))

    @block.sync
    def _(sp):
        sp.dma_start(subk, io["sub_keysT"]).then_inc(subk_ld, 16)
        for n in range(2 * PH):
            query.load(sp, n, w_q[:, :, n * P:(n + 1) * P])

    @block.tensor
    def _(pe):
        pe.matmul(ps[:, 0], k.const("ones"), total, start=True, stop=True).then_inc(ss_done, 1)

        def scores(n):
            pe.wait_ge(q_out, n + 1)
            if n >= 2:
                pe.wait_ge(sc_out, n - 1)
            for t in range(TT):
                last = pe.matmul(ps[:, 3 + n % 2, t * P:(t + 1) * P], qT[:, n % 2, t * P:(t + 1) * P], subk[:, n],
                                 start=True, stop=True)
            last.then_inc(sc_done, 1)

        pe.wait_ge(subk_ld, 16)
        for n in range(2 * PH):
            if n >= 2:
                pe.wait_ge(q_out, n - 1)
            query.products(pe, n, ps[:, 1 + n % 2], x_ready=None if n else (hi_ready, lo_ready))
            if n:
                scores(n - 1)
        scores(2 * PH - 1)

    @block.scalar
    def _(act):
        act.wait_ge(ss_done, 1)
        act.activation(rstd, ps[:, 0], ACT.Sqrt, scale=1.0 / D, bias=k.eps[:, 0:1]).then_inc(rt_ready, 1)
        query.split_hi(act, 0)
        query.split_hi(act, 1)
        for n in range(KT):
            act.wait_ge(hn_ready, n + 1)
            act.activation(h_hi[:, n], hn[:, n], ACT.Copy).then_inc(hi_ready, 1)


        def score_copy(n):
            act.wait_ge(sc_done, n + 1)
            act.activation(sc[:, :, n], ps[:, 3 + n % 2].rearrange("p (t n) -> p t n", t=TT), ACT.Copy).then_inc(sc_out, 1)

        for n in range(2 * PH):
            if n + 2 < 2 * PH:
                query.split_hi(act, n + 2)
            act.wait_ge(q_done, n + 1)
            if n >= 2:
                act.wait_ge(sc_done, n - 1)
            act.activation(qT[:, n % 2], ps[:, 1 + n % 2], ACT.Copy, scale=1 / SCALE).then_inc(q_out, 1)
            if n:
                score_copy(n - 1)
        score_copy(2 * PH - 1)

    @block.vector
    def _(dve):
        dve.wait_ge(rt_ready, 1)
        dve.reciprocal(rstd, rstd).then_inc(rstd_ready, 1)
        dve.wait_ge(rstd_ready, 1)
        for n in range(KT):
            dve.scalar_tensor_tensor(hn[:, n], hT[:, n], k.vec("norm2_w", n), rstd, ALU.mult, ALU.mult).then_inc(hn_ready, 1)
        for n in range(KT):
            dve.wait_ge(hi_ready, n + 1)
            dve.tensor_tensor(h_lo[:, n], hn[:, n], h_hi[:, n], ALU.subtract).then_inc(lo_ready, 1)
            if n in (0, 4):
                query.split_lo(dve, n // 4)
        steps = 0
        for n in range(2 * PH):
            if n + 2 < 2 * PH:
                query.split_lo(dve, n + 2)
            dve.wait_ge(sc_out, n + 1)
            for t in range(0, TT, 2):
                two = [(sc[:, t + b, n], top[:, t + b, n], top_i[:, t + b, n], rest[:, b]) for b in range(2)]
                if steps:
                    dve.wait_ge(top_step, steps)
                for stage in (lambda s, v, i, r: dve.max(v[:, 0:8], s),
                              lambda s, v, i, r: dve.max_index(i[:, 0:8], v[:, 0:8], s),
                              lambda s, v, i, r: dve.match_replace(r, v[:, 0:8], s, -3.0e38),
                              lambda s, v, i, r: dve.max(v[:, 8:16], r),
                              lambda s, v, i, r: dve.max_index(i[:, 8:16], v[:, 8:16], r)):
                    for b in range(2):
                        stage(*two[b]).then_inc(top_step, 1)
                    steps += 2
                    dve.wait_ge(top_step, steps)


AHEAD_PICKS, AHEAD_PER_ROUND = 24, 8


class Ahead:

    def __init__(self, k, io):
        self.k, self.uT, self.acts = k, io["uT"], io["acts"]
        self.hn, self.h_hi, self.h_lo = k.view(0, [KT, T]), k.view(16, [KT, T], F16), k.view(24, [KT, T], F16)
        self.hi, self.lo = k.view(180, [4, KT, P], F16), k.view(188, [4, KT, P], F16)
        self.hi_ready, self.lo_ready = k.sem("ahead_hi_ready"), k.sem("ahead_lo_ready")
        self.u = [k.view(120 + 4 * s, [KT, P]) for s in range(4)]
        self.out = k.view(152, [4, T])
        self.u_ld = [k.sem(f"ahead_u_ld{s}") for s in range(4)]
        self.stored = [k.sem(f"ahead_stored{s}") for s in range(4)]
        self.done, self.ready = k.sem("ahead_done"), k.sem("ahead_ready")

    def load(self, eng, m, s):
        eng.dma_start(self.u[s], self.uT[bass.ds(m, 1)].rearrange("i p f e -> (i p) f e")).then_inc(self.u_ld[s], 16)

    def split_hi(self, act, m, s, fours):
        act.wait_ge(self.u_ld[s], (fours + 1) * 16)
        act.wait_ge(self.done, m - 3)
        act.activation(self.hi[:, s], self.u[s], ACT.Copy, scale=SCALE).then_inc(self.hi_ready, 1)

    def split_lo(self, dve, m, s, fours):
        dve.wait_ge(self.hi_ready, m - AHEAD_PICKS + 1)
        dve.scalar_tensor_tensor(self.lo[:, s], self.u[s], SCALE, self.hi[:, s], ALU.mult, ALU.subtract).then_inc(self.lo_ready, 1)

    def products(self, pe, m, s, fours, features, split=False):
        if features[0] == 0:
            if split:
                pe.wait_ge(self.lo_ready, m - AHEAD_PICKS + 1)
            else:
                pe.wait_ge(self.u_ld[s], (fours + 1) * 16)
            if not isinstance(m, int) or m >= 2:
                pe.wait_ge(self.ready, m - 1)
        parts = [(self.hi[:, s], self.h_hi), (self.hi[:, s], self.h_lo), (self.lo[:, s], self.h_hi)] if split else \
            [(self.u[s], self.hn)]
        for f in features:
            for n, (u, x) in enumerate(parts):
                last = pe.matmul(self.k.ps[:, 6 + s % 2], u[:, f], x[:, f], start=f == 0 and n == 0,
                                 stop=f == KT - 1 and n == len(parts) - 1)
        if features[-1] == KT - 1:
            last.then_inc(self.done, 1)

    def finish(self, act, m, s, fours, split=False):
        act.wait_ge(self.done, m + 1)
        self.load(act, m + 4, s)
        if not isinstance(m, int) or m >= 4:
            act.wait_ge(self.stored[s], fours * 16)
        act.activation(self.out[:, s], self.k.ps[:, 6 + s % 2], ACT.Gelu,
                       scale=1 / SCALE if split else 1.0).then_inc(self.ready, 1)
        act.wait_ge(self.ready, m + 1)
        act.dma_start(self.acts[bass.ds(m, 1)].rearrange("i p t -> (i p) t"), self.out[:, s]).then_inc(self.stored[s], 16)


def route_picks(block, k, io):
    top, top_i = k.top, k.top_i
    cand, rest = k.view(48, [PH, 256]), k.view(56, [2, 256])
    best, best_i = k.view(58, [PH, TOPK]), k.view(59, [PH, TOPK], U32)
    pos = k.view(60, [2, PICKS], U32)
    posf, keyf = k.view(61, [2, PICKS]), k.view(62, [2 * PH, TOPK])
    hit = k.view(64, [PICKS, TOPK])
    picked = k.view(72, [3, PICKS])
    gsum = k.view(74, [PH])
    picksT = k.picksT
    iota16 = k.const("iota")[:, 0:TOPK].unsqueeze(1).to_broadcast([P, PICKS, TOPK])
    ps = k.ps
    step, gate_in, gate_exp, picked_ready, turn_done, turn_out = map(
        k.sem, ("step", "gate_in", "gate_exp", "picked_ready", "turn_done", "turn_out"))
    ahead = k.ahead = Ahead(k, io)
    LATE = 2
    until = [(AHEAD_PICKS - LATE) * t // TT for t in range(TT + 1)]

    def tiles(first, end, do, eng):
        for m in range(first, end):
            do(eng, m, m % 4, m // 4)

    def whole(pe, m, s, fours):
        ahead.products(pe, m, s, fours, range(KT))

    @block.sync
    def _(sp):
        for m in range(4):
            ahead.load(sp, m, m)

    @block.tensor
    def _(pe):
        for t in range(TT):
            tiles(until[t], until[t + 1], whole, pe)
            pe.wait_ge(picked_ready, t + 1)
            for n in range(3):
                last = pe.matmul(ps[:, n, t * P:(t + 1) * P], picked[:, n], k.const("ident"), start=True, stop=True)
            last.then_inc(turn_done, 1)
        tiles(AHEAD_PICKS - LATE, AHEAD_PICKS, whole, pe)

    @block.scalar
    def _(act):
        for t in range(TT):
            early = (until[t] + until[t + 1]) // 2
            tiles(until[t], early, ahead.finish, act)
            act.wait_ge(gate_in, t + 1)
            act.activation(picked[:, 2], picked[:, 2], ACT.Exp).then_inc(gate_exp, 1)
            tiles(early, until[t + 1], ahead.finish, act)
        act.wait_ge(turn_done, TT)
        for n in range(3):
            act.activation(picksT[:, n], ps[:, n], ACT.Copy).then_inc(turn_out, 1)
        ahead.split_hi(act, AHEAD_PICKS, 0, AHEAD_PICKS // 4)
        tiles(AHEAD_PICKS - LATE, AHEAD_PICKS, ahead.finish, act)

    @block.vector
    def _(dve):
        link = chained(dve, step)
        for t in range(TT):
            pair = top[:, t].rearrange("p (h s) a -> p s h a", s=2)
            first, second = pair[:, 0], pair[:, 1]
            link(dve.tensor_copy(keyf[:, :, :], top_i[:, t]))
            link(dve.tensor_tensor(cand.rearrange("p h (a b) -> p h a b", a=TOPK),
                                   first.unsqueeze(3).to_broadcast([P, PH, TOPK, TOPK]),
                                   second.unsqueeze(2).to_broadcast([P, PH, TOPK, TOPK]), ALU.add))
            for h in range(0, PH, 2):
                two = [(cand[:, h + b], best[:, h + b], best_i[:, h + b], rest[:, b]) for b in range(2)]
                for stage in (lambda s, v, i, r: dve.max(v[:, 0:8], s),
                              lambda s, v, i, r: dve.max_index(i[:, 0:8], v[:, 0:8], s),
                              lambda s, v, i, r: dve.match_replace(r, v[:, 0:8], s, -3.0e38),
                              lambda s, v, i, r: dve.max(v[:, 8:16], r),
                              lambda s, v, i, r: dve.max_index(i[:, 8:16], v[:, 8:16], r)):
                    for b in range(2):
                        link(stage(*two[b]))
            if t:
                dve.wait_ge(turn_done, t)
            flat_i = best_i.rearrange("p h a -> p (h a)")
            link(dve.tensor_scalar(pos[:, 0], flat_i, 4, None, ALU.logical_shift_right))
            link(dve.tensor_scalar(pos[:, 1], flat_i, 15, None, ALU.bitwise_and))
            link(dve.tensor_copy(posf[:, :, :], pos[:, :, :]))
            dve.tensor_tensor(picked[:, 2].rearrange("p (h a) -> p h a", h=PH), best[:, :, :],
                              best[:, :, 0:1].to_broadcast([P, PH, TOPK]), ALU.subtract).then_inc(gate_in, 1)
            keys = keyf.rearrange("p (h s) a -> p s h a", s=2)
            for n in range(2):
                link(dve.tensor_tensor(hit[:, :, :], posf[:, n].unsqueeze(2).to_broadcast([P, PICKS, TOPK]), iota16, ALU.is_equal))
                link(dve.tensor_tensor(hit.rearrange("p (h q) a -> p h q a", h=PH), hit.rearrange("p (h q) a -> p h q a", h=PH),
                                       keys[:, n].unsqueeze(2).to_broadcast([P, PH, TOPK, TOPK]), ALU.mult))
                link(dve.tensor_reduce(picked[:, n], hit[:, :, :], AX.X, ALU.add))
            dve.wait_ge(gate_exp, t + 1)
            gates = picked[:, 2].rearrange("p (h a) -> p h a", h=PH)
            link(dve.tensor_reduce(gsum, gates, AX.X, ALU.add))
            link(dve.reciprocal(gsum, gsum))
            dve.tensor_tensor(gates, gates, gsum.unsqueeze(2).to_broadcast([P, PH, TOPK]), ALU.mult).then_inc(picked_ready, 1)
            dve.wait_ge(picked_ready, t + 1)
    return turn_out


STAGE = 64
GATE_SCALE = 2.0 ** 15
BANKS = 4
NAHEAD = AHEAD_PICKS + AHEAD_PER_ROUND * T // (2 * STAGE)


def gate_matrix(block, k, io, turn_out):
    key1, key2, gate = (k.picksT[:, n] for n in range(3))
    SL, FEW = 16, 8
    iota, one_j, gated_hi, gated_lo = (k.view(kb, [n, NK], F16) for kb, n in ((168, 1), (48, SL), (52, SL), (160, SL)))
    high16, exact, high, low, ratio = k.view(170, [T], F16), *(k.view(kb, [T]) for kb in (172, 174, 176, 178))
    stage = [k.view(56 + 32 * s, [NK, STAGE]) for s in range(2)]
    Gd = io["gates"]
    ps = k.ps
    hot_ready, low_ready, dve_low_ready, g_done, staged, parts_step = map(
        k.sem, ("hot_ready", "low_ready", "dve_low_ready", "g_done", "staged", "parts_step"))
    stored = k.gates_stored = [k.sem(f"stored{s}") for s in range(2)]
    ROUNDS = T // (2 * STAGE)
    ahead = k.ahead

    EVERY = 2 * STAGE // AHEAD_PER_ROUND

    def low_by_vector(t):
        return t // FEW % 4 == 3

    def ahead_tile(it, t):
        n = t // EVERY
        return AHEAD_PICKS + it * AHEAD_PER_ROUND + n, n % 4, AHEAD_PICKS // 4 + it * (AHEAD_PER_ROUND // 4) + n // 4

    def rounds(eng, body):
        body(0)
        with eng.Fori(1, ROUNDS) as it:
            body(it)

    def wait(eng, sem, value):
        if not isinstance(value, int) or value > 0:
            eng.wait_ge(sem, value)

    @block.vector
    def _(dve):
        link = chained(dve, parts_step)
        dve.wait_ge(turn_out, 3)
        link(dve.tensor_copy(iota[:, 0], k.const("iota")))
        link(dve.tensor_scalar(high16, gate, GATE_SCALE, None, ALU.mult))
        link(dve.tensor_copy(exact, high16))
        link(dve.scalar_tensor_tensor(low, gate, GATE_SCALE, exact, ALU.mult, ALU.subtract))
        link(dve.tensor_scalar(high, exact, 1e-9, None, ALU.max))
        link(dve.reciprocal(high, high))
        link(dve.tensor_tensor(ratio, low, high, ALU.mult))

        ahead.split_lo(dve, *ahead_tile(0, 0))

        def body(it):
            for t in range(0, 2 * STAGE, FEW):
                at = it * 2 * STAGE + t
                if t >= SL:
                    dve.wait_ge(g_done, at - FEW)
                else:
                    wait(dve, g_done, it * 2 * STAGE - SL + FEW + t if not isinstance(it, int) or it else 0)
                few = slice(t % SL, t % SL + FEW)
                dve.tensor_tensor(one_j[:, few], iota.to_broadcast([P, FEW, NK]),
                                  key2[:, bass.ds(at, FEW)].unsqueeze(2).to_broadcast([P, FEW, NK]), ALU.is_equal)
                for b in range(FEW):
                    dve.tensor_scalar(gated_hi[:, (t + b) % SL], iota[:, 0], key1[:, bass.ds(at + b, 1)],
                                      exact[:, bass.ds(at + b, 1)], ALU.is_equal, ALU.mult).then_inc(hot_ready, 1)
                if low_by_vector(t):
                    dve.wait_ge(hot_ready, it * 2 * STAGE + t + FEW)
                    dve.tensor_tensor(gated_lo[:, few], gated_hi[:, few],
                                      ratio[:, bass.ds(at, FEW)].unsqueeze(2).to_broadcast([P, FEW, NK]),
                                      ALU.mult).then_inc(dve_low_ready, 1)
                if t % EVERY == 0:
                    ahead.split_lo(dve, *ahead_tile(it, t + EVERY))
        rounds(dve, body)

    @block.tensor
    def _(pe):
        def body(it):
            for t in range(2 * STAGE):
                if t % 4 == 0:
                    before = it * (2 * STAGE // 4) + t // 4 - BANKS + 1
                    if not isinstance(it, int) or before > 0:
                        pe.wait_ge(staged, before)
                if low_by_vector(t):
                    pe.wait_ge(dve_low_ready, it * (2 * STAGE // FEW // 4) + t // FEW // 4 + 1)
                else:
                    pe.wait_ge(low_ready, it * (2 * STAGE * 3 // 4) + t - t // (4 * FEW) * FEW + 1)
                out = ps[:, t // 4 % BANKS, t % 4 * P:(t % 4 + 1) * P]
                pe.matmul(out, one_j[:, t % SL], gated_hi[:, t % SL], start=True, stop=False)
                pe.matmul(out, one_j[:, t % SL], gated_lo[:, t % SL], start=False, stop=True).then_inc(g_done, 1)
                if t % FEW == FEW - 1:
                    part = t // FEW % 2
                    ahead.products(pe, *ahead_tile(it, t), range(part * KT // 2, (part + 1) * KT // 2), split=True)
        rounds(pe, body)

    @block.scalar
    def _(act):
        act.wait_ge(parts_step, 7)
        FOURS = 2 * STAGE // 4

        def low(it, q):
            if q * 4 % EVERY == 0:
                ahead.split_hi(act, *ahead_tile(it, 4 * q + EVERY))
            for t in range(4 * q, 4 * q + 4) if not low_by_vector(4 * q) else ():
                act.wait_ge(hot_ready, it * 2 * STAGE + t + 1)
                act.activation(gated_lo[:, t % SL], gated_hi[:, t % SL], ACT.Copy,
                               scale=ratio[:, bass.ds(it * 2 * STAGE + t, 1)]).then_inc(low_ready, 1)

        def stage_four(it, q):
            s, at = divmod(4 * q, STAGE)
            if at == 0:
                wait(act, stored[s], it * 16)
            act.wait_ge(g_done, it * 2 * STAGE + 4 * q + 4)
            act.activation(stage[s][:, :, at:at + 4].rearrange("p i t -> p t i"),
                           ps[:, q % BANKS].rearrange("p (t i) -> p t i", t=4), ACT.Copy,
                           scale=1 / GATE_SCALE).then_inc(staged, 1)
            if (4 * q + 4) % EVERY == 0:
                ahead.finish(act, *ahead_tile(it, 4 * q), split=True)

        def body(it):
            for q in range(FOURS):
                low(it, q)
                if q >= 2:
                    stage_four(it, q - 2)
                elif not isinstance(it, int):
                    stage_four(it - 1, FOURS + q - 2)
        rounds(act, body)
        stage_four(ROUNDS - 1, FOURS - 2)
        stage_four(ROUNDS - 1, FOURS - 1)

    @block.sync
    def _(sp):
        def body(it):
            for s in range(2):
                sp.wait_ge(staged, it * (2 * STAGE // 4) + (s + 1) * (STAGE // 4))
                sp.dma_start(Gd[bass.ds(it * 2 + s, 1)].rearrange("s j i t -> (s j) i t"), stage[s]).then_inc(stored[s], 16)
        rounds(sp, body)


def phase_route(nc, k, io):
    with nc.Block() as block:
        route_scores(block, k, io)
        gate_matrix(block, k, io, route_picks(block, k, io))


A_SCALE = 64.0
GROUP = 4


def phase_experts(nc, k, io):
    h_hi, h_lo, y = k.view(16, [KT, T], F16), k.view(24, [KT, T], F16), k.view(32, [KT, T])
    u_raw, v_raw = k.view(120, [4, KT, P]), k.view(64, [4, D])
    u_hi, u_lo = k.view(48, [4, KT, P], F16), k.view(188, [4, KT, P], F16)
    v_hi, v_lo = k.view(0, [8, D], F16), k.view(172, [8, D], F16)
    a_hi, a_lo = k.view(80, [8, T], F16), k.view(136, [8, T], F16)
    G = k.view(144, [8, T])
    acts, loaded = k.view(56, [4, T]), k.view(164, [4, T])
    OWN = NK - NAHEAD
    uT, v, Gd = io["uT"], io["peer_v"].rearrange("(i j) d -> i j d", j=NK), io["gates"]
    out = io["outT"].rearrange("(k p) t -> p k t", p=P)
    ps = k.ps
    N = NK
    with nc.Block() as block:
        u_ld = k.ahead.u_ld
        v_ld = [k.sem(f"v_ld{s}") for s in range(4)]
        g_ld = [k.sem(f"g_ld{s}") for s in range(8)]
        acts_ld = [k.sem(f"acts_ld{s}") for s in range(4)]
        u_hi_ready, u_lo_ready, v_hi_ready, v_lo_ready, act_ready, weighted, a_hi_ready, a_ready = map(
            k.sem, ("u_hi_ready", "u_lo_ready", "v_hi_ready", "v_lo_ready", "act_ready", "weighted", "a_hi_ready", "a_ready"))
        act_done, out_done, y_added, stored = map(k.sem, ("act_done", "out_done", "y_added", "stored"))

        def wait(eng, sem, value):
            if not isinstance(value, int) or value > 0:
                eng.wait_ge(sem, value)

        def steps(eng, step):
            def eights(first, end, own):
                def eight(it):
                    for r in range(8):
                        step(it, r, it * 8 + r, own)
                eight(first)
                with eng.Fori(first + 1, end - 1) as it:
                    eight(it)
                eight(end - 1)

            eights(0, OWN // 8, True)
            eights(OWN // 8, N // 8, False)
            for r in range(GROUP):
                step(N // 8, r, N + r, False)

        def tile_of(n, end=N):
            return not isinstance(n, int) or n < end

        @block.sync
        def _(sp):
            def step(it, r, n, own):
                if tile_of(n):
                    if not own:
                        wait(sp, a_ready, n - 3)
                        sp.dma_start(loaded[:, r % 4], io["acts"][bass.ds(n - OWN, 1)].rearrange("i p t -> (i p) t")).then_inc(acts_ld[r % 4], 16)
                    elif not (isinstance(n, int) and n < 4):
                        sp.wait_ge(u_lo_ready, n - 3)
                        sp.dma_start(u_raw[:, r % 4], uT[bass.ds(n + NAHEAD, 1)].rearrange("i p f e -> (i p) f e")).then_inc(u_ld[r % 4], 16)
                    tile = n + NAHEAD if own else n - OWN
                    if isinstance(n, int) and n == 0:
                        sp.wait_ge(k.gates_stored[0], 16 * T // (2 * STAGE))
                    wait(sp, v_lo_ready, n - 3)
                    sp.dma_start(v_raw[:, r % 4], v[bass.ds(tile, 1)].rearrange("i j d -> (i j) d")).then_inc(v_ld[r % 4], 16)
                    wait(sp, weighted, n - 7)
                    if isinstance(n, int) and n == 0:
                        sp.wait_ge(k.gates_stored[1], 16 * T // (2 * STAGE))
                        for s in range(4):
                            sp.wait_ge(k.ahead.stored[s], 16 * NAHEAD // 4)
                    sp.dma_start(G[:, r].rearrange("p (s t) -> p s t", t=STAGE),
                                 Gd[:, :, bass.ds(tile, 1)].rearrange("s j i t -> j s (i t)")).then_inc(g_ld[r], 16)
            steps(sp, step)
            for d in range(KT):
                sp.wait_ge(y_added, (N // GROUP - 1) * KT + d + 1)
                sp.dma_start(out[:, d], y[:, d]).then_inc(stored, 16)
            sp.wait_ge(stored, 16 * KT)

        @block.scalar
        def _(act):
            def split_u(it, r, m):
                act.wait_ge(u_ld[r % 4], (NAHEAD // 4 + it * 2 + r // 4 + 1) * 16)
                wait(act, act_done, m - 3)
                act.activation(u_hi[:, r % 4], u_raw[:, r % 4], ACT.Copy, scale=SCALE).then_inc(u_hi_ready, 1)

            def step(it, r, n, own):
                if isinstance(n, int) and n == 0:
                    for m in range(3):
                        split_u(0, m, m)
                if own and tile_of(n + 3, OWN):
                    split_u(it + (r + 3) // 8, (r + 3) % 8, n + 3)
                if tile_of(n):
                    act.wait_ge(v_ld[r % 4], (it * 2 + r // 4 + 1) * 16)
                    wait(act, out_done, ((it * 2) + r // 4 - 1) * KT)
                    act.activation(v_hi[:, r], v_raw[:, r % 4], ACT.Copy, scale=SCALE).then_inc(v_hi_ready, 1)
                if own:
                    act.wait_ge(act_done, n + 1)
                    wait(act, a_ready, n - 3)
                    act.activation(acts[:, r % 4], ps[:, r % 2], ACT.Gelu, scale=1 / SCALE).then_inc(act_ready, 1)
            steps(act, step)

        @block.vector
        def _(dve):
            def split_u(r, m):
                dve.wait_ge(u_hi_ready, m + 1)
                dve.scalar_tensor_tensor(u_lo[:, r % 4], u_raw[:, r % 4], SCALE, u_hi[:, r % 4],
                                         ALU.mult, ALU.subtract).then_inc(u_lo_ready, 1)

            def step(it, r, n, own):
                if isinstance(n, int) and n == 0:
                    for m in range(3):
                        split_u(m, m)
                if own and tile_of(n + 3, OWN):
                    split_u(r + 3, n + 3)
                if tile_of(n):
                    dve.wait_ge(v_hi_ready, n + 1)
                    dve.scalar_tensor_tensor(v_lo[:, r], v_raw[:, r % 4], SCALE, v_hi[:, r],
                                             ALU.mult, ALU.subtract).then_inc(v_lo_ready, 1)
                    if own:
                        x = acts[:, r % 4]
                        dve.wait_ge(act_ready, n + 1)
                    else:
                        x = loaded[:, r % 4]
                        dve.wait_ge(acts_ld[r % 4], ((it - OWN // 8) * 2 + r // 4 + 1) * 16)
                    dve.wait_ge(g_ld[r], (it + 1) * 16)
                    dve.scalar_tensor_tensor(x, x, A_SCALE, G[:, r], ALU.mult, ALU.mult).then_inc(weighted, 1)
                    dve.wait_ge(weighted, n + 1)
                    wait(dve, out_done, ((it * 2) + r // 4 - 1) * KT)
                    dve.tensor_copy(a_hi[:, r], x).then_inc(a_hi_ready, 1)
                    dve.wait_ge(a_hi_ready, n + 1)
                    dve.tensor_tensor(a_lo[:, r], x, a_hi[:, r], ALU.subtract).then_inc(a_ready, 1)
                if not (isinstance(n, int) and n < GROUP):
                    for b in range(2):
                        d = 2 * (r % 4) + b
                        nth = (it * 2 + r // 4 - 1) * KT + d
                        dve.wait_ge(out_done, nth + 1)
                        wait(dve, y_added, nth + 1 - KT)
                        dve.scalar_tensor_tensor(y[:, d], ps[:, 2 + d % 4], 1 / (SCALE * A_SCALE), y[:, d], ALU.mult, ALU.add).then_inc(y_added, 1)
            steps(dve, step)

        @block.tensor
        def _(pe):
            def step(it, r, n, own):
                if own:
                    pe.wait_ge(u_lo_ready, n + 1)
                    wait(pe, act_ready, n - 1)
                    for f in range(KT):
                        for w, x in ((u_hi, h_hi), (u_hi, h_lo), (u_lo, h_hi)):
                            last = pe.matmul(ps[:, r % 2], w[:, r % 4, f], x[:, f],
                                             start=f == 0 and x is h_hi and w is u_hi, stop=f == KT - 1 and w is u_lo)
                    last.then_inc(act_done, 1)
                if not (isinstance(n, int) and n < GROUP):
                    group = it * 2 + r // 4 - 1
                    if r % 4 == 0:
                        pe.wait_ge(a_ready, (group + 1) * GROUP)
                        pe.wait_ge(v_lo_ready, (group + 1) * GROUP)
                    for b in range(2):
                        d = 2 * (r % 4) + b
                        wait(pe, y_added, group * KT + d - 3)
                        for q in range(GROUP):
                            s = (r // 4 + 1) % 2 * 4 + q
                            for w, x in ((v_hi, a_hi), (v_hi, a_lo), (v_lo, a_hi)):
                                last = pe.matmul(ps[:, 2 + d % 4], w[:, s, d * P:(d + 1) * P], x[:, s],
                                                 start=q == 0 and x is a_hi and w is v_hi, stop=q == GROUP - 1 and w is v_lo)
                        last.then_inc(out_done, 1)
            steps(pe, step)


def laid_out(inputs):
    get = lambda n: np.asarray(inputs[n])
    q_w = np.concatenate([get("mla_qn_nope_w"), get("mla_qn_pe_w")])
    k_w = np.concatenate([get("mla_kn_nope_w"), get("mla_kn_pe_w")])
    half = ROPE // 2
    freq = (np.float32(10000.0) ** (-np.arange(half, dtype=np.float32) / np.float32(half))).astype(np.float32)
    given = {"qn_w": q_w, "kn_w": k_w, "rw_mu": get("rw_mu")[:14 * P], "rw_mu_tail": get("rw_mu")[14 * P:],
             "inv_freq": np.concatenate([np.zeros(NOPE, np.float32), freq, freq])}
    columns = []
    for name, rows, tiles in VECS:
        v = given[name] if name in given else get(name).reshape(-1)
        padded = np.zeros((P, tiles), np.float32)
        padded[:rows] = v.reshape(tiles, rows).T
        columns.append(padded)
    out = {"xT": get("x")[0].T, "positions": get("positions"), "vecs": np.concatenate(columns, axis=1),
           "consts": constant_array()}
    for name in ("w_in", "rw_w2", "rw_a2", "rw_g2", "rw_w_o", "mla_w_uq", "mla_w_ukv", "mla_w_o", "w_out",
                 "peer_w_query", "peer_v"):
        out[name] = get(name)
    out["sub_keysT"] = get("peer_sub_keys").reshape(2 * PH, NK, P).transpose(2, 0, 1)
    out["uT"] = get("peer_u").reshape(NK, NK, KT, P).transpose(0, 3, 2, 1)
    return {name: np.ascontiguousarray(a) for name, a in out.items()}




def build(nc, io, upto=99, dbg=None):
    with ExitStack() as ctx:
        k = Kit()
        arena = ctx.enter_context(nc.sbuf_tensor("arena", [P, ARENA_KB * 256], F32))
        k.consts = ctx.enter_context(nc.sbuf_tensor("consts", [P, NCONST], F32))
        k.vecs = ctx.enter_context(nc.sbuf_tensor("vecs", [P, NV], F32))
        k.eps = ctx.enter_context(nc.sbuf_tensor("eps", [P, 2], F32))
        k.chunk_decay = ctx.enter_context(nc.sbuf_tensor("chunk_decay", [P, RT, NCH], F32))
        k.ps = ctx.enter_context(nc.psum_tensor("ps", [P, 8, 512], F32))

        io = dict(io, gates=nc.dram_tensor("gates", (T // STAGE, NK, NK, STAGE), F32, kind="Internal").ap(),
                  gate_acts=nc.dram_tensor("gate_acts", (2 * KT, P, T), F32, kind="Internal").ap(),
                  acts=nc.dram_tensor("acts", (NAHEAD, P, T), F32, kind="Internal").ap())

        def view(at_kb, shape, dtype=F32):
            words = int(np.prod(shape)) * mybir.dt.size(dtype) // 4
            a = arena[:, at_kb * 256:at_kb * 256 + words]
            if dtype != F32:
                a = a.bitcast(dtype)
            if len(shape) > 1:
                names = "abcd"[:len(shape)]
                a = a.rearrange(f"p ({' '.join(names)}) -> p {' '.join(names)}", **dict(zip(names[1:], shape[1:])))
            return a

        k.view = view
        k.top, k.top_i = view(136, [TT, 2 * PH, TOPK]), view(140, [TT, 2 * PH, TOPK], U32)
        k.picksT = view(144, [3, T])
        k.xn_parts = view(0, [KT, T], F16), view(8, [KT, T], F16)
        sems = []

        def sem(name):
            sems.append(nc.alloc_semaphore(name=f"{k.phase}_{name}"))
            return sems[-1]

        k.sem = sem
        k.vec = lambda name, n=0: k.vecs[:, VEC_AT[name] + n:VEC_AT[name] + n + 1]
        k.const = lambda name: k.consts[:, CONST_AT[name][0]:sum(CONST_AT[name])]
        for n, phase in enumerate(PHASES):
            if n < upto:
                k.phase = phase.__name__.removeprefix("phase_")
                phase(nc, k, io)
                if phase is phase_rwkv_out_and_mla_project:
                    nc.clear_and_free_semaphores(sems)
                    nc.all_engine_barrier()
                    sems.clear()
        if dbg:
            dbg(nc, k, io)


ARENA_KB = 196
PHASES = [phase_norm_and_rwkv_in, phase_rwkv_prepare, phase_delta_rule, phase_rwkv_out_and_mla_project,
          phase_attention_and_merge,
          phase_route, phase_experts]




def kernel(**inputs):
    import concourse.bacc as bacc
    from concourse.bass_utils import run_bass_kernel_spmd

    nc = bacc.Bacc("TRN2", target_bir_lowering=False, num_devices=1)
    arrays, io = {}, {}
    for name, a in laid_out(inputs).items():
        arrays[f"in_{name}_dram"] = a
        io[name] = nc.dram_tensor(f"in_{name}_dram", a.shape, mybir.dt.from_np(a.dtype), kind="ExternalInput").ap()
    io["outT"] = nc.dram_tensor("out_0_dram", (D, T), F32, kind="ExternalOutput").ap()
    build(nc, io)
    r = run_bass_kernel_spmd(nc, [arrays], core_ids=[0])
    return np.ascontiguousarray(r.results[0]["out_0_dram"].T)[None]
```
